# Optimizing a Trainium2 kernel written in Bass

```python
import jax, jax.numpy as jnp
from jax import lax
import numpy as np

D_MODEL = 1024
BATCH = 1
SEQ = 512
DEPTH = 1

MEM_LEN = 256
D_MIX = D_MODEL
HEAD_DIM = 64
SG_WIDTH = D_MIX // 2
SG_GROUPS = SG_WIDTH // HEAD_DIM
SG_CHUNK = 128
NSA_WIDTH = D_MIX - SG_WIDTH
NSA_HEADS = NSA_WIDTH // HEAD_DIM
NSA_KV_HEADS = 2
NSA_GROUP = NSA_HEADS // NSA_KV_HEADS
KV_WIDTH = NSA_KV_HEADS * HEAD_DIM
N_BRANCH = 3
CMP_BLOCK = 32
CMP_STRIDE = 16
CMP_HIDDEN = 256
SLC_BLOCK = 64
SLC_TOPK = 16
WINDOW = 512
Q_BLOCK = 128
FORCE_SCORE = 1e4
IN_COLS = 2 * SG_WIDTH + NSA_WIDTH + 6 * KV_WIDTH + NSA_HEADS * N_BRANCH
MEM_HEADS = 4
MEM_HEAD_DIM = 128
D_FF = 4 * D_MODEL
EPS = 1e-6


def rms_norm(x, g):
    xf = x.astype(jnp.float32)
    y = xf * lax.rsqrt(jnp.mean(xf * xf, axis=-1, keepdims=True) + EPS)
    return (y * g.astype(jnp.float32)).astype(x.dtype)

def layer_norm(x, g, b):
    xf = x.astype(jnp.float32)
    mu = jnp.mean(xf, axis=-1, keepdims=True)
    xc = xf - mu
    y = xc * lax.rsqrt(jnp.mean(xc * xc, axis=-1, keepdims=True) + EPS)
    return (y * g.astype(jnp.float32) + b.astype(jnp.float32)).astype(x.dtype)

def masked_softmax(s, mask):
    s = jnp.where(mask, s.astype(jnp.float32), -jnp.inf)
    m = jnp.max(s, axis=-1, keepdims=True)
    m = jnp.where(jnp.isfinite(m), m, 0.0)
    e = jnp.exp(s - m)
    d = jnp.sum(e, axis=-1, keepdims=True)
    return e / jnp.where(d > 0, d, 1.0)

def spatial_gating_unit(u, v, ln_g, ln_b, w_s, b_s):
    B, T, _ = u.shape
    v = layer_norm(v, ln_g, ln_b)
    vb = v.reshape(B, T // SG_CHUNK, SG_CHUNK, SG_GROUPS, HEAD_DIM)
    causal = jnp.tril(jnp.ones((SG_CHUNK, SG_CHUNK), dtype=bool))
    w = jnp.where(causal[None], w_s, 0)
    s = jnp.einsum('gts,bcsgd->bctgd', w, vb) + b_s.T[None, None, :, :, None]
    return u * s.reshape(B, T, SG_WIDTH)

def compress_blocks(k, pos, w1, b1, w2, b2):
    B, T, H, d = k.shape
    kc = k.reshape(B, T // CMP_STRIDE, CMP_STRIDE, H, d)
    blocks = jnp.concatenate([kc[:, :-1], kc[:, 1:]], axis=2) + pos[None, None, :, None, :]
    flat = blocks.transpose(0, 1, 3, 2, 4).reshape(B, -1, H, CMP_BLOCK * d)
    h = jax.nn.gelu(flat @ w1 + b1)
    return h @ w2 + b2

def nsa_attention(q, kv, gate_logits, q_norm_g, k_norm_g, cmp_pos, cmp_w1, cmp_b1, cmp_w2, cmp_b2):
    B, T = q.shape[:2]
    H, G, d = NSA_KV_HEADS, NSA_GROUP, HEAD_DIM
    n_cmp = T // CMP_STRIDE - 1
    n_slc = T // SLC_BLOCK
    n_sel = min(SLC_TOPK, n_slc)
    n_qb = T // Q_BLOCK
    scale = HEAD_DIM ** -0.5
    t_pos = jnp.arange(T)

    q = rms_norm(q.reshape(B, T, H, G, d), q_norm_g)
    k_cmp, v_cmp, k_slc, v_slc, k_win, v_win = [
        a.reshape(B, T, H, d) for a in jnp.split(kv, 6, axis=-1)]

    kc = rms_norm(compress_blocks(k_cmp, cmp_pos[0], cmp_w1[0], cmp_b1[0], cmp_w2[0], cmp_b2[0]), k_norm_g[0])
    vc = compress_blocks(v_cmp, cmp_pos[1], cmp_w1[1], cmp_b1[1], cmp_w2[1], cmp_b2[1])
    s_cmp = jnp.einsum('bthgd,bnhd->bhgtn', q, kc) * scale
    cmp_end = jnp.arange(n_cmp) * CMP_STRIDE + CMP_BLOCK - 1
    p_cmp = masked_softmax(s_cmp, cmp_end[None, :] <= t_pos[:, None])
    o_cmp = jnp.einsum('bhgtn,bnhd->bthgd', p_cmp.astype(vc.dtype), vc)

    cs = jnp.arange(n_cmp) * CMP_STRIDE
    ss = jnp.arange(n_slc) * SLC_BLOCK
    overlap = jnp.clip(jnp.minimum(cs[:, None] + CMP_BLOCK, ss[None, :] + SLC_BLOCK)
                       - jnp.maximum(cs[:, None], ss[None, :]), 0, None).astype(jnp.float32) / CMP_BLOCK
    imp = jnp.einsum('bhgtn,nj->bhtj', p_cmp, overlap)
    t_blk = t_pos[:, None] // SLC_BLOCK
    j = jnp.arange(n_slc)[None, :]
    forced = (j == 0) | (j == t_blk) | (j == t_blk - 1)
    imp = jnp.where(forced, FORCE_SCORE, jnp.where(j <= t_blk, imp, -FORCE_SCORE))
    _, sel = lax.top_k(imp, n_sel)

    k_slc = rms_norm(k_slc, k_norm_g[1])
    kb = k_slc.reshape(B, n_slc, SLC_BLOCK, H, d).transpose(0, 3, 1, 2, 4)
    vb = v_slc.reshape(B, n_slc, SLC_BLOCK, H, d).transpose(0, 3, 1, 2, 4)
    qb = q.reshape(B, n_qb, Q_BLOCK, H, G, d).transpose(1, 0, 2, 3, 4, 5)
    sb = sel.reshape(B, H, n_qb, Q_BLOCK, n_sel).transpose(2, 0, 1, 3, 4)
    tb = t_pos.reshape(n_qb, Q_BLOCK)
    bi = jnp.arange(B)[:, None, None, None]
    hi = jnp.arange(H)[None, :, None, None]

    def selected_block(args):
        qc, ic, tc = args
        kg = kb[bi, hi, ic].reshape(B, H, Q_BLOCK, n_sel * SLC_BLOCK, d)
        vg = vb[bi, hi, ic].reshape(B, H, Q_BLOCK, n_sel * SLC_BLOCK, d)
        key_pos = (ic[..., None] * SLC_BLOCK + jnp.arange(SLC_BLOCK)).reshape(B, H, Q_BLOCK, n_sel * SLC_BLOCK)
        mask = (key_pos <= tc[None, None, :, None])[:, :, None]
        s = jnp.einsum('bthgd,bhtmd->bhgtm', qc, kg) * scale
        p = masked_softmax(s, mask)
        return jnp.einsum('bhgtm,bhtmd->bthgd', p.astype(vg.dtype), vg)

    o_slc = lax.map(selected_block, (qb, sb, tb)).transpose(1, 0, 2, 3, 4, 5).reshape(B, T, H, G, d)

    k_win = rms_norm(k_win, k_norm_g[2])
    pad = ((0, 0), (WINDOW, 0), (0, 0), (0, 0))
    kp = jnp.pad(k_win, pad)
    vp = jnp.pad(v_win, pad)
    win_idx = jnp.arange(n_qb)[:, None] * Q_BLOCK + jnp.arange(WINDOW + Q_BLOCK)[None, :]
    kw = kp[:, win_idx]
    vw = vp[:, win_idx]
    qw = q.reshape(B, n_qb, Q_BLOCK, H, G, d)
    s_win = jnp.einsum('bcthgd,bckhd->bhgctk', qw, kw) * scale
    q_abs = tb[:, :, None]
    k_abs = (win_idx - WINDOW)[:, None, :]
    win_mask = (k_abs <= q_abs) & (k_abs > q_abs - WINDOW) & (k_abs >= 0)
    p_win = masked_softmax(s_win, win_mask)
    o_win = jnp.einsum('bhgctk,bckhd->bcthgd', p_win.astype(vw.dtype), vw).reshape(B, T, H, G, d)

    g = jax.nn.sigmoid(gate_logits.astype(jnp.float32)).reshape(B, T, H, G, N_BRANCH).astype(q.dtype)
    o = g[..., 0:1] * o_cmp + g[..., 1:2] * o_slc + g[..., 2:3] * o_win
    return o.reshape(B, T, NSA_WIDTH)

def memory_cross_attention(h, mem, kv_norm_g, w_mq, w_mkv, q_g, k_g, w_mo):
    B, T, _ = h.shape
    M = mem.shape[1]
    q = rms_norm((h @ w_mq).reshape(B, T, MEM_HEADS, MEM_HEAD_DIM), q_g)
    k, v = jnp.split(rms_norm(mem, kv_norm_g) @ w_mkv, 2, axis=-1)
    k = rms_norm(k.reshape(B, M, MEM_HEADS, MEM_HEAD_DIM), k_g)
    v = v.reshape(B, M, MEM_HEADS, MEM_HEAD_DIM)
    s = jnp.einsum('bthd,bmhd->bhtm', q, k) * MEM_HEAD_DIM ** -0.5
    p = jax.nn.softmax(s.astype(jnp.float32), axis=-1).astype(v.dtype)
    o = jnp.einsum('bhtm,bmhd->bthd', p, v).reshape(B, T, MEM_HEADS * MEM_HEAD_DIM)
    return o @ w_mo

def first_inputs(seed: int = 0) -> dict:
    key = jax.random.key(seed)
    ks = jax.random.split(key, 32)

    def nrm(k, shape, scale):
        return jax.random.normal(k, shape, jnp.float32) * scale

    def gain(k, shape):
        return 1.0 + 0.05 * jax.random.normal(k, shape, jnp.float32)

    L = DEPTH
    return {
        'x': nrm(ks[0], (BATCH, SEQ, D_MODEL), 1.0),
        'mem': nrm(ks[1], (BATCH, MEM_LEN, D_MODEL), 1.0),
        'norm_mix_g': gain(ks[2], (L, D_MODEL)),
        'w_in': nrm(ks[3], (L, D_MODEL, IN_COLS), D_MODEL ** -0.5),
        'sg_ln_g': gain(ks[4], (L, SG_WIDTH)),
        'sg_ln_b': nrm(ks[5], (L, SG_WIDTH), 0.02),
        'sg_w': nrm(ks[6], (L, SG_GROUPS, SG_CHUNK, SG_CHUNK), SG_CHUNK ** -0.5),
        'sg_b': 1.0 + nrm(ks[7], (L, SG_GROUPS, SG_CHUNK), 0.1),
        'q_norm_g': gain(ks[8], (L, HEAD_DIM)),
        'k_norm_g': gain(ks[9], (L, N_BRANCH, HEAD_DIM)),
        'cmp_pos': nrm(ks[10], (L, 2, CMP_BLOCK, HEAD_DIM), 0.5),
        'cmp_w1': nrm(ks[11], (L, 2, CMP_BLOCK * HEAD_DIM, CMP_HIDDEN), (CMP_BLOCK * HEAD_DIM) ** -0.5),
        'cmp_b1': nrm(ks[12], (L, 2, CMP_HIDDEN), 0.02),
        'cmp_w2': nrm(ks[13], (L, 2, CMP_HIDDEN, HEAD_DIM), CMP_HIDDEN ** -0.5),
        'cmp_b2': nrm(ks[14], (L, 2, HEAD_DIM), 0.02),
        'mix_out_g': gain(ks[15], (L, 2, SG_WIDTH)),
        'w_out': nrm(ks[16], (L, D_MIX, D_MODEL), D_MIX ** -0.5),
        'norm_mem_g': gain(ks[17], (L, D_MODEL)),
        'mem_kv_norm_g': gain(ks[18], (L, D_MODEL)),
        'w_mq': nrm(ks[19], (L, D_MODEL, MEM_HEADS * MEM_HEAD_DIM), D_MODEL ** -0.5),
        'w_mkv': nrm(ks[20], (L, D_MODEL, 2 * MEM_HEADS * MEM_HEAD_DIM), D_MODEL ** -0.5),
        'mem_q_norm_g': gain(ks[21], (L, MEM_HEAD_DIM)),
        'mem_k_norm_g': gain(ks[22], (L, MEM_HEAD_DIM)),
        'w_mo': nrm(ks[23], (L, MEM_HEADS * MEM_HEAD_DIM, D_MODEL), (MEM_HEADS * MEM_HEAD_DIM) ** -0.5),
        'norm_ffn_g': gain(ks[24], (L, D_MODEL)),
        'w_ff1': nrm(ks[25], (L, D_MODEL, D_FF), D_MODEL ** -0.5),
        'w_ff2': nrm(ks[26], (L, D_FF, D_MODEL), D_FF ** -0.5),
    }

def first_block(x, mem, norm_mix_g, w_in, sg_ln_g, sg_ln_b, sg_w, sg_b, q_norm_g, k_norm_g,
              cmp_pos, cmp_w1, cmp_b1, cmp_w2, cmp_b2, mix_out_g, w_out,
              norm_mem_g, mem_kv_norm_g, w_mq, w_mkv, mem_q_norm_g, mem_k_norm_g, w_mo,
              norm_ffn_g, w_ff1, w_ff2):
    splits = [SG_WIDTH, 2 * SG_WIDTH, 2 * SG_WIDTH + NSA_WIDTH,
              2 * SG_WIDTH + NSA_WIDTH + 6 * KV_WIDTH]
    for l in range(DEPTH):
        h = rms_norm(x, norm_mix_g[l])
        z = h @ w_in[l]
        u, v, q, kv, gl = jnp.split(z, splits, axis=-1)
        a = spatial_gating_unit(jax.nn.gelu(u), jax.nn.gelu(v), sg_ln_g[l], sg_ln_b[l], sg_w[l], sg_b[l])
        b = nsa_attention(q, kv, gl, q_norm_g[l], k_norm_g[l], cmp_pos[l], cmp_w1[l], cmp_b1[l],
                          cmp_w2[l], cmp_b2[l])
        mixed = jnp.concatenate([rms_norm(a, mix_out_g[l, 0]), rms_norm(b, mix_out_g[l, 1])], axis=-1)
        x = x + mixed @ w_out[l]
        x = x + memory_cross_attention(rms_norm(x, norm_mem_g[l]), mem, mem_kv_norm_g[l], w_mq[l],
                                       w_mkv[l], mem_q_norm_g[l], mem_k_norm_g[l], w_mo[l])
        h = rms_norm(x, norm_ffn_g[l])
        x = x + jnp.square(jax.nn.relu(h @ w_ff1[l])) @ w_ff2[l]
    return x


DEPTH_2 = 2

GRID_W = 64
CTX_LEN = 256
D_FF_2 = ((8 * D_MODEL // 3 + 255) // 256) * 256
HALF_STEP = 0.5
N_MOD = 9
RMS_EPS = 1e-6
NEG_INF = -1e30

CONV_CH = D_MODEL // 4
CONV_K = 3
POOL_CH = D_MODEL // 4
POOL_WINDOWS = (2, 4, 8, 16)
POOL_GROUP = POOL_CH // 4
NA_HEAD_DIM = 64
NA_CH = D_MODEL // 2
NA_HEADS = NA_CH // NA_HEAD_DIM
NA_KH_MAX = 8
NA_KW = 16
NA_QC = 16
NA_KB = NA_QC + NA_KW - 1
D_MIX_2 = CONV_CH + POOL_CH + NA_CH
OFF_B = CONV_CH
OFF_C = 2 * CONV_CH
OFF_P = 3 * CONV_CH
OFF_Q = 3 * CONV_CH + POOL_CH
OFF_K = OFF_Q + NA_CH
OFF_V = OFF_K + NA_CH
D_IN = OFF_V + NA_CH


def rms_norm_2(x, g):
    xf = x.astype(jnp.float32)
    y = xf * lax.rsqrt(jnp.mean(xf * xf, axis=-1, keepdims=True) + RMS_EPS)
    return (y * g.astype(jnp.float32)).astype(x.dtype)

def mod_norm(x, m, i, g):
    return rms_norm_2(x, g) * (1 + m[:, 3 * i + 1, None]) + m[:, 3 * i, None]

def swiglu(h, w1, w2):
    a, b = jnp.split(h @ w1, 2, axis=-1)
    return (jax.nn.silu(a) * b) @ w2

def ffn_sublayer(x, m, i, g, w1, w2):
    return x + HALF_STEP * m[:, 3 * i + 2, None] * swiglu(mod_norm(x, m, i, g), w1, w2)

def short_conv(u, w):
    return lax.conv_general_dilated(
        u, w[:, None, :].astype(u.dtype), window_strides=(1,),
        padding=[(CONV_K // 2, CONV_K // 2)],
        dimension_numbers=('NWC', 'WIO', 'NWC'), feature_group_count=u.shape[-1])

def gated_conv_mixer(h, b_gate, c_gate, conv_w):
    return b_gate * short_conv(c_gate * h, conv_w)

def multiscale_pool_mixer(v, pool_w, pool_scale):
    L = v.shape[1]
    vf = v.astype(jnp.float32)
    cs = jnp.concatenate([jnp.zeros_like(vf[:, :1]), jnp.cumsum(vf, axis=1)], axis=1)
    t = jnp.arange(L)
    outs = []
    for g, w in enumerate(POOL_WINDOWS):
        left = w // 2
        right = w - 1 - left
        lo = jnp.clip(t - left, 0, L)
        hi = jnp.clip(t + right + 1, 0, L)
        sl = slice(g * POOL_GROUP, (g + 1) * POOL_GROUP)
        mean = (cs[:, hi, sl] - cs[:, lo, sl]) / (hi - lo).astype(jnp.float32)[None, :, None]
        outs.append((mean - vf[..., sl]).astype(v.dtype) @ pool_w[g])
    return jnp.concatenate(outs, axis=-1) * pool_scale

def context_attention(q, k, v):
    B, L = q.shape[:2]
    s = jnp.einsum('bqhd,bkhd->bhqk', q, k, preferred_element_type=jnp.float32) * (NA_HEAD_DIM ** -0.5)
    p = jax.nn.softmax(s, axis=-1).astype(v.dtype)
    return jnp.einsum('bhqk,bkhd->bqhd', p, v).reshape(B, L, NA_CH)

def neighbourhood_attention(q, k, v, k_ctx, v_ctx, rpb):
    B, S = q.shape[:2]
    rows = S // GRID_W
    kh = min(NA_KH_MAX, rows)
    nj = GRID_W // NA_QC
    scale = NA_HEAD_DIM ** -0.5
    qg = q.reshape(B, rows, GRID_W, NA_HEADS, NA_HEAD_DIM)
    kg = k.reshape(B, rows, GRID_W, NA_HEADS, NA_HEAD_DIM)
    vg = v.reshape(B, rows, GRID_W, NA_HEADS, NA_HEAD_DIM)
    qcol = jnp.arange(GRID_W).reshape(nj, NA_QC)
    band0 = jnp.clip(jnp.arange(nj) * NA_QC - NA_KW // 2, 0, GRID_W - NA_KB)
    kcol = band0[:, None] + jnp.arange(NA_KB)
    cstart = jnp.clip(qcol - NA_KW // 2, 0, GRID_W - NA_KW)
    col_valid = (kcol[:, None, :] >= cstart[..., None]) & (kcol[:, None, :] < cstart[..., None] + NA_KW)
    col_off = kcol[:, None, :] - qcol[..., None] + NA_KW - 1
    n_loc = kh * NA_KB

    def row_block(r):
        rs = jnp.clip(r - kh // 2, 0, rows - kh)
        q_r = lax.dynamic_index_in_dim(qg, r, axis=1, keepdims=False).reshape(
            B, nj, NA_QC, NA_HEADS, NA_HEAD_DIM)
        k_b = lax.dynamic_slice_in_dim(kg, rs, kh, axis=1)[:, :, kcol]
        v_b = lax.dynamic_slice_in_dim(vg, rs, kh, axis=1)[:, :, kcol]
        row_off = rs + jnp.arange(kh) - r + NA_KH_MAX - 1
        bias = rpb[:, row_off[None, None, :, None], col_off[:, :, None, :]].astype(jnp.float32)
        bias = jnp.where(col_valid[None, :, :, None, :], bias, NEG_INF)
        s_loc = jnp.einsum('bjqhd,bijkhd->bhjqik', q_r, k_b,
                           preferred_element_type=jnp.float32) * scale + bias
        s_ctx = jnp.einsum('bjqhd,bchd->bhjqc', q_r, k_ctx,
                           preferred_element_type=jnp.float32) * scale
        s = jnp.concatenate([s_loc.reshape(B, NA_HEADS, nj, NA_QC, n_loc), s_ctx], axis=-1)
        p = jax.nn.softmax(s, axis=-1).astype(v.dtype)
        p_loc = p[..., :n_loc].reshape(B, NA_HEADS, nj, NA_QC, kh, NA_KB)
        o = (jnp.einsum('bhjqik,bijkhd->bjqhd', p_loc, v_b)
             + jnp.einsum('bhjqc,bchd->bjqhd', p[..., n_loc:], v_ctx))
        return o.reshape(B, GRID_W, NA_CH)

    out = lax.map(row_block, jnp.arange(rows))
    return out.transpose(1, 0, 2, 3).reshape(B, S, NA_CH)

def heads(t):
    return t.reshape(t.shape[0], t.shape[1], NA_HEADS, NA_HEAD_DIM)

def second_inputs(seed: int = 0) -> dict:
    key = jax.random.key(seed)
    ks = jax.random.split(key, 16)
    f32 = jnp.float32
    nrm = lambda k, shape, s: jax.random.normal(k, shape, f32) * s
    return {
        'x': nrm(ks[0], (BATCH, SEQ, D_MODEL), 1.0),
        'c': nrm(ks[1], (BATCH, D_MODEL), 1.0),
        'ctx': nrm(ks[2], (BATCH, CTX_LEN, D_MODEL), 1.0),
        'c_ctx': nrm(ks[3], (D_MODEL,), 1.0),
        'w_mod': nrm(ks[4], (DEPTH_2, D_MODEL, N_MOD * D_MODEL), 0.5 * D_MODEL ** -0.5),
        'b_mod': nrm(ks[5], (DEPTH_2, N_MOD * D_MODEL), 0.01),
        'norm_g': 1.0 + nrm(ks[6], (DEPTH_2, 3, D_MODEL), 0.02),
        'ffn_w_in': nrm(ks[7], (DEPTH_2, 2, D_MODEL, 2 * D_FF_2), D_MODEL ** -0.5),
        'ffn_w_out': nrm(ks[8], (DEPTH_2, 2, D_FF_2, D_MODEL), D_FF_2 ** -0.5),
        'w_in': nrm(ks[9], (DEPTH_2, D_MODEL, D_IN), D_MODEL ** -0.5),
        'conv_w': nrm(ks[10], (DEPTH_2, CONV_K, CONV_CH), CONV_K ** -0.5),
        'pool_w': nrm(ks[11], (DEPTH_2, len(POOL_WINDOWS), POOL_GROUP, POOL_GROUP), POOL_GROUP ** -0.5),
        'pool_scale': 1.0 + nrm(ks[12], (DEPTH_2, POOL_CH), 0.1),
        'rpb': nrm(ks[13], (DEPTH_2, NA_HEADS, 2 * NA_KH_MAX - 1, 2 * NA_KW - 1), 0.1),
        'w_out': nrm(ks[14], (DEPTH_2, D_MIX_2, D_MODEL), D_MIX_2 ** -0.5),
        'final_g': 1.0 + nrm(ks[15], (D_MODEL,), 0.02),
    }

def second_block(x, c, ctx, c_ctx, w_mod, b_mod, norm_g, ffn_w_in, ffn_w_out, w_in,
              conv_w, pool_w, pool_scale, rpb, w_out, final_g):
    B = x.shape[0]
    xc = ctx
    for l in range(DEPTH_2):
        last = l == DEPTH_2 - 1
        m = (jax.nn.silu(c) @ w_mod[l] + b_mod[l]).reshape(B, N_MOD, D_MODEL)
        mc = (jax.nn.silu(c_ctx) @ w_mod[l] + b_mod[l]).reshape(1, N_MOD, D_MODEL)

        x = ffn_sublayer(x, m, 0, norm_g[l, 0], ffn_w_in[l, 0], ffn_w_out[l, 0])
        xc = ffn_sublayer(xc, mc, 0, norm_g[l, 0], ffn_w_in[l, 0], ffn_w_out[l, 0])

        h = mod_norm(x, m, 1, norm_g[l, 1])
        hc = mod_norm(xc, mc, 1, norm_g[l, 1])
        u = h @ w_in[l]
        if last:
            uc_kv = hc @ w_in[l][:, OFF_K:]
            kc, vc = heads(uc_kv[..., :NA_CH]), heads(uc_kv[..., NA_CH:])
        else:
            uc = hc @ w_in[l]
            kc, vc = heads(uc[..., OFF_K:OFF_V]), heads(uc[..., OFF_V:])
            yc = jnp.concatenate([
                gated_conv_mixer(uc[..., :OFF_B], uc[..., OFF_B:OFF_C], uc[..., OFF_C:OFF_P], conv_w[l]),
                multiscale_pool_mixer(uc[..., OFF_P:OFF_Q], pool_w[l], pool_scale[l]),
                context_attention(heads(uc[..., OFF_Q:OFF_K]), kc, vc),
            ], axis=-1) @ w_out[l]
            xc = xc + mc[:, 5, None] * yc
            xc = ffn_sublayer(xc, mc, 2, norm_g[l, 2], ffn_w_in[l, 1], ffn_w_out[l, 1])
        y = jnp.concatenate([
            gated_conv_mixer(u[..., :OFF_B], u[..., OFF_B:OFF_C], u[..., OFF_C:OFF_P], conv_w[l]),
            multiscale_pool_mixer(u[..., OFF_P:OFF_Q], pool_w[l], pool_scale[l]),
            neighbourhood_attention(heads(u[..., OFF_Q:OFF_K]), heads(u[..., OFF_K:OFF_V]),
                                    heads(u[..., OFF_V:]), kc, vc, rpb[l]),
        ], axis=-1) @ w_out[l]
        x = x + m[:, 5, None] * y

        x = ffn_sublayer(x, m, 2, norm_g[l, 2], ffn_w_in[l, 1], ffn_w_out[l, 1])
    return rms_norm_2(x, final_g)


def setup_inputs(seed=0):
    out = dict(first_inputs(seed))
    for name, value in second_inputs(seed + 1).items():
        if name != "x":
            out[name + "_2"] = value
    return out


def reference(
    x, mem, norm_mix_g, w_in, sg_ln_g, sg_ln_b, sg_w, sg_b, q_norm_g, k_norm_g, cmp_pos, cmp_w1,
    cmp_b1, cmp_w2, cmp_b2, mix_out_g, w_out, norm_mem_g, mem_kv_norm_g, w_mq, w_mkv,
    mem_q_norm_g, mem_k_norm_g, w_mo, norm_ffn_g, w_ff1, w_ff2, c_2, ctx_2, c_ctx_2, w_mod_2,
    b_mod_2, norm_g_2, ffn_w_in_2, ffn_w_out_2, w_in_2, conv_w_2, pool_w_2, pool_scale_2, rpb_2,
    w_out_2, final_g_2,
):
    x = first_block(
        x, mem, norm_mix_g, w_in, sg_ln_g, sg_ln_b, sg_w, sg_b, q_norm_g, k_norm_g, cmp_pos,
        cmp_w1, cmp_b1, cmp_w2, cmp_b2, mix_out_g, w_out, norm_mem_g, mem_kv_norm_g, w_mq,
        w_mkv, mem_q_norm_g, mem_k_norm_g, w_mo, norm_ffn_g, w_ff1, w_ff2,
    )
    return second_block(
        x, c_2, ctx_2, c_ctx_2, w_mod_2, b_mod_2, norm_g_2, ffn_w_in_2, ffn_w_out_2, w_in_2,
        conv_w_2, pool_w_2, pool_scale_2, rpb_2, w_out_2, final_g_2,
    )


_drawn_inputs = setup_inputs


def setup_inputs(seed=0):
    import zlib

    import numpy as np

    out = dict(_drawn_inputs(seed))
    spreads = {}
    factors = {'sg_ln_g': 3.793,
     'sg_ln_b': 8.0,
     'q_norm_g': 5.044,
     'k_norm_g': 4.7,
     'cmp_b1': 4.897,
     'cmp_b2': 2.968,
     'norm_mem_g': 8.0,
     'mem_kv_norm_g': 8.0,
     'mem_q_norm_g': 8.0,
     'mem_k_norm_g': 8.0,
     'ctx_2': 4.169,
     'b_mod_2': 6.71,
     'norm_g_2': 8.0,
     'pool_scale_2': 26.133,
     'rpb_2': 64.0,
     'final_g_2': 8.18}
    for name, (base, spread) in spreads.items():
        noise = np.random.default_rng([zlib.crc32(name.encode()), seed]).standard_normal(out[name].shape)
        drawn = base * np.exp(spread * noise) if base else spread * noise
        out[name] = __import__('jax').numpy.asarray(drawn.astype(out[name].dtype))
    for name, factor in factors.items():
        out[name] = (out[name] * factor).astype(out[name].dtype)
    return out
```

```python
from contextlib import ExitStack

import numpy as np

import concourse.bass as bass
from concourse import mybir

F32 = mybir.dt.float32
F32R = mybir.dt.float32r
ALU = mybir.AluOpType
ACT = mybir.ActivationFunctionType
AX = mybir.AxisListType

NEG = -1e30
EPS = 1e-6
T = 512
TC = 256
FF2 = 2816
RAW = 3
HL = 3
AHEAD = 2

PARAMS = [("norm_mix_g", 8), ("mix_out_g", 8), ("norm_mem_g", 8), ("mem_kv_norm_g", 8),
          ("norm_ffn_g", 8), ("q_norm_g", 1), ("k_norm_g", 3), ("cmp_b1", 4), ("cmp_b2", 1),
          ("mem_q_norm_g", 1), ("mem_k_norm_g", 1), ("sg_b", 8), ("cmp_pos", 32),
          ("norm_g_2", 48), ("b_mod_2", 144), ("cc_2", 16), ("conv_w_2", 12),
          ("pool_scale_2", 4), ("final_g_2", 8)]
PCOL = {}
_at = 0
for _n, _w in PARAMS:
    PCOL[_n] = _at
    _at += _w
NPAR = _at
CIDENT, CONES, CBLOCK, NCONST = 0, 128, 256, 384
C1_CAUSAL, C1_SGU, C1_CMP, NC1 = 0, 128, 256, 256 + 124
C2_MASK, C2_EDGE, C2_RW, NC2 = 0, 768, 768 + 32, 768 + 34
BAND0 = [0, 8, 24, 32]
KIND = [0, 1, 1, 2]


def constants():
    c = np.zeros((128, NCONST), np.float32)
    c[:, CIDENT:CIDENT + 128] = np.eye(128)
    c[:, CONES:CONES + 128] = 1
    c[:64, CBLOCK:CBLOCK + 64] = 1
    c[64:, CBLOCK + 64:CBLOCK + 128] = 1
    c1 = np.zeros((128, NC1), np.float32)
    q, k = np.arange(128)[:, None], np.arange(128)[None, :]
    c1[:, C1_CAUSAL:C1_CAUSAL + 128] = np.where(k <= q, 0, NEG)
    c1[:, C1_SGU:C1_SGU + 128] = q <= k
    for i in range(4):
        n = np.arange(31)[None, :]
        c1[:, C1_CMP + 31 * i:C1_CMP + 31 * i + 31] = np.where(16 * n + 31 <= q + 128 * i, 0, NEG)
    c2 = np.zeros((128, NC2), np.float32)
    for kind, j in ((0, 0), (1, 1), (2, 3)):
        col = 16 * j + np.arange(128)[:, None] % 16
        kc = BAND0[j] + np.arange(256)[None, :] % 32
        start = np.clip(col - 8, 0, 48)
        c2[:, C2_MASK + 256 * kind:C2_MASK + 256 * kind + 256] = np.where((kc >= start) & (kc < start + 16), 0, NEG)
    for tile in range(2):
        for half in range(2):
            w = (2, 4, 8, 16)[2 * tile + half]
            rows = slice(64 * half, 64 * half + 64)
            for e in range(8):
                c2[rows, C2_EDGE + 16 * tile + e] = 1 / (min(e + w - w // 2, 10 ** 6) - max(e - w // 2, 0))
                back = 8 - e
                c2[rows, C2_EDGE + 16 * tile + 8 + e] = 1 / (min(w - w // 2, back) + w // 2)
            c2[rows, C2_RW + tile] = 1 / w
    return c, c1, c2


class Recorder:

    def activation(self, *a, **k):
        return lambda e: e.activation(*a, **k)

    def tensor_tensor(self, *a, **k):
        return lambda e: e.tensor_tensor(*a, **k)

    def tensor_scalar(self, *a, **k):
        return lambda e: e.tensor_scalar(*a, **k)

    def scalar_tensor_tensor(self, *a, **k):
        return lambda e: e.scalar_tensor_tensor(*a, **k)

    def tensor_reduce(self, *a, **k):
        return lambda e: e.tensor_reduce(*a, **k)

    def tensor_copy(self, *a, **k):
        return lambda e: e.tensor_copy(*a, **k)

    def reciprocal(self, *a, **k):
        return lambda e: e.reciprocal(*a, **k)

    def memset(self, *a, **k):
        return lambda e: e.memset(*a, **k)

    def bn_stats(self, *a, **k):
        return lambda e: e.bn_stats(*a, **k)

    def bn_aggr(self, *a, **k):
        return lambda e: e.bn_aggr(*a, **k)

    def matmul(self, *a, **k):
        return lambda e: e.matmul(*a, **k)

    def transpose(self, *a, **k):
        return lambda e: e.transpose(*a, **k)

    def dma_start(self, *a, **k):
        return lambda e: e.dma_start(*a, **k)


RECORD = Recorder()


class Lane:

    def __init__(self, name, sem):
        self.name, self.sem, self.n, self.ops, self.seen = name, sem, 0, [], {}

    def wait(self, *toks):
        for t in toks:
            if t is None:
                continue
            if isinstance(t, list):
                self.wait(*t)
                continue
            sem, v = t
            if self.seen.get(id(sem), 0) < v:
                self.seen[id(sem)] = v
                self.ops.append(("w", sem, v))

    def do(self, fn, *toks):
        self.wait(*toks)
        self.n += 1
        self.ops.append(("i", fn(RECORD), self.sem, 1))
        return (self.sem, self.n)

    def go(self, fn, *toks):
        self.wait(*toks)
        self.ops.append(("n", fn(RECORD)))

    def dma(self, fn, count, *toks):
        self.wait(*toks)
        count[1] += 16
        self.ops.append(("i", fn(RECORD), count[0], 16))
        return (count[0], count[1])

    def last(self):
        return (self.sem, self.n) if self.n else None

    def play(self, eng):
        for op in self.ops:
            if op[0] == "w":
                eng.wait_ge(op[1], op[2])
            elif op[0] == "i":
                op[1](eng).then_inc(op[2], op[3])
            else:
                op[1](eng)


class Banks:

    def __init__(self, n):
        self.free = [(i, []) for i in range(n)]

    def take(self):
        return self.free.pop(0)

    def give(self, i, *toks):
        self.free.append((i, list(toks)))


class Ring:

    def __init__(self, n):
        self.n, self.at, self.toks = n, 0, [[] for _ in range(n)]

    def take(self):
        i = self.at % self.n
        self.at += 1
        t, self.toks[i] = self.toks[i], None
        assert t is not None
        return i, t

    def give(self, i, *toks):
        self.toks[i] = list(toks)


class Chunk:

    def __init__(self, i, kt, cols, raw):
        self.i, self.kt, self.cols, self.raw = i, kt, cols, raw


def program(nc, d, plan, stop=None, taps=None):
    listing = []
    ctx = ExitStack()
    with ctx:
        def sb(name, shape, dt=F32, where=None):
            return (where or ctx).enter_context(nc.sbuf_tensor(name, shape, dt))

        def sem(name):
            return ctx.enter_context(nc.semaphore(name))

        PE, A, V, G, S = (Lane(n, sem("done_" + n)) for n in ("pe", "act", "dve", "pool", "sp"))
        LANES = [PE, A, V, G]
        raw_sem = [[sem(f"raw{i}"), 0] for i in range(RAW)]
        load_sems = [[sem(f"load{i}"), 0] for i in range(24)]
        load_at = [0]
        store_sem = [sem("store"), 0]

        ps = ctx.enter_context(nc.psum_tensor("ps", [128, 8, 512], F32))
        X = sb("X", [128, 8, T])
        Hh = sb("Hh", [128, 8, T + TC], F32R)
        Hl = sb("Hl", [128, 8, T + TC], F32R)
        rawb = sb("rawb", [128, RAW, 1024])
        hib = sb("hib", [128, HL, 1024], F32R)
        lob = sb("lob", [128, HL, 1024], F32R)
        Tm = sb("Tm", [128, 4, 512])
        ACC = sb("ACC", [128, T + TC])
        par = sb("par", [128, NPAR])
        con = sb("con", [128, NCONST])
        M = sb("M", [128, 2, 72, 2])
        gm = sb("gm", [128, 8])
        sm = sb("sm", [128, 32, 8])
        ident, ones, blk = con[:, 0:128], con[:, 128:256], con[:, 256:384]

        banks = Banks(8)
        tmp = Ring(4)
        small = Ring(32)
        chunks_done = {}
        hl_done = {}
        ready = {}
        later = []
        state = {"issued": 0, "used": 0, "extra_sem": 0}

        def load(lane, dst, src, *toks):
            s = load_sems[load_at[0]]
            load_at[0] += 1
            return lane.dma(lambda e: e.dma_start(dst, src), s, *toks)

        def p(name, i=0, n=1):
            return par[:, PCOL[name] + i:PCOL[name] + i + n]

        def issue(upto):
            while state["issued"] < min(upto, len(plan)):
                i = state["issued"]
                state["issued"] += 1
                src, kt, cols, raw = plan[i]
                r = rawb[:, i % RAW, 0:kt * cols].rearrange("p (k c) -> p k c", c=cols)
                each = cols // len(src)
                for n, piece in enumerate(src):
                    t = S.dma(lambda e, o=r[:, :, n * each:n * each + each], x=piece: e.dma_start(o, x),
                              raw_sem[i % RAW], chunks_done.get(i - RAW))
                if raw:
                    ready[i] = t
                    continue
                flat = rawb[:, i % RAW, 0:kt * cols]
                hi, lo = hib[:, i % HL, 0:kt * cols], lob[:, i % HL, 0:kt * cols]
                a = A.do(lambda e, hi=hi, flat=flat: e.activation(hi, flat, ACT.Copy), t, hl_done.get(i - HL))
                b = V.do(lambda e, hi=hi, lo=lo, flat=flat: e.tensor_tensor(lo, flat, hi, ALU.subtract),
                         a, hl_done.get(i - HL))
                ready[i] = [a, b]
                chunks_done[i] = [a, b]

        def chunk(src, kt, cols, raw=False):
            listing.append((src, kt, cols, raw))
            c = Chunk(state["used"], kt, cols, raw)
            state["used"] += 1
            if plan is not None:
                issue(c.i + 1 + AHEAD)
            c.ready = ready.get(c.i)
            if raw:
                c.w = rawb[:, c.i % RAW, 0:kt * cols].rearrange("p (k c) -> p k c", c=cols)
            else:
                c.hi = hib[:, c.i % HL, 0:kt * cols].rearrange("p (k c) -> p k c", c=cols)
                c.lo = lob[:, c.i % HL, 0:kt * cols].rearrange("p (k c) -> p k c", c=cols)
            return c

        def used(c, tok):
            hl_done[c.i] = tok
            if c.raw:
                chunks_done[c.i] = tok

        def mm(out, lhsT, rhs, start, stop, *toks, inc=False):
            f = lambda e: e.matmul(out, lhsT, rhs, start=start, stop=stop)
            if inc:
                return PE.do(f, *toks)
            PE.go(f, *toks)

        def run_later():
            todo, later[:] = later[:], []
            for f in todo:
                f()

        def gemm(parts, outs, pick, post):
            got = [banks.take() for _ in outs]
            last_k = parts[-1][1] + parts[-1][2] - 1
            toks = [None] * len(outs)
            for src, k0, kt, cols in parts:
                c = chunk(src, kt, cols)
                for n, o in enumerate(outs):
                    b, free = got[n]
                    for kc in range(kt):
                        k = k0 + kc
                        out, lh, ll, rh, rl, wt = pick(o, c, k, kc)
                        dst = out(b)
                        mm(dst, lh, rh, k == 0, False, c.ready, free if k == 0 else None, wt)
                        mm(dst, lh, rl, False, False)
                        end = kc == kt - 1
                        t = mm(dst, ll, rh, False, k == last_k, inc=end)
                    toks[n] = t
                used(c, t)
                run_later()
                mod_step()
            for n, o in enumerate(outs):
                post(o, got[n][0], toks[n])

        def rows(w, k0, kt, c0, cols):
            return [w.rearrange("(k p) n -> p k n", p=128)[:, k0:k0 + kt, c0:c0 + cols]]

        def k_parts(total):
            return [(k, min(4, total - k)) for k in range(0, total, 4)]

        def gemm_fm(w, kt, cols2, acts, post):
            parts = []
            for k0, n in k_parts(kt):
                if len(cols2) == 1:
                    parts.append((rows(w, k0, n, cols2[0], 128), k0, n, 128))
                elif cols2[1] == cols2[0] + 128:
                    parts.append((rows(w, k0, n, cols2[0], 256), k0, n, 256))
                else:
                    parts.append((rows(w, k0, n, cols2[0], 128) + rows(w, k0, n, cols2[1], 128), k0, n, 256))
            outs = [(n, a) for n in range(len(cols2)) for a in acts]

            def pick(o, c, k, kc):
                n, (_, hi, lo, t0, nt, tk) = o
                return (lambda b: ps[:, b, 0:nt], c.hi[:, kc, 128 * n:128 * n + 128],
                        c.lo[:, kc, 128 * n:128 * n + 128], hi[:, k, t0:t0 + nt], lo[:, k, t0:t0 + nt],
                        tk[k])
            gemm(parts, outs, pick, lambda o, b, t: post(o[0], o[1][0], b, t))

        def gemm_tm(w, kt, c0, cols, act, tiles, post, sub=(0, None)):
            parts = [(rows(w, k0, n, c0, cols), k0, n, cols) for k0, n in
                     (k_parts(kt) if cols > 128 else [(0, kt)])]
            _, hi, lo, t0, _, tk = act
            pass_cols = cols

            def pick(o, c, k, kc):
                a = t0 + 128 * o
                return (lambda b: ps[:, b, 0:pass_cols], hi[:, k, a:a + 128], lo[:, k, a:a + 128],
                        c.hi[:, kc, :], c.lo[:, kc, :], tk[k])
            gemm(parts, list(range(tiles)), pick, post)

        mods = []
        mod_state = {}

        def mod_begin(layer, tok):
            b, free = banks.take()
            mod_state.update(layer=layer, bank=b, free=[free, tok])
            w = d["w_mod_2"][layer]
            mods.extend((w, n) for n in range(72))

        def mod_step():
            if not mods:
                return
            w, n = mods.pop(0)
            c = chunk(rows(w, 0, 8, 128 * n, 128), 8, 128, raw=True)
            b = mod_state["bank"]
            for k in range(8):
                t = mm(ps[:, b, 2 * n:2 * n + 2], c.w[:, k, :], SC[:, k, :], k == 0, k == 7, c.ready,
                       mod_state["free"], inc=k == 7)
            used(c, t)
            mod_state["tok"] = t

        def mod_end():
            while mods:
                mod_step()
            l, b = mod_state["layer"], mod_state["bank"]
            bias = p("b_mod_2", 72 * l, 72)
            for s in range(2):
                src = ps[:, b, 0:144].rearrange("p (n s) -> p n s", s=2)[:, :, s]
                t = V.do(lambda e, s=s, src=src: e.tensor_tensor(M[:, l, :, s], src, bias, ALU.add),
                         mod_state["tok"])
            banks.give(b, t)
            return t

        def mcol(l, i, k, s):
            return M[:, l, 8 * i + k, s:s + 1]

        def square_in(src, t0, nt, k, *toks):
            acc = ACC[:, t0:t0 + nt]
            if k == 0:
                return A.do(lambda e: e.activation(acc, src, ACT.Square), *toks)
            i, free = tmp.take()
            a = A.do(lambda e: e.activation(Tm[:, i, 0:nt], src, ACT.Square), free, *toks[:-1])
            v = V.do(lambda e: e.tensor_tensor(acc, acc, Tm[:, i, 0:nt], ALU.add), a, toks[-1])
            tmp.give(i, v)
            return v

        def rstd_rows(sum_tok, t0, nt, width):
            n = nt // 128
            b, free = banks.take()
            for i in range(n):
                t = mm(ps[:, b, i:i + 1], ACC[:, t0 + 128 * i:t0 + 128 * i + 128], ones[:, 0:1], True, True,
                       sum_tok, free, inc=i == n - 1)
            j, fr = small.take()
            a = A.do(lambda e: e.activation(sm[:, j, 0:n], ps[:, b, 0:n], ACT.Sqrt, bias=eps[:, 0:1],
                                            scale=1.0 / width), t, fr)
            v = V.do(lambda e: e.reciprocal(sm[:, j, 4:4 + n], sm[:, j, 0:n]), a)
            i, free2 = tmp.take()
            for q in range(n):
                w = V.do(lambda e, q=q: e.tensor_scalar(Tm[:, i, 128 * q:128 * q + 128], ident,
                                                       sm[:, j, 4 + q:5 + q], None, ALU.mult), v, free2)
            small.give(j, w)
            t = mm(ps[:, b, 0:nt], ones, Tm[:, i, 0:nt], True, True, w, a, inc=True)
            tmp.give(i, t)
            return b, t, t

        def split_to(src, hi, lo, toks, shift=None, eng=None):
            if shift is None:
                a = A.do(lambda e: e.activation(hi, src, ACT.Copy), *toks)
                v = (eng or V).do(lambda e: e.tensor_tensor(lo, src, hi, ALU.subtract), a, *toks)
            else:
                a = A.do(lambda e: e.activation(hi, src, ACT.Identity, bias=shift), *toks)
                v = V.do(lambda e: e.scalar_tensor_tensor(lo, src, shift, hi, ALU.add, ALU.subtract), a, *toks)
            return a, v

        def norm(src, s0, nt, t0, sum_tok, gain, shift, *toks, dst=None):
            b, t, used_acc = rstd_rows(sum_tok, t0, nt, 1024)
            out = []
            v0 = []
            for k in range(8):
                i, free = tmp.take()
                v = V.do(lambda e, k=k, i=i: e.scalar_tensor_tensor(
                    Tm[:, i, 0:nt], src[:, k, s0:s0 + nt], gain(k), ps[:, b, 0:nt], ALU.mult, ALU.mult),
                    t, free, *toks)
                v0.append(v)
                hi, lo = Hh[:, k, t0:t0 + nt], Hl[:, k, t0:t0 + nt]
                a, w = split_to(Tm[:, i, 0:nt], hi, lo, [v, *toks], shift(k) if shift else None)
                tmp.give(i, w, a)
                out.append([a, w])
            banks.give(b, v0[-1])
            return out, [v0[-1], out[-1][1], used_acc]

        def head_norm(b, tok, width, nt, gain, out, blocked=True, *toks):
            i, free = tmp.take()
            a = A.do(lambda e: e.activation(Tm[:, i, 0:nt], ps[:, b, 0:nt], ACT.Square), tok, free)

            def second():
                b2, fr = banks.take()
                t = mm(ps[:, b2, 0:nt], blk if blocked else ones, Tm[:, i, 0:nt], True, True, a, fr, inc=True)
                r = A.do(lambda e: e.activation(Tm[:, i, 0:nt], ps[:, b2, 0:nt], ACT.Sqrt,
                                                bias=eps[:, 0:1], scale=1.0 / width), t)
                v = V.do(lambda e: e.reciprocal(Tm[:, i, 0:nt], Tm[:, i, 0:nt]), r)
                for q, o in out[0]:
                    w = V.do(lambda e, q=q, o=o: e.scalar_tensor_tensor(
                        o, ps[q, b, 0:nt], gain[q], Tm[q, i, 0:nt], ALU.mult, ALU.mult), v, *toks)
                tmp.give(i, w)
                banks.give(b2, r)
                banks.give(b, w)
                out[1](w)
            later.append(second)

        def tap(name, ap, *toks):
            if taps is not None and name in taps:
                t = A.dma(lambda e: e.dma_start(taps[name], ap), store_sem, *toks)
                for lane in LANES:
                    lane.wait(t)

        def fence():
            ts = [l.last() for l in LANES]
            for l in LANES:
                l.wait(*ts)

        def softmax(b, n, tok, P, i, free, scale=1.0):
            j, fr = small.take()
            v = V.do(lambda e: e.tensor_reduce(sm[:, j, 0:1], ps[:, b, 0:n], AX.X, ALU.max, negate=True),
                     tok, fr)
            bias = sm[:, j, 0:1]
            if scale != 1.0:
                v = V.do(lambda e: e.tensor_scalar(sm[:, j, 2:3], sm[:, j, 0:1], scale, None, ALU.mult), v)
                bias = sm[:, j, 2:3]
            a = A.do(lambda e: e.activation(P[:, i, 0:n], ps[:, b, 0:n], ACT.Exp, bias=bias, scale=scale,
                                            accum_out=sm[:, j, 1:2]), v, free)
            banks.give(b, a)
            return j, a

        flip = [0]

        def turn(P, i, n, tok, PT, pring, ptring):
            b, free = banks.take()
            for k in range(n // 128):
                t = (PE.do if k == n // 128 - 1 else PE.go)(
                    lambda e, k=k: e.transpose(ps[:, b, 128 * k:128 * k + 128], P[:, i, 128 * k:128 * k + 128],
                                               ident), tok, free)
            pring.give(i, t)
            m, fr = ptring.take()
            flip[0] += 1
            lane = (V, A)[flip[0] % 2]
            f = ((lambda e: e.tensor_copy(PT[:, m, 0:n], ps[:, b, 0:n])) if lane is V else
                 (lambda e: e.activation(PT[:, m, 0:n], ps[:, b, 0:n], ACT.Copy)))
            v = lane.do(f, t, fr)
            banks.give(b, v)
            return m, v

        def pipeline(units, stages, skew):
            box = [{} for _ in units]
            for step in range(len(units) + skew[-1]):
                for s, f in enumerate(stages):
                    u = step - skew[s]
                    if 0 <= u < len(units):
                        f(units[u], box[u])

        eps = sb("eps", [128, 1])
        SC = sb("SC", [128, 8, 2])
        t_con = load(A, con[:, :], d["con"])
        t_par = load(A, par[:, :], d["par"])
        t_x = load(G, X[:, :, :], d["x"].rearrange("(k p) t -> p k t", p=128))
        t_eps = V.do(lambda e: e.memset(eps[:, :], EPS))
        start = [t_con, t_par, t_eps]
        for l in LANES:
            l.wait(*start)
        t_sc = A.do(lambda e: e.activation(SC[:, :, :].rearrange("p k s -> p (k s)"), p("cc_2", 0, 16),
                                           ACT.Silu))
        mod_begin(0, t_sc)

        s1 = ctx.enter_context(ExitStack())
        U = sb("U", [128, 4, 512], where=s1)
        VV = sb("VV", [128, 4, 512], where=s1)
        sgw = sb("sgw", [128, 8, 128], where=s1)
        QT = sb("QT", [128, 4, 512], where=s1)
        KS = sb("KS", [128, 2, 512], where=s1)
        KW = sb("KW", [128, 2, 512], where=s1)
        KC2 = sb("KC2", [128, 2, 2, 512], where=s1)
        XIN = sb("XIN", [128, 16, 2, 31], where=s1)
        HC = sb("HC", [128, 2, 2, 62], where=s1)
        KCT = sb("KCT", [128, 2, 31], where=s1)
        VC = sb("VC", [128, 2, 64], where=s1)
        VS = sb("VS", [128, 4, 128], where=s1)
        VW = sb("VW", [128, 4, 128], where=s1)
        OB = sb("OB", [128, 4, 512], where=s1)
        P = sb("P", [128, 4, 512], where=s1)
        PT = sb("PT", [128, 4, 512], where=s1)
        GA = sb("GA", [128, 4, 24], where=s1)
        rowp = sb("rowp", [128, 1088], where=s1)
        c1 = sb("c1", [128, NC1], where=s1)
        W2 = sb("W2", [128, 2, 2, 128], where=s1)
        ms = sb("ms", [128, 32], where=s1)
        t_row = load(A, rowp[:, :], d["rows"])
        t_c1 = load(A, c1[:, :], d["c1"])
        t_sgw = load(G, sgw[:, :, :], d["sg_w"])
        t_w2 = load(G, W2[:, :, :, :], d["cmp_w2"])
        kz = [G.do(lambda e, x=x: e.memset(x[:, :, :], 0.0)) for x in (KS, KW, KCT)]
        causal = c1[:, C1_CAUSAL:C1_CAUSAL + 128]

        tk = t_x
        for k in range(8):
            tk = square_in(X[:, k, :], 0, T, k, t_x, tk)
        hx, _ = norm(X, 0, T, 0, tk, lambda k: p("norm_mix_g", k), None, t_x)
        ax = ("x", Hh, Hl, 0, T, hx)
        w_in = d["w_in"]

        u_tok, v_tok = [], []
        for dst, c0, box in ((VV, 512, v_tok), (U, 0, u_tok)):
            for half in range(2):
                def post(i, b, t, dst=dst, half=half, box=box):
                    a = A.do(lambda e: e.activation(dst[:, i, 256 * half:256 * half + 256], ps[:, b, 0:256],
                                                    ACT.Gelu_apprx_tanh), t)
                    banks.give(b, a)
                    box.append(a)
                gemm_tm(w_in, 8, c0 + 256 * half, 256, ax, 4, post)

        sgm = V.do(lambda e: e.tensor_tensor(sgw[:, :, :], sgw[:, :, :],
                                             c1[:, C1_SGU:C1_SGU + 128].unsqueeze(1).to_broadcast([128, 8, 128]),
                                             ALU.mult), t_sgw, t_c1)
        lane_toks = []
        for i in range(4):
            row = VV[:, i, :]
            j, fr = small.take()
            j2, fr2 = small.take()
            v = V.do(lambda e, j=j, row=row: e.bn_stats(sm[:, j, 0:6], row), v_tok, fr)
            v = V.do(lambda e, j=j, j2=j2: e.bn_aggr(sm[:, j2, 0:2], sm[:, j, 0:6]), v, fr2)
            a = A.do(lambda e, j2=j2: e.activation(sm[:, j2, 2:3], sm[:, j2, 1:2], ACT.Sqrt, bias=eps[:, 0:1],
                                                   scale=1.0), v)
            v = V.do(lambda e, j2=j2: e.reciprocal(sm[:, j2, 3:4], sm[:, j2, 2:3]), a)
            v = V.do(lambda e, j2=j2, row=row: e.tensor_scalar(row, row, sm[:, j2, 0:1], sm[:, j2, 3:4],
                                                               ALU.subtract, ALU.mult), v)
            small.give(j, v)
            small.give(j2, v)
            g = G.do(lambda e, row=row: e.tensor_tensor(row, row, rowp[:, 0:512], ALU.mult), v, t_row)
            g = G.do(lambda e, row=row: e.tensor_tensor(row, row, rowp[:, 512:1024], ALU.add), g)
            lane_toks.append(g)

        gq = V.do(lambda e: e.tensor_scalar(gm[:, 0:1], p("q_norm_g"), 0.125, None, ALU.mult))
        q_toks, k_toks = [], {}
        for pair in range(2):
            def post(n, s, b, t, pair=pair):
                head_norm(b, t, 64, T, gm[:, 0:1], ([(slice(0, 128), QT[:, 2 * pair + n, :])], q_toks.append), True, gq)
            gemm_fm(w_in, 8, [1024 + 256 * pair, 1152 + 256 * pair], [ax], post)

        c_toks = [[], []]

        def post(n, s, b, t):
            last = []
            for h in range(2):
                src = ps[64 * h:64 * h + 64, b, :]
                a = A.do(lambda e, h=h, src=src: e.activation(KC2[0:64, n, h, :], src, ACT.Copy), t)
                v = V.do(lambda e, h=h, src=src: e.tensor_copy(KC2[64:128, n, h, 0:511], src[:, 1:512]), t, a)
                last += [a, v]
            banks.give(b, *last)
            c_toks[n] += last
        gemm_fm(w_in, 8, [1536, 1664], [ax], post)

        kv_v = []
        for n, (kdst, vdst, gi) in enumerate(((KS, VS, 1), (KW, VW, 2))):
            c0 = 1792 + 256 * n
            got = [banks.take() for _ in range(5)]
            for k0, kt in k_parts(8):
                c = chunk(rows(w_in, k0, kt, c0, 256), kt, 256)
                for kc in range(kt):
                    k = k0 + kc
                    b, free = got[4]
                    mm(ps[:, b, :], c.hi[:, kc, 0:128], Hh[:, k, 0:T], k == 0, False, c.ready, free, hx[k])
                    mm(ps[:, b, :], c.hi[:, kc, 0:128], Hl[:, k, 0:T], False, False)
                    t = mm(ps[:, b, :], c.lo[:, kc, 0:128], Hh[:, k, 0:T], False, k == 7, inc=True)
                kt_tok = t
                vts = []
                for i in range(4):
                    b, free = got[i]
                    for kc in range(kt):
                        k = k0 + kc
                        h_, l_ = Hh[:, k, 128 * i:128 * i + 128], Hl[:, k, 128 * i:128 * i + 128]
                        mm(ps[:, b, 0:128], h_, c.hi[:, kc, 128:256], k == 0, False, free)
                        mm(ps[:, b, 0:128], h_, c.lo[:, kc, 128:256], False, False)
                        t = mm(ps[:, b, 0:128], l_, c.hi[:, kc, 128:256], False, k == 7, inc=True)
                    vts.append(t)
                used(c, t)
                run_later()
                mod_step()
            for i in range(4):
                b = got[i][0]
                v = V.do(lambda e, b=b, i=i, vdst=vdst: e.tensor_copy(vdst[:, i, :], ps[:, b, 0:128]), vts[i])
                banks.give(b, v)
                kv_v.append(v)
            head_norm(got[4][0], kt_tok, 64, T, p("k_norm_g", gi),
                      ([(slice(64 * h, 64 * h + 64), kdst[64 * h:64 * h + 64, h, :]) for h in range(2)],
                       lambda w, n=n: k_toks.update({n: w})), True, kz)

        g_toks = []

        def post(i, b, t):
            a = A.do(lambda e: e.activation(GA[:, i, :], ps[:, b, 0:24], ACT.Sigmoid), t)
            banks.give(b, a)
            g_toks.append(a)
        gemm_tm(w_in, 8, 2304, 24, ax, 4, post)
        run_later()
        run_later()
        tap("QT", QT[:, :, :], q_toks)
        tap("KS", KS[:, :, :], k_toks[0])
        tap("VS", VS[:, :, :], kv_v)
        tap("GA", GA[:, :, :], g_toks)
        tap("VV", VV[:, :, :], lane_toks)

        a_toks = []
        for g in range(8):
            b, free = banks.take()
            t = mm(ps[:, b, 0:256].rearrange("p (c x) -> p c x", x=64), sgw[:, g, :], VV[:, :, 64 * g:64 * g + 64],
                   True, True, sgm, lane_toks, free, inc=True)
            uu = U[:, :, 64 * g:64 * g + 64]
            v = V.do(lambda e, b=b, g=g, uu=uu: e.scalar_tensor_tensor(
                uu, ps[:, b, 0:256].rearrange("p (c x) -> p c x", x=64), p("sg_b", g), uu, ALU.add, ALU.mult),
                t, u_tok)
            banks.give(b, v)
            a_toks.append(v)
        tap("U", U[:, :, :], a_toks)

        def to_mixed(src, i, k0, gcol, toks, j):
            q, free = tmp.take()
            a = A.do(lambda e: e.activation(Tm[:, q, :], src[:, i, :], ACT.Square, accum_out=ms[:, j:j + 1]),
                     free, toks)
            a = A.do(lambda e: e.activation(ms[:, 8 + j:9 + j], ms[:, j:j + 1], ACT.Sqrt, bias=eps[:, 0:1],
                                            scale=1.0 / 512), a)
            v = V.do(lambda e: e.reciprocal(ms[:, 16 + j:17 + j], ms[:, 8 + j:9 + j]), a)
            v = V.do(lambda e: e.tensor_scalar(Tm[:, q, :], src[:, i, :], ms[:, 16 + j:17 + j], None, ALU.mult), v)
            b, fr = banks.take()
            for k in range(4):
                t = (PE.do if k == 3 else PE.go)(
                    lambda e, k=k: e.transpose(ps[:, b, 128 * k:128 * k + 128], Tm[:, q, 128 * k:128 * k + 128],
                                               ident), v, fr)
            out = []
            for k in range(4):
                hi = Hh[:, k0 + k, 128 * i:128 * i + 128]
                pk = ps[:, b, 128 * k:128 * k + 128]
                a = A.do(lambda e, hi=hi, pk=pk, k=k: e.activation(hi, pk, ACT.Copy, scale=gcol(k)), t,
                         h_free)
            for k in range(4):
                hi = Hh[:, k0 + k, 128 * i:128 * i + 128]
                lo = Hl[:, k0 + k, 128 * i:128 * i + 128]
                pk = ps[:, b, 128 * k:128 * k + 128]
                v = V.do(lambda e, hi=hi, lo=lo, pk=pk, k=k: e.scalar_tensor_tensor(
                    lo, pk, gcol(k), hi, ALU.mult, ALU.subtract), a)
                out += [a, v]
            tmp.give(q, t)
            banks.give(b, *out)
            return out

        h_free = [PE.last()]
        mix = [[] for _ in range(8)]
        for i in range(4):
            o = to_mixed(U, i, 0, lambda k: p("mix_out_g", k), a_toks, i)
            for k in range(4):
                mix[k] += o

        for n in range(2):
            if n:
                XIN_free = hc_tok
            x_t = []
            for h in range(2):
                src = KC2[:, n, h, 0:496]
                for part in range(2):
                    s2 = KC2[:, n, h, 16 * part:16 * part + 496].rearrange("p (m j e) -> p j m e", m=31, e=2)[:, :, :, 0]
                    po = p("cmp_pos", 16 * n + 8 * part, 8).unsqueeze(2).to_broadcast([128, 8, 31])
                    v = V.do(lambda e, s2=s2, po=po, h=h, part=part: e.tensor_tensor(
                        XIN[:, 8 * part:8 * part + 8, h, :], s2, po, ALU.add), c_toks[n],
                        XIN_free if n else None)
                    x_t.append(v)
            b0, f0 = banks.take()
            b1, f1 = banks.take()
            w1 = d["cmp_w1"][n].rearrange("(j p) n -> p j n", p=128)
            for q in range(4):
                c = chunk([w1[:, 4 * q:4 * q + 4, :]], 4, 256, raw=True)
                for half, b, f in ((0, b0, f0), (1, b1, f1)):
                    for jj in range(4):
                        j = 4 * q + jj
                        t = mm(ps[:, b, 0:62], c.w[:, jj, 128 * half:128 * half + 128],
                               XIN[:, j, :, :].rearrange("p h m -> p (h m)"), j == 0, j == 15,
                               c.ready, x_t, f, inc=jj == 3)
                    if half == 0:
                        t0_ = t
                used(c, t)
            hc_tok = [t0_, t]
            hh = []
            for half, b, tt in ((0, b0, t0_), (1, b1, t)):
                a = A.do(lambda e, half=half, b=b, n=n: e.activation(
                    HC[:, n, half, :], ps[:, b, 0:62], ACT.Gelu_apprx_tanh, bias=p("cmp_b1", 2 * n + half),
                    scale=1.0), tt)
                banks.give(b, a)
                hh.append(a)
            if n == 0:
                b, f = banks.take()
                for half in range(2):
                    t = mm(ps[:, b, 0:62], W2[:, 0, half, :], HC[:, 0, half, :], half == 0, half == 1, hh, t_w2,
                           f, inc=half == 1)
                j, fr = tmp.take()
                kc = Tm[:, j, 0:62]
                sq = Tm[:, j, 64:126]
                a = A.do(lambda e: e.activation(kc, ps[:, b, 0:62], ACT.Identity, bias=p("cmp_b2")), t, fr)
                a2 = A.do(lambda e: e.activation(sq, kc, ACT.Square), a)
                banks.give(b, a)
                b, f = banks.take()
                t = mm(ps[:, b, 0:62], blk, sq, True, True, a2, f, inc=True)
                a = A.do(lambda e: e.activation(Tm[:, j, 128:190], ps[:, b, 0:62], ACT.Sqrt, bias=eps[:, 0:1],
                                                scale=1.0 / 64), t)
                v = V.do(lambda e: e.reciprocal(Tm[:, j, 192:254], Tm[:, j, 128:190]), a)
                banks.give(b, a)
                kct = []
                for h in range(2):
                    r = slice(64 * h, 64 * h + 64)
                    kct.append(V.do(lambda e, r=r, h=h: e.scalar_tensor_tensor(
                        KCT[r, h, :], Tm[r, j, 31 * h:31 * h + 31], p("k_norm_g", 0)[r],
                        Tm[r, j, 192 + 31 * h:192 + 31 * h + 31], ALU.mult, ALU.mult), v, kz))
                tmp.give(j, *kct)
            else:
                vct = []
                for h in range(2):
                    b, f = banks.take()
                    for half in range(2):
                        t = mm(ps[0:31, b, 0:64], HC[:, 1, half, 31 * h:31 * h + 31], W2[:, 1, half, 0:64],
                               half == 0, half == 1, hh, t_w2, f, inc=half == 1)
                    v = V.do(lambda e, b=b, h=h: e.tensor_tensor(VC[0:31, h, :], ps[0:31, b, 0:64],
                                                                 rowp[0:31, 1024:1088], ALU.add), t)
                    banks.give(b, v)
                    vct.append(v)
        tap("KCT", KCT[:, :, :], kct)
        tap("VC", VC[0:31, :, :], vct)

        pr, ptr = Ring(4), Ring(4)
        ob = {}

        def gate(i, h, br):
            return GA[:, i, 3 * h + br:3 * h + br + 1]

        def c_scores(i, box):
            b, f = banks.take()
            for h in range(8):
                t = mm(ps[:, b, 32 * h:32 * h + 31], QT[:, h % 4, 128 * i:128 * i + 128], KCT[:, h // 4, :], True, True,
                       q_toks, kct, f, inc=h == 7)
            s3 = ps[:, b, 0:256].rearrange("p (h n) -> p h n", n=32)[:, :, 0:31]
            mk = c1[:, C1_CMP + 31 * i:C1_CMP + 31 * i + 31].unsqueeze(1).to_broadcast([128, 8, 31])
            v = V.do(lambda e: e.tensor_tensor(s3, s3, mk, ALU.add), t)
            j, fr = small.take()
            j2, fr2 = small.take()
            v = V.do(lambda e: e.tensor_reduce(sm[:, j, :], s3, AX.X, ALU.max), v, fr)
            v = V.do(lambda e: e.tensor_scalar(sm[:, j, :], sm[:, j, :], -1e29, None, ALU.max), v)
            q, fq = pr.take()
            P3 = P[:, q, 0:256].rearrange("p (h n) -> p h n", n=32)
            vz = V.do(lambda e: e.memset(P[:, q, 0:256], 0.0), fq)
            v = V.do(lambda e: e.tensor_tensor(P3[:, :, 0:31], s3, sm[:, j, :].unsqueeze(2).to_broadcast([128, 8, 31]),
                                               ALU.subtract), v, vz)
            banks.give(b, v)
            a = A.do(lambda e: e.activation(P3[:, :, 0:31], P3[:, :, 0:31], ACT.Exp), v)
            v = V.do(lambda e: e.tensor_reduce(sm[:, j2, :], P3[:, :, 0:31], AX.X, ALU.add), a, fr2)
            v = V.do(lambda e: e.tensor_scalar(sm[:, j2, :], sm[:, j2, :], 1e-6, None, ALU.max), v)
            v = V.do(lambda e: e.reciprocal(sm[:, j, :], sm[:, j2, :]), v)
            g8 = GA[:, i, :].rearrange("p (h b) -> p h b", b=3)[:, :, 0]
            v = V.do(lambda e: e.tensor_tensor(sm[:, j2, :], sm[:, j, :], g8, ALU.mult), v, g_toks)
            small.give(j, v)
            box.update(q=q, j=j2, t=[a, v])

        def c_turn(i, box):
            q = box["q"]
            b, f = banks.take()
            b2, f2 = banks.take()
            for h in range(8):
                t = (PE.do if h == 7 else PE.go)(
                    lambda e, h=h: e.transpose(ps[0:32, (b, b2)[h // 4], 128 * (h % 4):128 * (h % 4) + 128],
                                               P[:, q, 32 * h:32 * h + 32], ident), box["t"], f, f2)
            pr.give(q, t)
            m, fm_ = ptr.take()
            m2, fm2 = ptr.take()
            v = V.do(lambda e: e.tensor_copy(PT[0:32, m, :], ps[0:32, b, :]), t, fm_)
            a = A.do(lambda e: e.activation(PT[0:32, m2, :], ps[0:32, b2, :], ACT.Copy), t, fm2)
            banks.give(b, v)
            banks.give(b2, a)
            box.update(m=(m, m2), t2=[v, a])

        def c_out(i, box):
            b, f = banks.take()
            for h in range(8):
                t = mm(ps[:, b, 64 * h:64 * h + 64], PT[0:31, box["m"][h // 4], 128 * (h % 4):128 * (h % 4) + 128],
                       VC[0:31, h // 4, :], True, True, box["t2"], vct, f, inc=h == 7)
            ptr.give(box["m"][0], t)
            ptr.give(box["m"][1], t)
            o3 = ps[:, b, :].rearrange("p (h x) -> p h x", x=64)
            v = V.do(lambda e: e.tensor_tensor(OB[:, i, :].rearrange("p (h x) -> p h x", x=64), o3,
                                               sm[:, box["j"], :].unsqueeze(2).to_broadcast([128, 8, 64]), ALU.mult), t)
            small.give(box["j"], v)
            banks.give(b, v)
            for h in range(8):
                ob[i, h] = v
        pipeline(list(range(4)), [c_scores, c_turn, c_out], [0, 1, 2])
        tap("OB0", OB[:, :, :], [ob[i, 0] for i in range(4)])

        def f_scores(u, box):
            i, h, br = u
            n = 128 * (i + 1)
            kk = (KS, KW)[br - 1]
            b, f = banks.take()
            mm(ps[:, b, 0:n], QT[:, h % 4, 128 * i:128 * i + 128], kk[:, h // 4, 0:n], True, False, q_toks,
               k_toks[br - 1], f)
            t = mm(ps[:, b, n - 128:n], ident, causal, False, True, inc=True)
            q, fq = pr.take()
            j, a = softmax(b, n, t, P, q, fq)
            v = V.do(lambda e: e.reciprocal(sm[:, j, 3:4], sm[:, j, 1:2]), a)
            v = V.do(lambda e: e.tensor_tensor(sm[:, j, 4:5], sm[:, j, 3:4], gate(i, h, br), ALU.mult), v)
            box.update(q=q, j=j, t=a, v=v)

        def f_turn(u, box):
            box["m"], box["t2"] = turn(P, box["q"], 128 * (u[0] + 1), box["t"], PT, pr, ptr)

        def f_out(u, box):
            i, h, br = u
            vv = (VS, VW)[br - 1]
            b, f = banks.take()
            m = box["m"]
            for k in range(i + 1):
                t = mm(ps[:, b, 0:64], PT[:, m, 128 * k:128 * k + 128], vv[:, k, 64 * (h // 4):64 * (h // 4) + 64],
                       k == 0, k == i, box["t2"], kv_v, f, inc=k == i)
            ptr.give(m, t)
            o = OB[:, i, 64 * h:64 * h + 64]
            v = V.do(lambda e: e.scalar_tensor_tensor(o, ps[:, b, 0:64], sm[:, box["j"], 4:5], o, ALU.mult,
                                                      ALU.add), t, box["v"], ob[i, h])
            small.give(box["j"], v)
            banks.give(b, v)
            ob[i, h] = v
        pipeline([(i, h, br) for i in range(4) for h in range(8) for br in (1, 2)],
                 [f_scores, f_turn, f_out], [0, 2, 3])
        tap("OB", OB[:, :, :], [ob[i, h] for i in range(4) for h in range(8)])
        for i in range(4):
            o = to_mixed(OB, i, 4, lambda k: p("mix_out_g", 4 + k), [ob[i, h] for h in range(8)], 4 + i)
            for k in range(4):
                mix[4 + k] += o

        xt = {("x", k): t_x for k in range(8)}
        sums = {}

        def residual(w, kt, acts, coef, C=None, first=True, final=True, k_base=0, extra=None):
            def post(n, s, b, t, n0=None):
                k = n0 + n
                dst, nt, t0 = (X, T, 0) if s == "x" else (C, TC, T)
                o = dst[:, k, :]
                cf = coef(k, s)
                if cf is None:
                    v = V.do(lambda e: e.tensor_tensor(o, ps[:, b, 0:nt], o, ALU.add), t, xt[s, k], extra)
                else:
                    v = V.do(lambda e: e.scalar_tensor_tensor(o, ps[:, b, 0:nt], cf, o, ALU.mult, ALU.add),
                             t, xt[s, k], extra)
                xt[s, k] = v
                banks.give(b, v)
                if final:
                    sums[s] = square_in(o, t0, nt, k, v, sums.get((s, "free"), []) if k == 0 else sums[s])
            for pair in range(4):
                gemm_fm(w, kt, [256 * pair, 256 * pair + 128], acts,
                        lambda n, s, b, t, pair=pair: post(n, s, b, t, 2 * pair))

        am = ("x", Hh, Hl, 0, T, mix)
        residual(d["w_out"], 8, [am], lambda k, s: None)
        tap("X1", X[:, :, :], [xt["x", k] for k in range(8)])
        if stop == 1:
            pass
        fence()
        s1.close()

        s2 = ctx.enter_context(ExitStack())
        MT = sb("MT", [128, 8, TC], where=s2)
        MQ = sb("MQ", [128, 4, T], where=s2)
        MK = sb("MK", [128, 4, TC], where=s2)
        MV = sb("MV", [128, 2, 512], where=s2)
        P = sb("P2", [128, 4, 512], where=s2)
        PT = sb("PT2", [128, 16, 256], where=s2)
        t_m = load(G, MT[:, :, :], d["mem"].rearrange("(k p) t -> p k t", p=128))
        tk = t_m
        for k in range(8):
            tk = square_in(MT[:, k, :], T, TC, k, t_m, tk)
        hm, mdone = norm(MT, 0, TC, T, tk, lambda k: p("mem_kv_norm_g", k), None, t_m)
        amem = ("c", Hh, Hl, T, TC, hm)
        mk_toks, mq_toks, mv_toks = [], [], []
        w_mkv = d["w_mkv"]
        for pair in range(2):
            def post(n, s, b, t, pair=pair):
                head_norm(b, t, 128, TC, p("mem_k_norm_g"), ([(slice(0, 128), MK[:, 2 * pair + n, :])], mk_toks.append), False)
            gemm_fm(w_mkv, 8, [256 * pair, 256 * pair + 128], [amem], post)
        for half in range(2):
            def post(i, b, t, half=half):
                v = V.do(lambda e: e.tensor_copy(MV[:, i, 256 * half:256 * half + 256], ps[:, b, 0:256]), t)
                banks.give(b, v)
                mv_toks.append(v)
            gemm_tm(w_mkv, 8, 512 + 256 * half, 256, amem, 2, post)
        h1, h1done = norm(X, 0, T, 0, sums["x"], lambda k: p("norm_mem_g", k), None)
        sums["x", "free"] = h1done
        ax = ("x", Hh, Hl, 0, T, h1)
        for pair in range(2):
            def post(n, s, b, t, pair=pair):
                head_norm(b, t, 128, T, p("mem_q_norm_g"), ([(slice(0, 128), MQ[:, 2 * pair + n, :])], mq_toks.append), False)
            gemm_fm(d["w_mq"], 8, [256 * pair, 256 * pair + 128], [ax], post)
        run_later()
        run_later()
        h_free = [PE.last()]
        pr = Ring(4)
        ms_scale = 128.0 ** -0.5
        ptoks = {}

        def m_scores(u, box):
            h, i = u
            b, f = banks.take()
            t = mm(ps[:, b, 0:TC], MQ[:, h, 128 * i:128 * i + 128], MK[:, h, :], True, True, mq_toks, mk_toks,
                   f, inc=True)
            q, fq = pr.take()
            j, a = softmax(b, TC, t, P, q, fq, scale=ms_scale)
            v = V.do(lambda e: e.reciprocal(sm[:, j, 3:4], sm[:, j, 1:2]), a)
            v = V.do(lambda e: e.tensor_scalar(P[:, q, 0:TC], P[:, q, 0:TC], sm[:, j, 3:4], None, ALU.mult), v)
            small.give(j, v)
            box.update(q=q, t=v)

        def m_turn(u, box):
            h, i = u
            b, f = banks.take()
            for k in range(2):
                t = (PE.do if k == 1 else PE.go)(
                    lambda e, k=k: e.transpose(ps[:, b, 128 * k:128 * k + 128],
                                               P[:, box["q"], 128 * k:128 * k + 128], ident), box["t"], f)
            pr.give(box["q"], t)
            dst = PT[:, 4 * h:4 * h + 4, :].rearrange("p a b -> p (a b)").rearrange("p (k t) -> p k t", k=2)[
                :, :, 128 * i:128 * i + 128]
            src = ps[:, b, 0:256].rearrange("p (k t) -> p k t", k=2)
            v = V.do(lambda e: e.tensor_copy(dst, src), t)
            banks.give(b, v)
            ptoks.setdefault(h, []).append(v)

        ho = [[] for _ in range(4)]

        def m_out(u, box):
            h, i = u
            if i != 3:
                return
            b, f = banks.take()
            pt = PT[:, 4 * h:4 * h + 4, :].rearrange("p a b -> p (a b)").rearrange("p (k t) -> p k t", k=2)
            for k in range(2):
                t = mm(ps[:, b, :], MV[:, k, 128 * h:128 * h + 128], pt[:, k, :], k == 0, k == 1, ptoks[h],
                       mv_toks, f, inc=k == 1)
            a, v = split_to(ps[:, b, :], Hh[:, h, 0:T], Hl[:, h, 0:T], [t, *h_free])
            banks.give(b, a, v)
            ho[h] = [a, v]
        pipeline([(h, i) for h in range(4) for i in range(4)], [m_scores, m_turn, m_out], [0, 2, 3])
        residual(d["w_mo"], 4, [("x", Hh, Hl, 0, T, ho)], lambda k, s: None)
        tap("X2", X[:, :, :], [xt["x", k] for k in range(8)])
        fence()
        s2.close()

        s3 = ctx.enter_context(ExitStack())
        C = None
        Gh = sb("Gh", [128, 11, T + TC], F32R, where=s3)
        Gl = sb("Gl", [128, 11, T + TC], F32R, where=s3)
        h1, h1done = norm(X, 0, T, 0, sums["x"], lambda k: p("norm_ffn_g", k), None)
        sums["x", "free"] = h1done
        ax = ("x", Hh, Hl, 0, T, h1)
        g_free = [None]
        for part in range(4):
            gt = [[] for _ in range(8)]
            for pair in range(4):
                def post(n, s, b, t, pair=pair):
                    k = 2 * pair + n
                    i, fr = tmp.take()
                    a = A.do(lambda e: e.activation(Tm[:, i, :], ps[:, b, :], ACT.Relu), t, fr)
                    banks.give(b, a)
                    v = V.do(lambda e: e.tensor_tensor(Tm[:, i, :], Tm[:, i, :], Tm[:, i, :], ALU.mult), a)
                    a, v = split_to(Tm[:, i, :], Gh[:, k, 0:T], Gl[:, k, 0:T], [v, *g_free])
                    tmp.give(i, a, v)
                    gt[k] = [a, v]
                gemm_fm(d["w_ff1"], 8, [1024 * part + 256 * pair, 1024 * part + 256 * pair + 128], [ax], post)
            residual(d["w_ff2"][1024 * part:1024 * part + 1024, :], 8, [("x", Gh, Gl, 0, T, gt)],
                     lambda k, s: None, final=part == 3)
            g_free = [PE.last()]
        tap("X3", X[:, :, :], [xt["x", k] for k in range(8)])
        mod_tok = mod_end()
        fence()
        s3.close()

        sC = ctx.enter_context(ExitStack())
        C = sb("C", [128, 8, TC], where=sC)
        t_c = load(G, C[:, :, :], d["ctx_2"].rearrange("(k p) t -> p k t", p=128))
        for k in range(8):
            xt["c", k] = t_c
        tk = t_c
        for k in range(8):
            tk = square_in(C[:, k, :], T, TC, k, t_c, tk)
        sums["c"] = tk

        CF = sb("CF", [128, 6, 8, 2])

        def mod_norm_cols(l, i):
            out = []
            for s in range(2):
                g = p("norm_g_2", 24 * l + 8 * i, 8)
                mm_ = M[:, l, 8 * (3 * i + 1):8 * (3 * i + 2), s]
                mg = M[:, l, 8 * (3 * i + 2):8 * (3 * i + 3), s]
                half = 1.0 if i == 1 else 0.5
                out.append(V.do(lambda e, s=s, g=g, mm_=mm_: e.scalar_tensor_tensor(
                    CF[:, i, :, s], mm_, 1.0, g, ALU.add, ALU.mult), mod_tok, *cf_free))
                out.append(V.do(lambda e, s=s, mg=mg: e.tensor_scalar(CF[:, 3 + i, :, s], mg, half, None, ALU.mult),
                                *cf_free))
            return out

        SI = {"x": 0, "c": 1}

        def norm2(l, i, sets):
            acts = []
            for s in sets:
                src, nt, t0 = (X, T, 0) if s == "x" else (C, TC, T)
                toks, done = norm(src, 0, nt, t0, sums[s],
                                  lambda k, s=s: CF[:, i, k, SI[s]:SI[s] + 1],
                                  lambda k, s=s: mcol(l, 3 * i, k, SI[s]),
                                  *cf_tok, [xt[s, k] for k in range(8)], h_free2)
                sums[s, "free"] = done
                acts.append((s, Hh, Hl, t0, nt, toks))
            return acts

        def ffn(l, j, i, sets, tokname):
            s4 = ctx.enter_context(ExitStack())
            Gh = sb(f"Gh{tokname}", [128, 11, T + TC], F32R, where=s4)
            Gl = sb(f"Gl{tokname}", [128, 11, T + TC], F32R, where=s4)
            acts = norm2(l, i, sets)
            g_free = [None]
            w1, w2 = d["ffn_w_in_2"][l, j], d["ffn_w_out_2"][l, j]
            for part in range(2):
                gt = {s: [None] * 11 for s in sets}
                for f in range(11):
                    fc = 11 * part + f
                    box = {}

                    def post(n, s, b, t, f=f, box=box, gt=gt):
                        if n == 0:
                            box[s] = (b, t)
                            return
                        ba, ta = box[s]
                        nt, t0 = (T, 0) if s == "x" else (TC, T)
                        q, fr = tmp.take()
                        a = A.do(lambda e: e.activation(Tm[:, q, 0:nt], ps[:, ba, 0:nt], ACT.Silu), ta, fr)
                        banks.give(ba, a)
                        v = V.do(lambda e: e.tensor_tensor(Tm[:, q, 0:nt], Tm[:, q, 0:nt], ps[:, b, 0:nt], ALU.mult),
                                 a, t)
                        banks.give(b, v)
                        a, v = split_to(Tm[:, q, 0:nt], Gh[:, f, t0:t0 + nt], Gl[:, f, t0:t0 + nt], [v, *g_free])
                        tmp.give(q, a, v)
                        gt[s][f] = [a, v]
                    gemm_fm(w1, 8, [128 * fc, FF2 + 128 * fc], acts, post)
                residual(w2[1408 * part:1408 * part + 1408, :], 11,
                         [(s, Gh, Gl, 0 if s == "x" else T, T if s == "x" else TC, gt[s]) for s in sets],
                         lambda k, s: CF[:, 3 + i, k, SI[s]:SI[s] + 1], C=C, final=part == 1)
                g_free = [PE.last()]
            fence()
            s4.close()

        h_free2 = [None]
        cf_free = [None]
        for l in range(2):
            if l == 1:
                mod_tok = mod_end()
                cf_free = [V.last(), A.last()]
            cf_tok = [mod_tok]
            for i in range(3):
                cf_tok += mod_norm_cols(l, i)
            if l == 0:
                mod_begin(1, t_sc)
            ffn(l, 0, 0, ["x", "c"], f"a{l}")
            tap(f"X4{l}", X[:, :, :], [xt["x", k] for k in range(8)])
            tap(f"C4{l}", C[:, :, :], [xt["c", k] for k in range(8)])

            s5 = ctx.enter_context(ExitStack())
            CV = sb(f"CV{l}", [128, 2, T + TC], where=s5)
            PV = sb(f"PV{l}", [128, 2, T + TC], where=s5)
            QQ = sb(f"QQ{l}", [128, 4, T + TC], where=s5)
            KK = sb(f"KK{l}", [128, 4, T + TC], where=s5)
            VB = sb(f"VB{l}", [128, 4, 2, 512], where=s5)
            VX = sb(f"VX{l}", [128, 2, 512], where=s5)
            P = sb(f"P{l}", [128, 4, 512], where=s5)
            PT = sb(f"PTt{l}", [128, 1584], where=s5)
            RB = sb(f"RB{l}", [128, 4, 512], where=s5)
            c2 = sb(f"c2{l}", [128, NC2], where=s5)
            PW = sb(f"PW{l}", [128, 2, 128], where=s5)
            t_c2 = load(A, c2[:, :], d["c2"])
            z = G.do(lambda e: e.memset(PW[:, :, :], 0.0))
            t_pw = []
            for g in range(4):
                r = slice(64 * (g % 2), 64 * (g % 2) + 64)
                t_pw.append(load(G, PW[r, g // 2, 64 * (g % 2):64 * (g % 2) + 64], d["pool_w_2"][l, g], z))
            sets = ["x", "c"]
            full = sets if l == 0 else ["x"]
            acts = norm2(l, 1, sets)
            by = {a[0]: a for a in acts}
            fa = [by[s] for s in full]
            w = d["w_in_2"][l]
            OFF = {"x": (0, T), "c": (T, TC)}
            cv = {}
            vn = []
            for half in range(2):
                def post(i, b, t, half=half):
                    v = A.do(lambda e: e.activation(P[:, i, 256 * half:256 * half + 256], ps[:, b, 0:256], ACT.Copy), t)
                    banks.give(b, v)
                    vn.append(v)
                gemm_tm(w, 8, 2048 + 256 * half, 256, by["x"], 4, post)
            vb_toks = []
            vb_sem = [sem(f"vb{l}"), 0]
            for j in range(4):
                for i in range(8):
                    r0 = 64 * (i % 2) + BAND0[j]
                    t = G.dma(lambda e, j=j, i=i, r0=r0: e.dma_start(
                        VB[32 * (i % 4):32 * (i % 4) + 32, j, i // 4, :], P[r0:r0 + 32, i // 2, :]), vb_sem, *vn)
            vb_toks = [t]
            vx = []
            for half in range(2):
                def post(i, b, t, half=half):
                    v = V.do(lambda e: e.tensor_copy(VX[:, i, 256 * half:256 * half + 256], ps[:, b, 0:256]), t)
                    banks.give(b, v)
                    vx.append(v)
                gemm_tm(w, 8, 2048 + 256 * half, 256, by["c"], 2, post)
            kk_toks, qq_toks = {"x": [], "c": []}, {"x": [], "c": []}
            for pair in range(2):
                def post(n, s, b, t, pair=pair):
                    t0, nt = OFF[s]
                    v = V.do(lambda e: e.tensor_copy(KK[:, 2 * pair + n, t0:t0 + nt], ps[:, b, 0:nt]), t)
                    banks.give(b, v)
                    kk_toks[s].append(v)
                gemm_fm(w, 8, [1536 + 256 * pair, 1664 + 256 * pair], [by[s] for s in sets], post)
            for pair in range(2):
                def post(n, s, b, t, pair=pair):
                    t0, nt = OFF[s]
                    dst, src = QQ[:, 2 * pair + n, t0:t0 + nt], ps[:, b, 0:nt]
                    if s == "x":
                        dst = dst.rearrange("p (j r c) -> p r j c", j=4, c=16)
                        src = src.rearrange("p (r j c) -> p r j c", r=8, c=16)
                    v = V.do(lambda e: e.tensor_scalar(dst, src, 0.125, None, ALU.mult), t)
                    banks.give(b, v)
                    qq_toks[s].append(v)
                gemm_fm(w, 8, [1024 + 256 * pair, 1152 + 256 * pair], fa, post)
            for stage, c0 in enumerate((0, 512, 256)):
                def post(n, s, b, t, stage=stage):
                    t0, nt = OFF[s]
                    o = CV[:, n, t0:t0 + nt]
                    src = ps[:, b, 0:nt]
                    if stage == 0:
                        v = V.do(lambda e: e.tensor_copy(o, src), t)
                    elif stage == 1:
                        i, fr = tmp.take()
                        a_ = Tm[:, i, 0:nt]
                        cw = lambda k: p("conv_w_2", 6 * l + 2 * k + n)
                        v = V.do(lambda e: e.tensor_tensor(a_, o, src, ALU.mult), t, cv[n, s], fr)
                        v = V.do(lambda e: e.tensor_scalar(o, a_, cw(1), None, ALU.mult), v)
                        v = V.do(lambda e: e.scalar_tensor_tensor(o[:, 1:nt], a_[:, 0:nt - 1], cw(0), o[:, 1:nt],
                                                                  ALU.mult, ALU.add), v)
                        v = V.do(lambda e: e.scalar_tensor_tensor(o[:, 0:nt - 1], a_[:, 1:nt], cw(2),
                                                                  o[:, 0:nt - 1], ALU.mult, ALU.add), v)
                        tmp.give(i, v)
                    else:
                        v = V.do(lambda e: e.tensor_tensor(o, o, src, ALU.mult), t, cv[n, s])
                    banks.give(b, v)
                    cv[n, s] = v
                gemm_fm(w, 8, [c0, c0 + 128], fa, post)
            pv = {}
            pt_free = [None]

            def pool_post(n, s, b, t):
                t0, nt = OFF[s]
                W_ = nt + 16
                buf = [PT[:, 528 * q:528 * q + W_] for q in range(3)]
                v0 = V.do(lambda e: e.memset(buf[0], 0.0), *pt_free)
                v = V.do(lambda e: e.tensor_copy(buf[0][:, 8:8 + nt], ps[:, b, 0:nt]), t, v0)
                banks.give(b, v)

                def add(dst, src, lo, hi, a, b_, rows, *tk):
                    r = slice(*rows)
                    return V.do(lambda e: e.tensor_tensor(dst[r, lo:hi], src[r, lo - a:hi - a],
                                                          src[r, lo + b_:hi + b_], ALU.add), *tk)
                s2_ = add(buf[1], buf[0], 1, W_, 1, 0, (0, 128), v, *pt_free)
                if n == 0:
                    s4_ = add(buf[2], buf[1], 8, 8 + nt, 1, 1, (64, 128), s2_)
                    src = [(slice(0, 64), buf[1]), (slice(64, 128), buf[2])]
                    last = [s2_, s4_]
                else:
                    s4_ = add(buf[2], buf[1], 2, W_ - 1, 1, 1, (0, 128), s2_)
                    s8_ = add(buf[1], buf[2], 4, W_ - 3, 2, 2, (0, 128), s4_)
                    s16 = add(buf[2], buf[1], 8, 8 + nt, 4, 4, (64, 128), s8_)
                    src = [(slice(0, 64), buf[1]), (slice(64, 128), buf[2])]
                    last = [s8_, s16]
                o = PV[:, n, t0:t0 + nt]
                ws = []
                for r, bf in src:
                    ws.append(V.do(lambda e, r=r, bf=bf: e.scalar_tensor_tensor(
                        o[r, 8:nt - 8], bf[r, 16:nt], c2[r, C2_RW + n:C2_RW + n + 1], buf[0][r, 16:nt],
                        ALU.mult, ALU.subtract), *last, t_c2))
                    for e0, x0 in ((0, 0), (8, nt - 8)):
                        ed = c2[r, C2_EDGE + 16 * n + e0:C2_EDGE + 16 * n + e0 + 8]
                        q = V.do(lambda e, r=r, bf=bf, ed=ed, x0=x0: e.tensor_tensor(
                            o[r, x0:x0 + 8], bf[r, 8 + x0:16 + x0], ed, ALU.mult), *last, t_c2)
                        ws.append(V.do(lambda e, r=r, x0=x0: e.tensor_tensor(
                            o[r, x0:x0 + 8], o[r, x0:x0 + 8], buf[0][r, 8 + x0:16 + x0], ALU.subtract), q))
                pt_free[:] = ws

                def second():
                    b2, fr = banks.take()
                    t2 = mm(ps[:, b2, 0:nt], PW[:, n, :], o, True, True, ws, t_pw, fr, inc=True)
                    v2 = V.do(lambda e: e.tensor_scalar(o, ps[:, b2, 0:nt], p("pool_scale_2", 2 * l + n), None,
                                                        ALU.mult), t2)
                    banks.give(b2, v2)
                    pv[n, s] = v2
                later.append(second)
            gemm_fm(w, 8, [768, 896], fa, pool_post)
            run_later()
            h_free = [PE.last()]
            mix = {s: [[] for _ in range(8)] for s in full}
            for s in full:
                t0, nt = OFF[s]
                for n in range(2):
                    a, v = split_to(CV[:, n, t0:t0 + nt], Hh[:, n, t0:t0 + nt], Hl[:, n, t0:t0 + nt],
                                    [cv[n, s], *h_free])
                    mix[s][n] = [a, v]
                    a, v = split_to(PV[:, n, t0:t0 + nt], Hh[:, 2 + n, t0:t0 + nt], Hl[:, 2 + n, t0:t0 + nt],
                                    [pv[n, s], *h_free])
                    mix[s][2 + n] = [a, v]
            tap(f"CV{l}", CV[:, :, :], [cv[n, s] for n in range(2) for s in full])
            tap(f"PV{l}", PV[:, :, :], [pv[n, s] for n in range(2) for s in full])
            tap(f"QQ{l}", QQ[:, :, :], qq_toks["x"], qq_toks["c"])

            pr, ptr = Ring(4), Ring(3)
            for q in range(4):
                pr.give(q, vb_toks[0])
            for q in range(3):
                ptr.give(q, *pt_free)
            PT3 = PT[:, 0:1584].rearrange("p (a b) -> p a b", a=3)
            rb_done = {}
            rb_tok = {}
            rb_sem = [[sem(f"rb{l}{i}"), 0] for i in range(4)]

            def bias_load(h):
                for r in range(8):
                    src = bass.AP(d["rpb_2"].tensor, ((l * 8 + h) * 16 + 7 - r) * 64, [[1, 16], [1, 512]])
                    t = G.dma(lambda e, r=r, src=src: e.dma_start(RB[16 * r:16 * r + 16, h % 4, :], src),
                              rb_sem[h % 4], rb_done.get(h - 4))
                rb_tok[h] = t

            def n_scores(u, box):
                h, kind, j = u
                if kind == "x" and j == 0 and h % 2 == 0:
                    for hh in ([0, 1, 2, 3] if h == 0 else [h + 2, h + 3] if h < 6 else []):
                        bias_load(hh)
                r = slice(64 * (h % 2), 64 * (h % 2) + 64)
                b, f = banks.take()
                if kind == "x":
                    q_ = QQ[r, h // 2, 128 * j:128 * j + 128]
                    kl = KK[r, h // 2, 0:T].rearrange("p (i c) -> p i c", c=64)[:, :, BAND0[j]:BAND0[j] + 32]
                    mm(ps[:, b, 0:256].rearrange("p (i c) -> p i c", c=32), q_, kl, True, True, qq_toks["x"],
                       kk_toks["x"], f)
                    t = mm(ps[:, b, 256:512], q_, KK[r, h // 2, T:T + TC], True, True, kk_toks["c"], inc=True)
                    sl = ps[:, b, 0:256].rearrange("p (i c) -> p i c", c=32)
                    off = BAND0[j] - 16 * j
                    bi = RB[:, h % 4, :].rearrange("p (i c) -> p i c", c=64)[:, :, 32 - off:-off:-1]
                    v = V.do(lambda e: e.tensor_tensor(sl, sl, bi, ALU.add), t, rb_tok[h])
                    if j == 3:
                        rb_done[h] = v
                    mk = c2[:, C2_MASK + 256 * KIND[j]:C2_MASK + 256 * KIND[j] + 256]
                    t = V.do(lambda e: e.tensor_tensor(ps[:, b, 0:256], ps[:, b, 0:256], mk, ALU.add), v, t_c2)
                    n = 512
                else:
                    t = mm(ps[:, b, 0:TC], QQ[r, h // 2, T + 128 * j:T + 128 * j + 128], KK[r, h // 2, T:T + TC],
                           True, True, qq_toks["c"], kk_toks["c"], f, inc=True)
                    n = TC
                q, fq = pr.take()
                jj, a = softmax(b, n, t, P, q, fq)
                v = V.do(lambda e: e.reciprocal(sm[:, jj, 3:4], sm[:, jj, 1:2]), a)
                box.update(q=q, j=jj, t=a, v=v, n=n)

            def n_turn(u, box):
                box["m"], box["t2"] = turn(P, box["q"], box["n"], box["t"], PT3, pr, ptr)

            def n_out(u, box):
                h, kind, j = u
                m = box["m"]
                b, f = banks.take()
                o = ps[:, b, 0:64]
                nk = box["n"] // 128
                for k in range(nk):
                    if kind == "x":
                        vv = VB[:, j, k, 64 * h:64 * h + 64] if k < 2 else VX[:, k - 2, 64 * h:64 * h + 64]
                    else:
                        vv = VX[:, k, 64 * h:64 * h + 64]
                    t = mm(o, PT3[:, m, 128 * k:128 * k + 128], vv, k == 0, k == nk - 1, box["t2"], vb_toks, vx,
                           f, inc=k == nk - 1)
                ptr.give(m, t)
                hp, hb = h // 2, h % 2
                key = (hp, kind, j)
                if hb == 0:
                    i, fr = tmp.take()
                    ot[key] = [i, []]
                else:
                    i, fr = ot[key][0], []
                v = V.do(lambda e: e.tensor_scalar(Tm[:, i, 64 * hb:64 * hb + 64], o, sm[:, box["j"], 3:4], None,
                                                   ALU.mult), t, box["v"], fr)
                small.give(box["j"], v)
                banks.give(b, v)
                ot[key][1].append(v)

            def n_final(u, box):
                h, kind, j = u
                if h % 2 == 0:
                    return
                key = (h // 2, kind, j)
                i, vs = ot[key]
                b, f = banks.take()
                t = PE.do(lambda e: e.transpose(ps[:, b, 0:128], Tm[:, i, 0:128], ident), vs, f)
                tmp.give(i, t)
                k = 4 + h // 2
                if kind == "x":
                    hi, lo = (H_[:, k, 0:T].rearrange("p (r j c) -> p r j c", r=8, c=16)[:, :, j, :]
                              for H_ in (Hh, Hl))
                    src = ps[:, b, 0:128].rearrange("p (r c) -> p r c", c=16)
                else:
                    hi, lo = (H_[:, k, T + 128 * j:T + 128 * j + 128] for H_ in (Hh, Hl))
                    src = ps[:, b, 0:128]
                a, v = split_to(src, hi, lo, [t, *h_free])
                banks.give(b, a, v)
                mix[kind][k] += [a, v]
            ot = {}
            units = []
            for hp in range(4):
                for kind in full:
                    for j in range(4 if kind == "x" else 2):
                        units += [(2 * hp, kind, j), (2 * hp + 1, kind, j)]
            pipeline(units, [n_scores, n_turn, n_out, n_final], [0, 2, 3, 4])
            residual(d["w_out_2"][l], 8, [(s, Hh, Hl, OFF[s][0], OFF[s][1], mix[s]) for s in full],
                     lambda k, s: CF[:, 4, k, SI[s]:SI[s] + 1], C=C)
            fence()
            s5.close()
            tap(f"X5{l}", X[:, :, :], [xt["x", k] for k in range(8)])
            if l == 0:
                tap(f"C5{l}", C[:, :, :], [xt["c", k] for k in range(8)])
            ffn(l, 1, 2, full, f"b{l}")
            tap(f"X6{l}", X[:, :, :], [xt["x", k] for k in range(8)])

        b, t, _ = rstd_rows(sums["x"], 0, T, 1024)
        for k in range(8):
            v = V.do(lambda e, k=k: e.scalar_tensor_tensor(X[:, k, :], X[:, k, :], p("final_g_2", k), ps[:, b, :],
                                                           ALU.mult, ALU.mult), t)
            st = S.dma(lambda e, k=k: e.dma_start(d["out"][128 * k:128 * k + 128, :], X[:, k, :]), store_sem, v)
        S.wait(st)

        if plan is not None:
            block = ctx.enter_context(nc.Block())
            block.sync(S.play)
            block.tensor(PE.play)
            block.scalar(A.play)
            block.vector(V.play)
            block.gpsimd(G.play)
    return listing


def layouts(a):
    def cols(v):
        return v.reshape(-1, 128).T

    two = lambda v: np.concatenate([v, v], 0)
    pk = {
        "norm_mix_g": cols(a["norm_mix_g"][0]), "mix_out_g": cols(a["mix_out_g"][0].reshape(-1)),
        "norm_mem_g": cols(a["norm_mem_g"][0]), "mem_kv_norm_g": cols(a["mem_kv_norm_g"][0]),
        "norm_ffn_g": cols(a["norm_ffn_g"][0]), "q_norm_g": two(a["q_norm_g"][0])[:, None],
        "k_norm_g": two(a["k_norm_g"][0].T), "cmp_b1": cols(a["cmp_b1"][0].reshape(-1)),
        "cmp_b2": two(a["cmp_b2"][0, 0])[:, None], "mem_q_norm_g": a["mem_q_norm_g"][0][:, None],
        "mem_k_norm_g": a["mem_k_norm_g"][0][:, None], "sg_b": a["sg_b"][0].T,
        "cmp_pos": a["cmp_pos"][0].reshape(2, 16, 128).transpose(2, 0, 1).reshape(128, 32),
        "norm_g_2": cols(a["norm_g_2"].reshape(-1)), "b_mod_2": cols(a["b_mod_2"].reshape(-1)),
        "cc_2": np.stack([cols(a["c_2"][0]), cols(a["c_ctx_2"])], 2).reshape(128, 16),
        "conv_w_2": cols(a["conv_w_2"].reshape(-1)), "pool_scale_2": cols(a["pool_scale_2"].reshape(-1)),
        "final_g_2": cols(a["final_g_2"]),
    }
    c, c1, c2 = constants()
    w_in = a["w_in"][0]
    q = w_in[:, 1024:1536].reshape(1024, 2, 4, 64).transpose(0, 2, 1, 3).reshape(1024, 512)
    rows = np.concatenate([a["sg_ln_g"][0], a["sg_ln_b"][0], a["cmp_b2"][0, 1]])
    return {
        "x": a["x"][0].T, "mem": a["mem"][0].T, "ctx_2": a["ctx_2"][0].T,
        "par": np.concatenate([pk[n] for n, _ in PARAMS], 1), "con": c, "c1": c1, "c2": c2,
        "rows": np.broadcast_to(rows, (128, 1088)),
        "w_in": np.concatenate([w_in[:, :1024], q, w_in[:, 1536:]], 1),
        "sg_w": a["sg_w"][0].transpose(2, 0, 1), "cmp_w1": a["cmp_w1"][0],
        "cmp_w2": np.concatenate([a["cmp_w2"][0]] * 2, 2).reshape(2, 2, 128, 128).transpose(2, 0, 1, 3),
        "w_out": a["w_out"][0], "w_mq": a["w_mq"][0], "w_mkv": a["w_mkv"][0], "w_mo": a["w_mo"][0],
        "w_ff1": a["w_ff1"][0], "w_ff2": a["w_ff2"][0], "w_mod_2": a["w_mod_2"],
        "ffn_w_in_2": a["ffn_w_in_2"], "ffn_w_out_2": a["ffn_w_out_2"], "w_in_2": a["w_in_2"],
        "pool_w_2": a["pool_w_2"], "w_out_2": a["w_out_2"],
        "rpb_2": np.pad(a["rpb_2"], ((0, 0), (0, 0), (0, 1), (16, 17)))[..., ::-1],
    }


def kernel(**inputs):
    import concourse.bacc as _bacc
    from concourse.bass_utils import run_bass_kernel_spmd as _run

    arrays = {k: np.ascontiguousarray(v) for k, v in layouts({k: np.asarray(v) for k, v in inputs.items()}).items()}

    nc = _bacc.Bacc("TRN2", target_bir_lowering=False, num_devices=1)
    scratch = _bacc.Bacc("TRN2", target_bir_lowering=False, num_devices=1)
    build(nc, scratch, {k: v.shape for k, v in arrays.items()})
    r = _run(nc, [{f"in_{k}": v for k, v in arrays.items()}], core_ids=[0])
    return np.ascontiguousarray(r.results[0]["out"].T).reshape(1, T, 1024)


def build(nc, scratch, shapes, taps=None, stop=None):
    d = {k: nc.dram_tensor(f"in_{k}", s, F32, kind="ExternalInput").ap() for k, s in shapes.items()}
    d["out"] = nc.dram_tensor("out", (1024, T), F32, kind="ExternalOutput").ap()
    tp = {k: nc.dram_tensor("tap_" + k, s, F32, kind="ExternalOutput").ap() for k, s in (taps or {}).items()}
    plan = program(scratch, d, None, stop, tp)
    program(nc, d, plan, stop, tp)
```

```python
from contextlib import ExitStack

import numpy as np

import concourse.bass as bass
from concourse import mybir

F32 = mybir.dt.float32
F32R = mybir.dt.float32r
ALU = mybir.AluOpType
ACT = mybir.ActivationFunctionType
AX = mybir.AxisListType

NEG = -1e30
EPS = 1e-6
T = 512
TC = 256
FF2 = 2816
RAW = 3
HL = 3
AHEAD = 2

PARAMS = [("norm_mix_g", 8), ("mix_out_g", 8), ("norm_mem_g", 8), ("mem_kv_norm_g", 8),
          ("norm_ffn_g", 8), ("q_norm_g", 1), ("k_norm_g", 3), ("cmp_b1", 4), ("cmp_b2", 1),
          ("mem_q_norm_g", 1), ("mem_k_norm_g", 1), ("sg_b", 8), ("cmp_pos", 32),
          ("norm_g_2", 48), ("b_mod_2", 144), ("conv_w_2", 12),
          ("pool_scale_2", 4), ("final_g_2", 8)]
PCOL = {}
_at = 0
for _n, _w in PARAMS:
    PCOL[_n] = _at
    _at += _w
NPAR = _at
CIDENT, CONES, CBLOCK, NCONST = 0, 128, 256, 384
C1_CAUSAL, C1_SGU, C1_CMP, NC1 = 0, 128, 256, 256 + 124
C2_EDGE, C2_RW, C2_MASK, NC2 = 0, 32, 34, 34 + 768
BAND0 = [0, 8, 24, 32]
KIND = [0, 1, 1, 2]


def constants():
    c = np.zeros((128, NCONST), np.float32)
    c[:, CIDENT:CIDENT + 128] = np.eye(128)
    c[:, CONES:CONES + 128] = 1
    c[:64, CBLOCK:CBLOCK + 64] = 1
    c[64:, CBLOCK + 64:CBLOCK + 128] = 1
    c1 = np.zeros((128, NC1), np.float32)
    q, k = np.arange(128)[:, None], np.arange(128)[None, :]
    c1[:, C1_CAUSAL:C1_CAUSAL + 128] = np.where(k <= q, 0, NEG)
    c1[:, C1_SGU:C1_SGU + 128] = q <= k
    for i in range(4):
        n = np.arange(31)[None, :]
        c1[:, C1_CMP + 31 * i:C1_CMP + 31 * i + 31] = np.where(16 * n + 31 <= q + 128 * i, 0, NEG)
    c2 = np.zeros((128, NC2), np.float32)
    for kind, j in ((0, 0), (1, 1), (2, 3)):
        col = 16 * j + np.arange(128)[:, None] % 16
        kc = BAND0[j] + np.arange(256)[None, :] % 32
        start = np.clip(col - 8, 0, 48)
        c2[:, C2_MASK + 256 * kind:C2_MASK + 256 * kind + 256] = np.where((kc >= start) & (kc < start + 16), 0, NEG)
    for tile in range(2):
        for half in range(2):
            w = (2, 4, 8, 16)[2 * tile + half]
            rows = slice(64 * half, 64 * half + 64)
            for e in range(8):
                c2[rows, C2_EDGE + 16 * tile + e] = 1 / (min(e + w - w // 2, 10 ** 6) - max(e - w // 2, 0))
                back = 8 - e
                c2[rows, C2_EDGE + 16 * tile + 8 + e] = 1 / (min(w - w // 2, back) + w // 2)
            c2[rows, C2_RW + tile] = 1 / w
    return c, c1, c2


class Recorder:

    def activation(self, *a, **k):
        return lambda e: e.activation(*a, **k)

    def tensor_tensor(self, *a, **k):
        return lambda e: e.tensor_tensor(*a, **k)

    def tensor_scalar(self, *a, **k):
        return lambda e: e.tensor_scalar(*a, **k)

    def scalar_tensor_tensor(self, *a, **k):
        return lambda e: e.scalar_tensor_tensor(*a, **k)

    def tensor_tensor_reduce(self, *a, **k):
        return lambda e: e.tensor_tensor_reduce(*a, **k)

    def tensor_reduce(self, *a, **k):
        return lambda e: e.tensor_reduce(*a, **k)

    def tensor_copy(self, *a, **k):
        return lambda e: e.tensor_copy(*a, **k)

    def reciprocal(self, *a, **k):
        return lambda e: e.reciprocal(*a, **k)

    def memset(self, *a, **k):
        return lambda e: e.memset(*a, **k)

    def bn_stats(self, *a, **k):
        return lambda e: e.bn_stats(*a, **k)

    def bn_aggr(self, *a, **k):
        return lambda e: e.bn_aggr(*a, **k)

    def matmul(self, *a, **k):
        return lambda e: e.matmul(*a, **k)

    def transpose(self, *a, **k):
        return lambda e: e.transpose(*a, **k)

    def dma_start(self, *a, **k):
        return lambda e: e.dma_start(*a, **k)


RECORD = Recorder()


class Lane:

    def __init__(self, name, sem):
        self.name, self.sem, self.n, self.ops, self.seen = name, sem, 0, [], {}

    def wait(self, *toks):
        for t in toks:
            if t is None:
                continue
            if isinstance(t, list):
                self.wait(*t)
                continue
            sem, v = t
            if self.seen.get(id(sem), 0) < v:
                self.seen[id(sem)] = v
                self.ops.append(("w", sem, v))

    def do(self, fn, *toks):
        self.wait(*toks)
        self.n += 1
        self.ops.append(("i", fn(RECORD), self.sem, 1))
        return (self.sem, self.n)

    def go(self, fn, *toks):
        self.wait(*toks)
        self.ops.append(("n", fn(RECORD)))

    def dma(self, fn, count, *toks):
        self.wait(*toks)
        count[1] += 16
        self.ops.append(("i", fn(RECORD), count[0], 16))
        return (count[0], count[1])

    def last(self):
        return (self.sem, self.n) if self.n else None

    def play(self, eng):
        for op in self.ops:
            if op[0] == "w":
                eng.wait_ge(op[1], op[2])
            elif op[0] == "i":
                op[1](eng).then_inc(op[2], op[3])
            else:
                op[1](eng)


class Banks:

    def __init__(self, n):
        self.free = [(i, []) for i in range(n)]

    def take(self):
        return self.free.pop(0)

    def give(self, i, *toks):
        self.free.append((i, list(toks)))


class Ring:

    def __init__(self, n):
        self.n, self.at, self.toks = n, 0, [[] for _ in range(n)]

    def take(self):
        i = self.at % self.n
        self.at += 1
        t, self.toks[i] = self.toks[i], None
        assert t is not None
        return i, t

    def give(self, i, *toks):
        self.toks[i] = list(toks)


class Chunk:

    def __init__(self, i, kt, cols, raw):
        self.i, self.kt, self.cols, self.raw = i, kt, cols, raw


def program(nc, d, plan, stop=None, taps=None):
    listing = []
    ctx = ExitStack()
    with ctx:
        def sb(name, shape, dt=F32, where=None):
            return (where or ctx).enter_context(nc.sbuf_tensor(name, shape, dt))

        def sem(name):
            return ctx.enter_context(nc.semaphore(name))

        PE, A, V, G, S = (Lane(n, sem("done_" + n)) for n in ("pe", "act", "dve", "pool", "sp"))
        LANES = [PE, A, V, G]
        raw_sem = [[sem(f"raw{i}"), 0] for i in range(RAW)]
        load_sems = [[sem(f"load{i}"), 0] for i in range(32)]
        load_at = [0]
        store_sem = [sem("store"), 0]

        ps = ctx.enter_context(nc.psum_tensor("ps", [128, 8, 512], F32))
        X = sb("X", [128, 8, T])
        Hh = sb("Hh", [128, 8, T + TC], F32R)
        Hl = sb("Hl", [128, 8, T + TC], F32R)
        rawb = sb("rawb", [128, RAW, 1024])
        hib = sb("hib", [128, HL, 1024], F32R)
        lob = sb("lob", [128, HL, 1024], F32R)
        Tm = sb("Tm", [128, 4, 512])
        ACC = sb("ACC", [128, T + TC])
        par = sb("par", [128, NPAR])
        con = sb("con", [128, NCONST])
        M = sb("M", [128, 2, 72, 2])
        M2 = sb("M2", [128, 72, 2])
        gm = sb("gm", [128, 8])
        sm = sb("sm", [128, 24, 8])
        identr = sb("identr", [128, 128], F32R)
        ident, ones, blk = con[:, 0:128], con[:, 128:256], con[:, 256:384]

        banks = Banks(8)
        tmp = Ring(4)
        small = Ring(24)
        chunks_done = {}
        hl_done = {}
        ready = {}
        later = []
        state = {"issued": 0, "used": 0, "extra_sem": 0}

        def load(lane, dst, src, *toks):
            s = load_sems[load_at[0]]
            load_at[0] += 1
            return lane.dma(lambda e: e.dma_start(dst, src), s, *toks)

        def p(name, i=0, n=1):
            return par[:, PCOL[name] + i:PCOL[name] + i + n]

        def issue(upto):
            while state["issued"] < min(upto, len(plan)):
                i = state["issued"]
                state["issued"] += 1
                src, kt, cols, raw = plan[i]
                r = rawb[:, i % RAW, 0:kt * cols].rearrange("p (k c) -> p k c", c=cols)
                each = cols // len(src)
                for n, piece in enumerate(src):
                    t = S.dma(lambda e, o=r[:, :, n * each:n * each + each], x=piece: e.dma_start(o, x),
                              raw_sem[i % RAW], chunks_done.get(i - RAW))
                if raw:
                    ready[i] = t
                    continue
                flat = rawb[:, i % RAW, 0:kt * cols]
                hi, lo = hib[:, i % HL, 0:kt * cols], lob[:, i % HL, 0:kt * cols]
                a = A.do(lambda e, hi=hi, flat=flat: e.activation(hi, flat, ACT.Copy), t, hl_done.get(i - HL))
                b = V.do(lambda e, hi=hi, lo=lo, flat=flat: e.tensor_tensor(lo, flat, hi, ALU.subtract),
                         a, hl_done.get(i - HL))
                ready[i] = [a, b]
                chunks_done[i] = [a, b]

        def chunk(src, kt, cols, raw=False):
            listing.append((src, kt, cols, raw))
            c = Chunk(state["used"], kt, cols, raw)
            state["used"] += 1
            if plan is not None:
                issue(c.i + 1 + AHEAD)
            c.ready = ready.get(c.i)
            if raw:
                c.w = rawb[:, c.i % RAW, 0:kt * cols].rearrange("p (k c) -> p k c", c=cols)
            else:
                c.hi = hib[:, c.i % HL, 0:kt * cols].rearrange("p (k c) -> p k c", c=cols)
                c.lo = lob[:, c.i % HL, 0:kt * cols].rearrange("p (k c) -> p k c", c=cols)
            return c

        def used(c, tok):
            hl_done[c.i] = tok
            if c.raw:
                chunks_done[c.i] = tok

        def mm(out, lhsT, rhs, start, stop, *toks, inc=False):
            f = lambda e: e.matmul(out, lhsT, rhs, start=start, stop=stop)
            if inc:
                return PE.do(f, *toks)
            PE.go(f, *toks)

        def run_later():
            todo, later[:] = later[:], []
            for f in todo:
                f()

        def gemm(parts, outs, pick, post):
            got = [banks.take() for _ in outs]
            last_k = parts[-1][1] + parts[-1][2] - 1
            toks = [None] * len(outs)
            for src, k0, kt, cols in parts:
                c = chunk(src, kt, cols)
                for n, o in enumerate(outs):
                    b, free = got[n]
                    for kc in range(kt):
                        k = k0 + kc
                        out, lh, ll, rh, rl, wt = pick(o, c, k, kc)
                        dst = out(b)
                        mm(dst, lh, rh, k == 0, False, c.ready, free if k == 0 else None, wt)
                        mm(dst, lh, rl, False, False)
                        end = kc == kt - 1
                        t = mm(dst, ll, rh, False, k == last_k, inc=end)
                    toks[n] = t
                used(c, t)
                run_later()
                mod_step()
            for n, o in enumerate(outs):
                post(o, got[n][0], toks[n])

        def rows(w, k0, kt, c0, cols):
            return [w.rearrange("(k p) n -> p k n", p=128)[:, k0:k0 + kt, c0:c0 + cols]]

        def k_parts(total):
            return [(k, min(4, total - k)) for k in range(0, total, 4)]

        def gemm_fm(w, kt, cols2, acts, post):
            parts = []
            for k0, n in k_parts(kt):
                if len(cols2) == 1:
                    parts.append((rows(w, k0, n, cols2[0], 128), k0, n, 128))
                elif cols2[1] == cols2[0] + 128:
                    parts.append((rows(w, k0, n, cols2[0], 256), k0, n, 256))
                else:
                    parts.append((rows(w, k0, n, cols2[0], 128) + rows(w, k0, n, cols2[1], 128), k0, n, 256))
            outs = [(n, a) for a in acts for n in range(len(cols2))]

            def pick(o, c, k, kc):
                n, (_, hi, lo, t0, nt, tk, *by_block) = o
                if by_block and k >= 4:
                    turned = lambda x: x[:, k, t0:t0 + nt].rearrange("p (j r c) -> p r j c", j=4, c=16)
                    return (lambda b: ps[:, b, 0:nt].rearrange("p (r j c) -> p r j c", j=4, c=16),
                            c.hi[:, kc, 128 * n:128 * n + 128], c.lo[:, kc, 128 * n:128 * n + 128],
                            turned(hi), turned(lo), tk[k])
                return (lambda b: ps[:, b, 0:nt], c.hi[:, kc, 128 * n:128 * n + 128],
                        c.lo[:, kc, 128 * n:128 * n + 128], hi[:, k, t0:t0 + nt], lo[:, k, t0:t0 + nt],
                        tk[k])
            gemm(parts, outs, pick, lambda o, b, t: post(o[0], o[1][0], b, t))

        def gemm_tm(w, kt, c0, cols, act, tiles, post, sub=(0, None)):
            parts = [(rows(w, k0, n, c0, cols), k0, n, cols) for k0, n in
                     (k_parts(kt) if cols > 128 else [(0, kt)])]
            _, hi, lo, t0, _, tk = act
            pass_cols = cols

            def pick(o, c, k, kc):
                a = t0 + 128 * o
                return (lambda b: ps[:, b, 0:pass_cols], hi[:, k, a:a + 128], lo[:, k, a:a + 128],
                        c.hi[:, kc, :], c.lo[:, kc, :], tk[k])
            gemm(parts, list(range(tiles)), pick, post)

        mods = []
        mod_state = {"loaded": 0, "used": 0, "slots": [], "left": 0, "last": None}
        mod_sem = [[sem(f"mod{i}"), 0] for i in range(4)]

        def mod_begin(layer):
            mod_state.update(layer=layer)
            mods.extend((n, h) for n in range(72) for h in range(2))

        def mod_open(count, slots, scb, junk):
            t = load(G, scb, d["cc_rows"])
            t = A.do(lambda e: e.activation(scb, scb, ACT.Silu), t)
            mod_state.update(slots=slots, scb=scb.rearrange("p (s h k) -> p s h k", s=2, h=2), junk=junk,
                             left=min(2 * count, len(mods)), done=[None] * 4, base=mod_state["used"],
                             loaded=mod_state["used"], silu=t, last=None)
            mod_load()

        def mod_slot(u):
            return (u - mod_state["base"]) % len(mod_state["slots"])

        def mod_load():
            while plan is not None and mod_state["loaded"] < mod_state["used"] + min(len(mod_state["slots"]), mod_state["left"]):
                u = mod_state["loaded"]
                mod_state["loaded"] += 1
                n, h = mods[u - mod_state["used"]]
                m = mod_slot(u)
                o = mod_state["slots"][m]
                x = d["w_mod_t"][mod_state["layer"]][128 * n:128 * n + 128, 512 * h:512 * h + 512]
                mod_state["tok", m] = G.dma(lambda e: e.dma_start(o, x), mod_sem[m], mod_state["done"][m])

        def mod_step():
            for _ in range(2):
                if not mod_state["left"] or plan is None:
                    return
                u, (n, h) = mod_state["used"], mods.pop(0)
                m = mod_slot(u)
                w, scb, l = mod_state["slots"][m], mod_state["scb"], mod_state["layer"]
                for q in range(2):
                    to = (M[:, l, n, q:q + 1], M2[:, n, q:q + 1])[h]
                    o = w if q else mod_state["junk"]
                    t = V.do(lambda e: e.tensor_tensor_reduce(o, w, scb[:, q, h, :], 1.0, 0.0, ALU.mult, ALU.add, to),
                             mod_state["tok", m], mod_state["silu"], mod_state["last"] if not q else None)
                    if not q:
                        mod_state["last"] = t
                mod_state["done"][m] = t
                mod_state["used"] += 1
                mod_state["left"] -= 1
                mod_load()

        def mod_close():
            while plan is not None and mod_state["left"]:
                mod_step()

        def mod_end():
            mod_close()
            if plan is None:
                mods[:] = []
            assert not mods
            l = mod_state["layer"]
            both = M[:, l, :, :]
            bias = p("b_mod_2", 72 * l, 72).unsqueeze(2).to_broadcast([128, 72, 2])
            t = V.do(lambda e: e.tensor_tensor(both, both, M2[:, :, :], ALU.add), V.last())
            return V.do(lambda e: e.tensor_tensor(both, both, bias, ALU.add), t)

        def mcol(l, i, k, s):
            return M[:, l, 8 * i + k, s:s + 1]

        def square_in(src, t0, nt, k, *toks):
            acc = ACC[:, t0:t0 + nt]
            if k == 0:
                return A.do(lambda e: e.activation(acc, src, ACT.Square), *toks)
            i, free = tmp.take()
            a = A.do(lambda e: e.activation(Tm[:, i, 0:nt], src, ACT.Square), free, *toks[:-1])
            v = V.do(lambda e: e.tensor_tensor(acc, acc, Tm[:, i, 0:nt], ALU.add), a, toks[-1])
            tmp.give(i, v)
            return v

        def rstd_sums(sum_tok, t0, nt, width):
            n = nt // 128
            b, free = banks.take()
            for i in range(n):
                t = mm(ps[:, b, i:i + 1], ACC[:, t0 + 128 * i:t0 + 128 * i + 128], ones[:, 0:1], True, True,
                       sum_tok, free, inc=i == n - 1)
            j, fr = small.take()
            a = A.do(lambda e: e.activation(sm[:, j, 0:n], ps[:, b, 0:n], ACT.Sqrt, bias=eps[:, 0:1],
                                            scale=1.0 / width), t, fr)
            v = V.do(lambda e: e.reciprocal(sm[:, j, 4:4 + n], sm[:, j, 0:n]), a)
            i, free2 = tmp.take()
            for q in range(n):
                w = V.do(lambda e, q=q: e.tensor_scalar(Tm[:, i, 128 * q:128 * q + 128], ident,
                                                       sm[:, j, 4 + q:5 + q], None, ALU.mult), v, free2)
            small.give(j, w)
            return b, i, w, a

        def rstd_spread(r, nt):
            b, i, w, a = r
            t = mm(ps[:, b, 0:nt], ones, Tm[:, i, 0:nt], True, True, w, a, inc=True)
            tmp.give(i, t)
            return b, t

        def split_to(src, hi, lo, toks, shift=None, eng=None):
            if shift is None:
                a = A.do(lambda e: e.activation(hi, src, ACT.Copy), *toks)
                v = (eng or V).do(lambda e: e.tensor_tensor(lo, src, hi, ALU.subtract), a, *toks)
            else:
                a = A.do(lambda e: e.activation(hi, src, ACT.Identity, bias=shift), *toks)
                v = V.do(lambda e: e.scalar_tensor_tensor(lo, src, shift, hi, ALU.add, ALU.subtract), a, *toks)
            return a, v

        def norm_steps(spec):
            src, nt, t0, sum_tok, gain, shift, toks = spec
            box, out, done = {}, [None] * 8, []

            def sums_():
                box["r"] = rstd_sums(sum_tok(), t0, nt, 1024)

            def spread():
                box["b"], box["t"] = rstd_spread(box["r"], nt)
                done.append(box["t"])

            def scale(k):
                b, t = box["b"], box["t"]
                i, free = tmp.take()
                v = V.do(lambda e: e.scalar_tensor_tensor(Tm[:, i, 0:nt], src[:, k, 0:nt], gain(k),
                                                          ps[:, b, 0:nt], ALU.mult, ALU.mult), t, free, toks())
                if k == 7:
                    banks.give(b, v)
                box[k] = (i, v)

            def apply(k):
                for x in {0: [0, 1], 7: []}.get(k, [k + 1]):
                    scale(x)
                i, v = box[k]
                hi, lo = Hh[:, k, t0:t0 + nt], Hl[:, k, t0:t0 + nt]
                a, w = split_to(Tm[:, i, 0:nt], hi, lo, [v, toks()], shift(k) if shift else None)
                tmp.give(i, w, a)
                out[k] = [a, w]
                if k == 7:
                    done.append([a, w])
            return [sums_, spread] + [lambda k=k: apply(k) for k in range(8)], out, done

        def norms(specs):
            got = [norm_steps(x) for x in specs]
            for fs in zip(*[g[0] for g in got]):
                for f in fs:
                    f()
            return [(g[1], g[2]) for g in got]

        def in_turn(steps, each=2):
            if not steps:
                return
            n = 1 if len(steps) > 8 else each

            def run():
                for f in steps[:n]:
                    f()
                in_turn(steps[n:], each)
            later.append(run)

        def head_norm(b, tok, width, nt, gain, out, blocked=True, *toks):
            i, free = tmp.take()
            a = A.do(lambda e: e.activation(Tm[:, i, 0:nt], ps[:, b, 0:nt], ACT.Square), tok, free)

            def second():
                b2, fr = banks.take()
                t = mm(ps[:, b2, 0:nt], blk if blocked else ones, Tm[:, i, 0:nt], True, True, a, fr, inc=True)
                r = A.do(lambda e: e.activation(Tm[:, i, 0:nt], ps[:, b2, 0:nt], ACT.Sqrt,
                                                bias=eps[:, 0:1], scale=1.0 / width), t)
                v = V.do(lambda e: e.reciprocal(Tm[:, i, 0:nt], Tm[:, i, 0:nt]), r)
                for q, o in out[0]:
                    w = V.do(lambda e, q=q, o=o: e.scalar_tensor_tensor(
                        o, ps[q, b, 0:nt], gain[q], Tm[q, i, 0:nt], ALU.mult, ALU.mult), v, *toks)
                tmp.give(i, w)
                banks.give(b2, r)
                banks.give(b, w)
                out[1](w)
            later.append(second)

        def tap(name, ap, *toks):
            if taps is not None and name in taps:
                t = A.dma(lambda e: e.dma_start(taps[name], ap), store_sem, *toks)
                for lane in LANES:
                    lane.wait(t)

        def fence():
            ts = [l.last() for l in LANES]
            for l in (A, V, G):
                l.wait(*ts)

        def softmax(b, n, tok, P, i, free, scale=1.0):
            j, fr = small.take()
            v = V.do(lambda e: e.tensor_reduce(sm[:, j, 0:1], ps[:, b, 0:n], AX.X, ALU.max, negate=True),
                     tok, fr)
            bias = sm[:, j, 0:1]
            if scale != 1.0:
                v = V.do(lambda e: e.tensor_scalar(sm[:, j, 2:3], sm[:, j, 0:1], scale, None, ALU.mult), v)
                bias = sm[:, j, 2:3]
            a = A.do(lambda e: e.activation(P[:, i, 0:n], ps[:, b, 0:n], ACT.Exp, bias=bias, scale=scale,
                                            accum_out=sm[:, j, 1:2]), v, free)
            banks.give(b, a)
            return j, a

        flip = [0]

        def turn(P, i, n, tok, PT, pring, ptring, lane=None):
            b, free = banks.take()
            for k in range(n // 128):
                t = (PE.do if k == n // 128 - 1 else PE.go)(
                    lambda e, k=k: e.transpose(ps[:, b, 128 * k:128 * k + 128], P[:, i, 128 * k:128 * k + 128],
                                               ident), tok, free)
            pring.give(i, t)
            m, fr = ptring.take()
            flip[0] += 1
            lane = lane or (V, A)[flip[0] % 2]
            f = ((lambda e: e.tensor_copy(PT[:, m, 0:n], ps[:, b, 0:n])) if lane is V else
                 (lambda e: e.activation(PT[:, m, 0:n], ps[:, b, 0:n], ACT.Copy)))
            v = lane.do(f, t, fr)
            banks.give(b, v)
            return m, v

        def pipeline(units, stages, skew, extra={}):
            box = [{} for _ in units]
            for step in range(len(units) + skew[-1]):
                for s, f in enumerate(stages):
                    u = step - skew[s]
                    if 0 <= u < len(units):
                        f(units[u], box[u])
                for f in extra.get(step, []):
                    f()

        eps = sb("eps", [128, 1])
        t_con = load(A, con[:, :], d["con"])
        t_par = load(A, par[:, :], d["par"])
        x_dram = d["x"].rearrange("(k p) t -> p k t", p=128)
        t_xs = [load((A, G)[k % 2], X[:, k, :], x_dram[:, k, :]) for k in range(8)]
        t_x = t_xs
        t_eps = V.do(lambda e: e.memset(eps[:, :], EPS))
        start = [t_con, t_par, t_eps]
        for l in LANES:
            l.wait(*start)
        t_ir = A.do(lambda e: e.activation(identr[:, :], ident, ACT.Copy))
        mod_begin(0)

        s2 = ctx.enter_context(ExitStack())
        U = sb("U", [128, 4, 512], where=s2)
        VV = sb("VV", [128, 4, 512], where=s2)
        s1 = ctx.enter_context(ExitStack())
        sgw = sb("sgw", [128, 8, 128], where=s1)
        QT = sb("QT", [128, 4, 512], where=s1)
        KS = sb("KS", [128, 2, 512], where=s1)
        KW = sb("KW", [128, 2, 512], where=s1)
        KC2 = sb("KC2", [128, 2, 2, 512], where=s1)
        XIN = sb("XIN", [128, 16, 2, 31], where=s1)
        HC = sb("HC", [128, 2, 2, 62], where=s1)
        KCT = sb("KCT", [128, 2, 31], where=s1)
        VC = sb("VC", [128, 2, 64], where=s1)
        VS = sb("VS", [128, 4, 128], where=s1)
        VW = sb("VW", [128, 4, 128], where=s1)
        OB = sb("OB", [128, 4, 512], where=s1)
        P = sb("P", [128, 4, 512], where=s1)
        PT = sb("PT", [128, 4, 512], where=s1)
        GA = sb("GA", [128, 4, 24], where=s1)
        rowp = sb("rowp", [128, 1088], where=s1)
        c1 = sb("c1", [128, NC1], where=s1)
        W2 = sb("W2", [128, 2, 2, 128], where=s1)
        ms = sb("ms", [128, 32], where=s1)
        kz = [G.do(lambda e, x=x: e.memset(x[:, :, :], 0.0)) for x in (KS, KW, KCT)]
        causal = c1[:, C1_CAUSAL:C1_CAUSAL + 128]

        tk = None
        for k in range(8):
            tk = square_in(X[:, k, :], 0, T, k, t_xs[k], tk)
        S.wait(t_xs[3])
        if plan is not None:
            issue(3)
        (hx, _), = norms([(X, T, 0, lambda: tk, lambda k: p("norm_mix_g", k), None, lambda: t_x)])
        mod_open(16, [P[:, q, :] for q in range(4)], OB[:, :, :].rearrange("p a b -> p (a b)"), PT[:, 0, :])
        t_row = load(G, rowp[:, :], d["rows"])
        t_c1 = load(G, c1[:, :], d["c1"])
        t_sgw = load(G, sgw[:, :, :], d["sg_w"])
        t_w2 = load(G, W2[:, :, :, :], d["cmp_w2"])
        ax = ("x", Hh, Hl, 0, T, hx)
        w_in = d["w_in"]

        u_tok, v_tok = [], []

        def uv_product(dst, c0, box):
            for half in range(2):
                def post(i, b, t, dst=dst, half=half, box=box):
                    a = A.do(lambda e: e.activation(dst[:, i, 256 * half:256 * half + 256], ps[:, b, 0:256],
                                                    ACT.Gelu_apprx_tanh), t)
                    banks.give(b, a)
                    box.append(a)
                gemm_tm(w_in, 8, c0 + 256 * half, 256, ax, 4, post)

        uv_product(VV, 512, v_tok)

        sgm = V.do(lambda e: e.tensor_tensor(sgw[:, :, :], sgw[:, :, :],
                                             c1[:, C1_SGU:C1_SGU + 128].unsqueeze(1).to_broadcast([128, 8, 128]),
                                             ALU.mult), t_sgw, t_c1)
        lane_toks = []
        for i in range(4):
            row = VV[:, i, :]
            j, fr = small.take()
            j2, fr2 = small.take()
            v = V.do(lambda e, j=j, row=row: e.bn_stats(sm[:, j, 0:6], row), v_tok, fr)
            v = V.do(lambda e, j=j, j2=j2: e.bn_aggr(sm[:, j2, 0:2], sm[:, j, 0:6]), v, fr2)
            a = A.do(lambda e, j2=j2: e.activation(sm[:, j2, 2:3], sm[:, j2, 1:2], ACT.Sqrt, bias=eps[:, 0:1],
                                                   scale=1.0), v)
            v = V.do(lambda e, j2=j2: e.reciprocal(sm[:, j2, 3:4], sm[:, j2, 2:3]), a)
            v = V.do(lambda e, j2=j2, row=row: e.tensor_scalar(row, row, sm[:, j2, 0:1], sm[:, j2, 3:4],
                                                               ALU.subtract, ALU.mult), v)
            small.give(j, v)
            small.give(j2, v)
            g = G.do(lambda e, row=row: e.tensor_tensor(row, row, rowp[:, 0:512], ALU.mult), v, t_row)
            g = G.do(lambda e, row=row: e.tensor_tensor(row, row, rowp[:, 512:1024], ALU.add), g)
            lane_toks.append(g)

        c_toks = [[], []]

        def post(n, s, b, t):
            last = []
            for h in range(2):
                src = ps[64 * h:64 * h + 64, b, :]
                a = A.do(lambda e, h=h, src=src: e.activation(KC2[0:64, n, h, :], src, ACT.Copy), t)
                v = V.do(lambda e, h=h, src=src: e.tensor_copy(KC2[64:128, n, h, 0:511], src[:, 1:512]), t, a)
                last += [a, v]
            banks.give(b, *last)
            c_toks[n] += last
        gemm_fm(w_in, 8, [1536, 1664], [ax], post)

        uv_product(U, 0, u_tok)
        a_toks = []
        for g in range(8):
            b, free = banks.take()
            t = mm(ps[:, b, 0:256].rearrange("p (c x) -> p c x", x=64), sgw[:, g, :], VV[:, :, 64 * g:64 * g + 64],
                   True, True, sgm, lane_toks, free, inc=True)
            uu = U[:, :, 64 * g:64 * g + 64]
            v = V.do(lambda e, b=b, g=g, uu=uu: e.scalar_tensor_tensor(
                uu, ps[:, b, 0:256].rearrange("p (c x) -> p c x", x=64), p("sg_b", g), uu, ALU.add, ALU.mult),
                t, u_tok)
            banks.give(b, v)
            a_toks.append(v)

        comp_state = {}
        kct, vct = [], []

        def compress(n):
            XIN_free = comp_state.get("xin")
            x_t = []
            for h in range(2):
                src = KC2[:, n, h, 0:496]
                for part in range(2):
                    s2 = KC2[:, n, h, 16 * part:16 * part + 496].rearrange("p (m j e) -> p j m e", m=31, e=2)[:, :, :, 0]
                    po = p("cmp_pos", 16 * n + 8 * part, 8).unsqueeze(2).to_broadcast([128, 8, 31])
                    v = V.do(lambda e, s2=s2, po=po, h=h, part=part: e.tensor_tensor(
                        XIN[:, 8 * part:8 * part + 8, h, :], s2, po, ALU.add), c_toks[n],
                        XIN_free)
                    x_t.append(v)
            run_later()
            b0, f0 = banks.take()
            b1, f1 = banks.take()
            w1 = d["cmp_w1"][n].rearrange("(j p) n -> p j n", p=128)
            for q in range(4):
                c = chunk([w1[:, 4 * q:4 * q + 4, :]], 4, 256, raw=True)
                for half, b, f in ((0, b0, f0), (1, b1, f1)):
                    for jj in range(4):
                        j = 4 * q + jj
                        t = mm(ps[:, b, 0:62], c.w[:, jj, 128 * half:128 * half + 128],
                               XIN[:, j, :, :].rearrange("p h m -> p (h m)"), j == 0, j == 15,
                               c.ready, x_t, f, inc=jj == 3)
                    if half == 0:
                        t0_ = t
                used(c, t)
            comp_state["xin"] = [t0_, t]
            hh = []
            for half, b, tt in ((0, b0, t0_), (1, b1, t)):
                a = A.do(lambda e, half=half, b=b, n=n: e.activation(
                    HC[:, n, half, :], ps[:, b, 0:62], ACT.Gelu_apprx_tanh, bias=p("cmp_b1", 2 * n + half),
                    scale=1.0), tt)
                banks.give(b, a)
                hh.append(a)
            if n == 0:
                b, f = banks.take()
                for half in range(2):
                    t = mm(ps[:, b, 0:62], W2[:, 0, half, :], HC[:, 0, half, :], half == 0, half == 1, hh, t_w2,
                           f, inc=half == 1)
                j, fr = tmp.take()
                kc = Tm[:, j, 0:62]
                sq = Tm[:, j, 64:126]
                a = A.do(lambda e: e.activation(kc, ps[:, b, 0:62], ACT.Identity, bias=p("cmp_b2")), t, fr)
                a2 = A.do(lambda e: e.activation(sq, kc, ACT.Square), a)
                banks.give(b, a)
                b, f = banks.take()
                t = mm(ps[:, b, 0:62], blk, sq, True, True, a2, f, inc=True)
                a = A.do(lambda e: e.activation(Tm[:, j, 128:190], ps[:, b, 0:62], ACT.Sqrt, bias=eps[:, 0:1],
                                                scale=1.0 / 64), t)
                v = V.do(lambda e: e.reciprocal(Tm[:, j, 192:254], Tm[:, j, 128:190]), a)
                banks.give(b, a)
                for h in range(2):
                    r = slice(64 * h, 64 * h + 64)
                    kct.append(V.do(lambda e, r=r, h=h: e.scalar_tensor_tensor(
                        KCT[r, h, :], Tm[r, j, 31 * h:31 * h + 31], p("k_norm_g", 0)[r],
                        Tm[r, j, 192 + 31 * h:192 + 31 * h + 31], ALU.mult, ALU.mult), v, kz))
                tmp.give(j, *kct)
            else:
                for h in range(2):
                    b, f = banks.take()
                    for half in range(2):
                        t = mm(ps[0:31, b, 0:64], HC[:, 1, half, 31 * h:31 * h + 31], W2[:, 1, half, 0:64],
                               half == 0, half == 1, hh, t_w2, f, inc=half == 1)
                    v = V.do(lambda e, b=b, h=h: e.tensor_tensor(VC[0:31, h, :], ps[0:31, b, 0:64],
                                                                 rowp[0:31, 1024:1088], ALU.add), t)
                    banks.give(b, v)
                    vct.append(v)
        compress(0)
        gq = V.do(lambda e: e.tensor_scalar(gm[:, 0:1], p("q_norm_g"), 0.125, None, ALU.mult))
        q_toks, k_toks = [], {}
        for pair in range(2):
            def post(n, s, b, t, pair=pair):
                head_norm(b, t, 64, T, gm[:, 0:1], ([(slice(0, 128), QT[:, 2 * pair + n, :])], q_toks.append), True, gq)
            gemm_fm(w_in, 8, [1024 + 256 * pair, 1152 + 256 * pair], [ax], post)

        compress(1)
        kv_v = []
        for n, (kdst, vdst, gi) in enumerate(((KS, VS, 1), (KW, VW, 2))):
            c0 = 1792 + 256 * n
            got = [banks.take() for _ in range(5)]
            for k0, kt in k_parts(8):
                c = chunk(rows(w_in, k0, kt, c0, 256), kt, 256)
                for kc in range(kt):
                    k = k0 + kc
                    b, free = got[4]
                    mm(ps[:, b, :], c.hi[:, kc, 0:128], Hh[:, k, 0:T], k == 0, False, c.ready, free, hx[k])
                    mm(ps[:, b, :], c.hi[:, kc, 0:128], Hl[:, k, 0:T], False, False)
                    t = mm(ps[:, b, :], c.lo[:, kc, 0:128], Hh[:, k, 0:T], False, k == 7, inc=True)
                kt_tok = t
                vts = []
                for i in range(4):
                    b, free = got[i]
                    for kc in range(kt):
                        k = k0 + kc
                        h_, l_ = Hh[:, k, 128 * i:128 * i + 128], Hl[:, k, 128 * i:128 * i + 128]
                        mm(ps[:, b, 0:128], h_, c.hi[:, kc, 128:256], k == 0, False, free)
                        mm(ps[:, b, 0:128], h_, c.lo[:, kc, 128:256], False, False)
                        t = mm(ps[:, b, 0:128], l_, c.hi[:, kc, 128:256], False, k == 7, inc=True)
                    vts.append(t)
                used(c, t)
                run_later()
                mod_step()
            for i in range(4):
                b = got[i][0]
                v = V.do(lambda e, b=b, i=i, vdst=vdst: e.tensor_copy(vdst[:, i, :], ps[:, b, 0:128]), vts[i])
                banks.give(b, v)
                kv_v.append(v)
            head_norm(got[4][0], kt_tok, 64, T, p("k_norm_g", gi),
                      ([(slice(64 * h, 64 * h + 64), kdst[64 * h:64 * h + 64, h, :]) for h in range(2)],
                       lambda w, n=n: k_toks.update({n: w})), True, kz)

        g_toks = []

        def post(i, b, t):
            a = A.do(lambda e: e.activation(GA[:, i, :], ps[:, b, 0:24], ACT.Sigmoid), t)
            banks.give(b, a)
            g_toks.append(a)
        gemm_tm(w_in, 8, 2304, 24, ax, 4, post)
        run_later()
        run_later()
        tap("QT", QT[:, :, :], q_toks)
        tap("KS", KS[:, :, :], k_toks[0])
        tap("VS", VS[:, :, :], kv_v)
        tap("GA", GA[:, :, :], g_toks)
        tap("VV", VV[:, :, :], lane_toks)

        def to_mixed(src, i, k0, gcol, toks, j):
            q, free = tmp.take()
            a = A.do(lambda e: e.activation(Tm[:, q, :], src[:, i, :], ACT.Square, accum_out=ms[:, j:j + 1]),
                     free, toks)
            a = A.do(lambda e: e.activation(ms[:, 8 + j:9 + j], ms[:, j:j + 1], ACT.Sqrt, bias=eps[:, 0:1],
                                            scale=1.0 / 512), a)
            v = V.do(lambda e: e.reciprocal(ms[:, 16 + j:17 + j], ms[:, 8 + j:9 + j]), a)
            v = V.do(lambda e: e.tensor_scalar(Tm[:, q, :], src[:, i, :], ms[:, 16 + j:17 + j], None, ALU.mult), v)
            b, fr = banks.take()
            for k in range(4):
                t = (PE.do if k == 3 else PE.go)(
                    lambda e, k=k: e.transpose(ps[:, b, 128 * k:128 * k + 128], Tm[:, q, 128 * k:128 * k + 128],
                                               ident), v, fr)
            out = []
            for k in range(4):
                hi = Hh[:, k0 + k, 128 * i:128 * i + 128]
                pk = ps[:, b, 128 * k:128 * k + 128]
                a = A.do(lambda e, hi=hi, pk=pk, k=k: e.activation(hi, pk, ACT.Copy, scale=gcol(k)), t,
                         h_free)
            for k in range(4):
                hi = Hh[:, k0 + k, 128 * i:128 * i + 128]
                lo = Hl[:, k0 + k, 128 * i:128 * i + 128]
                pk = ps[:, b, 128 * k:128 * k + 128]
                v = V.do(lambda e, hi=hi, lo=lo, pk=pk, k=k: e.scalar_tensor_tensor(
                    lo, pk, gcol(k), hi, ALU.mult, ALU.subtract), a)
                out += [a, v]
            tmp.give(q, t)
            banks.give(b, *out)
            return out

        mix = [[] for _ in range(8)]

        def mix_tile(src, i, k0, toks):
            o = to_mixed(src, i, k0, lambda k: p("mix_out_g", k0 + k), toks, k0 + i)
            for k in range(4):
                mix[k0 + k] += o
        h_free = [PE.last()]
        mod_close()

        pr, ptr = Ring(4), Ring(4)
        for q in range(4):
            pr.give(q, V.last())
            ptr.give(q, V.last())
        ob = {}

        def gate(i, h, br):
            return GA[:, i, 3 * h + br:3 * h + br + 1]

        def c_scores(i, box):
            b, f = banks.take()
            for h in range(8):
                t = mm(ps[:, b, 32 * h:32 * h + 31], QT[:, h % 4, 128 * i:128 * i + 128], KCT[:, h // 4, :], True, True,
                       q_toks, kct, f, inc=h == 7)
            s3 = ps[:, b, 0:256].rearrange("p (h n) -> p h n", n=32)[:, :, 0:31]
            mk = c1[:, C1_CMP + 31 * i:C1_CMP + 31 * i + 31].unsqueeze(1).to_broadcast([128, 8, 31])
            v = V.do(lambda e: e.tensor_tensor(s3, s3, mk, ALU.add), t)
            j, fr = small.take()
            j2, fr2 = small.take()
            v = V.do(lambda e: e.tensor_reduce(sm[:, j, :], s3, AX.X, ALU.max), v, fr)
            v = V.do(lambda e: e.tensor_scalar(sm[:, j, :], sm[:, j, :], -1e29, None, ALU.max), v)
            q, fq = pr.take()
            P3 = P[:, q, 0:256].rearrange("p (h n) -> p h n", n=32)
            vz = V.do(lambda e: e.memset(P[:, q, 0:256], 0.0), fq)
            v = V.do(lambda e: e.tensor_tensor(P3[:, :, 0:31], s3, sm[:, j, :].unsqueeze(2).to_broadcast([128, 8, 31]),
                                               ALU.subtract), v, vz)
            banks.give(b, v)
            a = A.do(lambda e: e.activation(P3[:, :, 0:31], P3[:, :, 0:31], ACT.Exp), v)
            v = V.do(lambda e: e.tensor_reduce(sm[:, j2, :], P3[:, :, 0:31], AX.X, ALU.add), a, fr2)
            v = V.do(lambda e: e.tensor_scalar(sm[:, j2, :], sm[:, j2, :], 1e-6, None, ALU.max), v)
            v = V.do(lambda e: e.reciprocal(sm[:, j, :], sm[:, j2, :]), v)
            g8 = GA[:, i, :].rearrange("p (h b) -> p h b", b=3)[:, :, 0]
            v = V.do(lambda e: e.tensor_tensor(sm[:, j2, :], sm[:, j, :], g8, ALU.mult), v, g_toks)
            small.give(j, v)
            box.update(q=q, j=j2, t=[a, v])

        def c_turn(i, box):
            q = box["q"]
            b, f = banks.take()
            b2, f2 = banks.take()
            for h in range(8):
                t = (PE.do if h == 7 else PE.go)(
                    lambda e, h=h: e.transpose(ps[0:32, (b, b2)[h // 4], 128 * (h % 4):128 * (h % 4) + 128],
                                               P[:, q, 32 * h:32 * h + 32], ident), box["t"], f, f2)
            pr.give(q, t)
            m, fm_ = ptr.take()
            m2, fm2 = ptr.take()
            v = V.do(lambda e: e.tensor_copy(PT[0:32, m, :], ps[0:32, b, :]), t, fm_)
            a = A.do(lambda e: e.activation(PT[0:32, m2, :], ps[0:32, b2, :], ACT.Copy), t, fm2)
            banks.give(b, v)
            banks.give(b2, a)
            box.update(m=(m, m2), t2=[v, a])

        def c_out(i, box):
            b, f = banks.take()
            for h in range(8):
                t = mm(ps[:, b, 64 * h:64 * h + 64], PT[0:31, box["m"][h // 4], 128 * (h % 4):128 * (h % 4) + 128],
                       VC[0:31, h // 4, :], True, True, box["t2"], vct, f, inc=h == 7)
            ptr.give(box["m"][0], t)
            ptr.give(box["m"][1], t)
            o3 = ps[:, b, :].rearrange("p (h x) -> p h x", x=64)
            v = V.do(lambda e: e.tensor_tensor(OB[:, i, :].rearrange("p (h x) -> p h x", x=64), o3,
                                               sm[:, box["j"], :].unsqueeze(2).to_broadcast([128, 8, 64]), ALU.mult), t)
            small.give(box["j"], v)
            banks.give(b, v)
            for h in range(8):
                ob[i, h] = v

        def f_scores(u, box):
            i, h, br = u
            n = 128 * (i + 1)
            kk = (KS, KW)[br - 1]
            b, f = banks.take()
            mm(ps[:, b, 0:n], QT[:, h % 4, 128 * i:128 * i + 128], kk[:, h // 4, 0:n], True, False, q_toks,
               k_toks[br - 1], f)
            t = mm(ps[:, b, n - 128:n], ident, causal, False, True, inc=True)
            q, fq = pr.take()
            j, a = softmax(b, n, t, P, q, fq)
            box.update(q=q, j=j, t=a)

        def f_turn(u, box):
            box["m"], box["t2"] = turn(P, box["q"], 128 * (u[0] + 1), box["t"], PT, pr, ptr)

        def f_out(u, box):
            i, h, br = u
            vv = (VS, VW)[br - 1]
            b, f = banks.take()
            m = box["m"]
            for k in range(i + 1):
                t = mm(ps[:, b, 0:64], PT[:, m, 128 * k:128 * k + 128], vv[:, k, 64 * (h // 4):64 * (h // 4) + 64],
                       k == 0, k == i, box["t2"], kv_v, f, inc=k == i)
            ptr.give(m, t)
            j = box["j"]
            v = V.do(lambda e: e.reciprocal(sm[:, j, 3:4], sm[:, j, 1:2]), box["t"])
            v2 = V.do(lambda e: e.tensor_tensor(sm[:, j, 4:5], sm[:, j, 3:4], gate(i, h, br), ALU.mult), v, g_toks)
            o = OB[:, i, 64 * h:64 * h + 64]
            v = V.do(lambda e: e.scalar_tensor_tensor(o, ps[:, b, 0:64], sm[:, box["j"], 4:5], o, ALU.mult,
                                                      ALU.add), t, v2, ob[i, h])
            small.give(box["j"], v)
            banks.give(b, v)
            ob[i, h] = v
        MT = U[:, :, :].rearrange("p a (b t) -> p (a b) t", b=2)
        MK = VV[:, 0:2, :].rearrange("p a (b t) -> p (a b) t", b=2)
        MV = VV[:, 2:4, :]
        mk_toks, mv_toks = [], []
        w_mkv = d["w_mkv"]
        mem = {}

        def mem_load():
            mem["t"] = load(G, MT, d["mem"].rearrange("(k p) t -> p k t", p=128), mix[0], mix[3])
            tk = None
            for k in range(8):
                tk = square_in(MT[:, k, :], T, TC, k, mem["t"], tk)
            mem["sum"] = tk

        def mem_norm():
            (hm, _), = norms([(MT, TC, T, lambda: mem["sum"], lambda k: p("mem_kv_norm_g", k), None, lambda: mem["t"])])
            mem["act"] = ("c", Hh, Hl, T, TC, hm)

        def mem_k(pair):
            def post(n, s, b, t):
                head_norm(b, t, 128, TC, p("mem_k_norm_g"), ([(slice(0, 128), MK[:, 2 * pair + n, :])], mk_toks.append),
                          False, a_toks)
            gemm_fm(w_mkv, 8, [256 * pair, 256 * pair + 128], [mem["act"]], post)

        def mem_v(half):
            def post(i, b, t):
                v = V.do(lambda e: e.tensor_copy(MV[:, i, 256 * half:256 * half + 256], ps[:, b, 0:256]), t)
                banks.give(b, v)
                mv_toks.append(v)
            gemm_tm(w_mkv, 8, 512 + 256 * half, 256, mem["act"], 2, post)

        extra = {}
        for n in range(4):
            extra.setdefault(1 + 2 * n, []).append(lambda n=n: mix_tile(U, n, 0, a_toks))
            if n < 3:
                extra.setdefault(17 * n + 21, []).append(
                    lambda n=n: mix_tile(OB, n, 4, [ob[n, h] for h in range(8)]))
        extra.setdefault(9, []).append(mem_load)
        extra.setdefault(14, []).append(mem_norm)
        for n in range(2):
            extra.setdefault(24 + 8 * n, []).append(lambda n=n: mem_k(n))
            extra.setdefault(40 + 8 * n, []).append(lambda n=n: mem_v(n))
        units = []
        for i in range(4):
            units += [(i, None, 0)] + [(i, h, br) for h in range(8) for br in (1, 2)]
        stages = [lambda u, box, c=c, f=f: c(u[0], box) if u[2] == 0 else f(u, box)
                  for c, f in ((c_scores, f_scores), (c_turn, f_turn), (c_out, f_out))]
        pipeline(units, stages, [0, 2, 3], extra)
        run_later()
        mix_tile(OB, 3, 4, [ob[3, h] for h in range(8)])

        xt = {("x", k): t_xs[k] for k in range(8)}
        sums = {}

        def residual(w, kt, acts, coef, C=None, final=True, next_norm=None):
            def post(n, s, b, t, n0=None):
                k = n0 + n
                dst, nt, t0 = (X, T, 0) if s == "x" else (C, TC, T)
                o = dst[:, k, :]
                cf = coef(k, s)
                if cf is None:
                    v = V.do(lambda e: e.tensor_tensor(o, ps[:, b, 0:nt], o, ALU.add), t, xt[s, k])
                else:
                    v = V.do(lambda e: e.scalar_tensor_tensor(o, ps[:, b, 0:nt], cf, o, ALU.mult, ALU.add),
                             t, xt[s, k])
                xt[s, k] = v
                banks.give(b, v)
                if final:
                    sums[s] = square_in(o, t0, nt, k, v, sums.get((s, "free"), []) if k == 0 else sums[s])
            for some in [[a] for a in acts] if next_norm else [acts]:
                for pair in range(4):
                    gemm_fm(w, kt, [256 * pair, 256 * pair + 128], some,
                            lambda n, s, b, t, pair=pair: post(n, s, b, t, 2 * pair))
                if next_norm and some[0][0] == "x":
                    steps, toks, done = norm_steps(next_norm)
                    in_turn(steps)
                    pending["x"] = (toks, done)
            if next_norm:
                while later:
                    run_later()

        am = ("x", Hh, Hl, 0, T, mix)
        residual(d["w_out"], 8, [am], lambda k, s: None)
        tap("X1", X[:, :, :], [xt["x", k] for k in range(8)])
        if stop == 1:
            pass
        fence()
        s1.close()

        MQ = sb("MQ", [128, 4, T], where=s2)
        P = sb("P2", [128, 4, 512], where=s2)
        PT = sb("PT2", [128, 16, 256], where=s2)
        mq_toks = []
        (h1, h1done), = norms([(X, T, 0, lambda: sums["x"], lambda k: p("norm_mem_g", k), None, lambda: [])])
        sums["x", "free"] = h1done
        ax = ("x", Hh, Hl, 0, T, h1)
        for pair in range(2):
            def post(n, s, b, t, pair=pair):
                head_norm(b, t, 128, T, p("mem_q_norm_g"), ([(slice(0, 128), MQ[:, 2 * pair + n, :])], mq_toks.append), False)
            gemm_fm(d["w_mq"], 8, [256 * pair, 256 * pair + 128], [ax], post)
        run_later()
        run_later()
        h_free = [PE.last()]
        pr = Ring(4)
        ms_scale = 128.0 ** -0.5
        ptoks = {}

        def m_scores(u, box):
            h, i = u
            b, f = banks.take()
            t = mm(ps[:, b, 0:TC], MQ[:, h, 128 * i:128 * i + 128], MK[:, h, :], True, True, mq_toks, mk_toks,
                   f, inc=True)
            q, fq = pr.take()
            j, a = softmax(b, TC, t, P, q, fq, scale=ms_scale)
            box.update(q=q, t=a, j=j)

        def m_turn(u, box):
            h, i = u
            q, j = box["q"], box["j"]
            v = V.do(lambda e: e.reciprocal(sm[:, j, 3:4], sm[:, j, 1:2]), box["t"])
            v = V.do(lambda e: e.tensor_scalar(P[:, q, 0:TC], P[:, q, 0:TC], sm[:, j, 3:4], None, ALU.mult), v)
            small.give(j, v)
            box["t"] = v
            b, f = banks.take()
            for k in range(2):
                t = (PE.do if k == 1 else PE.go)(
                    lambda e, k=k: e.transpose(ps[:, b, 128 * k:128 * k + 128],
                                               P[:, box["q"], 128 * k:128 * k + 128], ident), box["t"], f)
            pr.give(box["q"], t)
            dst = PT[:, 4 * h:4 * h + 4, :].rearrange("p a b -> p (a b)").rearrange("p (k t) -> p k t", k=2)[
                :, :, 128 * i:128 * i + 128]
            src = ps[:, b, 0:256].rearrange("p (k t) -> p k t", k=2)
            v = V.do(lambda e: e.tensor_copy(dst, src), t)
            banks.give(b, v)
            ptoks.setdefault(h, []).append(v)

        ho = [[] for _ in range(4)]

        def m_out(u, box):
            h, i = u
            if i != 3:
                return
            b, f = banks.take()
            pt = PT[:, 4 * h:4 * h + 4, :].rearrange("p a b -> p (a b)").rearrange("p (k t) -> p k t", k=2)
            for k in range(2):
                t = mm(ps[:, b, :], MV[:, k, 128 * h:128 * h + 128], pt[:, k, :], k == 0, k == 1, ptoks[h],
                       mv_toks, f, inc=k == 1)
            a, v = split_to(ps[:, b, :], Hh[:, h, 0:T], Hl[:, h, 0:T], [t, *h_free])
            banks.give(b, a, v)
            ho[h] = [a, v]
        pipeline([(h, i) for h in range(4) for i in range(4)], [m_scores, m_turn, m_out], [0, 2, 3])
        residual(d["w_mo"], 4, [("x", Hh, Hl, 0, T, ho)], lambda k, s: None)
        tap("X2", X[:, :, :], [xt["x", k] for k in range(8)])
        fence()
        s2.close()

        s3 = ctx.enter_context(ExitStack())
        C = None
        Gh = sb("Gh", [128, 11, T + TC], F32R, where=s3)
        Gl = sb("Gl", [128, 11, T + TC], F32R, where=s3)
        MR = sb("MR", [128, 9, 512], where=s3)
        mod_open(72, [MR[:, q, :] for q in range(4)], MR[:, 4:8, :].rearrange("p a b -> p (a b)"), MR[:, 8, :])
        (h1, h1done), = norms([(X, T, 0, lambda: sums["x"], lambda k: p("norm_ffn_g", k), None, lambda: [])])
        sums["x", "free"] = h1done
        ax = ("x", Hh, Hl, 0, T, h1)
        g_free = [None]
        for part in range(4):
            gt = [[] for _ in range(8)]
            for pair in range(4):
                def post(n, s, b, t, pair=pair):
                    k = 2 * pair + n
                    i, fr = tmp.take()
                    a = A.do(lambda e: e.activation(Tm[:, i, :], ps[:, b, :], ACT.Relu), t, fr)
                    banks.give(b, a)
                    v = V.do(lambda e: e.tensor_tensor(Tm[:, i, :], Tm[:, i, :], Tm[:, i, :], ALU.mult), a)
                    a, v = split_to(Tm[:, i, :], Gh[:, k, 0:T], Gl[:, k, 0:T], [v, *g_free])
                    tmp.give(i, a, v)
                    gt[k] = [a, v]
                gemm_fm(d["w_ff1"], 8, [1024 * part + 256 * pair, 1024 * part + 256 * pair + 128], [ax], post)
            residual(d["w_ff2"][1024 * part:1024 * part + 1024, :], 8, [("x", Gh, Gl, 0, T, gt)],
                     lambda k, s: None, final=part == 3)
            g_free = [PE.last()]
        tap("X3", X[:, :, :], [xt["x", k] for k in range(8)])
        mod_tok = mod_end()
        fence()
        s3.close()

        sC = ctx.enter_context(ExitStack())
        C = sb("C", [128, 8, TC], where=sC)
        t_c = load(G, C[:, :, :], d["ctx_2"].rearrange("(k p) t -> p k t", p=128))
        for k in range(8):
            xt["c", k] = t_c
        tk = t_c
        for k in range(8):
            tk = square_in(C[:, k, :], T, TC, k, t_c, tk)
        sums["c"] = tk

        CF = [sb(f"CF{l}", [128, 6, 8, 2]) for l in range(2)]

        def mod_norm_cols(l, i):
            out = []
            for s in range(2):
                g = p("norm_g_2", 24 * l + 8 * i, 8)
                mm_ = M[:, l, 8 * (3 * i + 1):8 * (3 * i + 2), s]
                mg = M[:, l, 8 * (3 * i + 2):8 * (3 * i + 3), s]
                half = 1.0 if i == 1 else 0.5
                out.append(V.do(lambda e, s=s, g=g, mm_=mm_: e.scalar_tensor_tensor(
                    CF[l][:, i, :, s], mm_, 1.0, g, ALU.add, ALU.mult), mod_tok))
                out.append(V.do(lambda e, s=s, mg=mg: e.tensor_scalar(CF[l][:, 3 + i, :, s], mg, half, None, ALU.mult),
                                mod_tok))
            return out

        SI = {"x": 0, "c": 1}

        pending = {}

        def norm2_spec(l, i, s):
            src, nt, t0 = (X, T, 0) if s == "x" else (C, TC, T)
            return (src, nt, t0, lambda: sums[s], lambda k: CF[l][:, i, k, SI[s]:SI[s] + 1],
                    lambda k: mcol(l, 3 * i, k, SI[s]), lambda: [cf_tok[l], [xt[s, k] for k in range(8)]])

        def norm2(l, i, sets):
            todo = [s for s in sets if s not in pending]
            got = dict(zip(todo, norms([norm2_spec(l, i, s) for s in todo])))
            got.update(pending)
            pending.clear()
            acts = []
            for s in sets:
                toks, done = got[s]
                sums[s, "free"] = done
                nt, t0 = (T, 0) if s == "x" else (TC, T)
                acts.append((s, Hh, Hl, t0, nt, toks))
            return acts

        def following(l, i):
            return norm2_spec(*((l, i + 1) if i < 2 else (l + 1, 0)), "x")

        def ffn(l, j, i, sets, tokname):
            s4 = ctx.enter_context(ExitStack())
            Gh = sb(f"Gh{tokname}", [128, 11, T + TC], F32R, where=s4)
            Gl = sb(f"Gl{tokname}", [128, 11, T + TC], F32R, where=s4)
            if mods:
                MR = sb(f"MR{tokname}", [128, 8, 512], where=s4)
                mod_open(72, [MR[:, q, :] for q in range(3)], MR[:, 3:7, :].rearrange("p a b -> p (a b)"),
                         MR[:, 7, :])
            acts = norm2(l, i, sets)
            g_free = [None]
            w1, w2 = d["ffn_w_in_2"][l, j], d["ffn_w_out_2"][l, j]
            for part in range(2):
                gt = {s: [None] * 11 for s in sets}
                for f in range(11):
                    fc = 11 * part + f
                    box = {}

                    def post(n, s, b, t, f=f, box=box, gt=gt):
                        if n == 0:
                            box[s] = (b, t)
                            return
                        ba, ta = box[s]
                        nt, t0 = (T, 0) if s == "x" else (TC, T)
                        q, fr = tmp.take()
                        a = A.do(lambda e: e.activation(Tm[:, q, 0:nt], ps[:, ba, 0:nt], ACT.Silu), ta, fr)
                        banks.give(ba, a)
                        v = V.do(lambda e: e.tensor_tensor(Tm[:, q, 0:nt], Tm[:, q, 0:nt], ps[:, b, 0:nt], ALU.mult),
                                 a, t)
                        banks.give(b, v)
                        a, v = split_to(Tm[:, q, 0:nt], Gh[:, f, t0:t0 + nt], Gl[:, f, t0:t0 + nt], [v, *g_free])
                        tmp.give(q, a, v)
                        gt[s][f] = [a, v]
                    gemm_fm(w1, 8, [128 * fc, FF2 + 128 * fc], acts, post)
                    if fc % 3 == 2:
                        mod_step()
                residual(w2[1408 * part:1408 * part + 1408, :], 11,
                         [(s, Gh, Gl, 0 if s == "x" else T, T if s == "x" else TC, gt[s]) for s in sets],
                         lambda k, s: CF[l][:, 3 + i, k, SI[s]:SI[s] + 1], C=C, final=part == 1,
                         next_norm=following(l, i) if part == 1 and len(sets) == 2 else None)
                g_free = [PE.last()]
            mod_close()
            fence()
            s4.close()

        cf_tok = {}
        for i in range(3):
            cf_tok.setdefault(0, []).extend(mod_norm_cols(0, i))
        mod_begin(1)
        for l in range(2):
            ffn(l, 0, 0, ["x", "c"], f"a{l}")
            if l == 0:
                mod_tok = mod_end()
                for i in range(3):
                    cf_tok.setdefault(1, []).extend(mod_norm_cols(1, i))
            tap(f"X4{l}", X[:, :, :], [xt["x", k] for k in range(8)])
            tap(f"C4{l}", C[:, :, :], [xt["c", k] for k in range(8)])

            s5 = ctx.enter_context(ExitStack())
            CV = sb(f"CV{l}", [128, 2, T + TC], where=s5)
            PV = sb(f"PV{l}", [128, 2, T + TC], where=s5)
            KH = sb(f"KH{l}", [128, 4, T + TC], F32R, where=s5)
            KL = sb(f"KL{l}", [128, 4, T + TC], F32R, where=s5)
            VB = sb(f"VB{l}", [128, 4, 2, 512], where=s5)
            VX = sb(f"VX{l}", [128, 2, 512], where=s5)
            P = sb(f"P{l}", [128, 4, 512], where=s5)
            PT = sb(f"PTt{l}", [128, 1584], where=s5)
            RB = sb(f"RB{l}", [128, 4, 512], where=s5)
            c2 = sb(f"c2{l}", [128, C2_MASK], where=s5)
            maskr = sb(f"maskr{l}", [128, 768], F32R, where=s5)
            PW = sb(f"PW{l}", [128, 2, 128], where=s5)
            t_c2 = load(A, c2[:, :], d["c2"][:, 0:C2_MASK])
            raw_mask = RB[:, 0:2, :].rearrange("p a b -> p (a b)")[:, 0:768]
            t_mask = load(A, raw_mask, d["c2"][:, C2_MASK:NC2])
            t_mask = A.do(lambda e: e.activation(maskr[:, :], raw_mask, ACT.Copy), t_mask)
            z = G.do(lambda e: e.memset(PW[:, :, :], 0.0))
            t_pw = []
            for g in range(4):
                r = slice(64 * (g % 2), 64 * (g % 2) + 64)
                t_pw.append(load(G, PW[r, g // 2, 64 * (g % 2):64 * (g % 2) + 64], d["pool_w_2"][l, g], z))
            sets = ["x", "c"]
            full = sets if l == 0 else ["x"]
            acts = norm2(l, 1, sets)
            by = {a[0]: a for a in acts}
            fa = [by[s] for s in full]
            w = d["w_in_2"][l]
            OFF = {"x": (0, T), "c": (T, TC)}
            cv = {}
            vn = []
            for half in range(2):
                def post(i, b, t, half=half):
                    v = A.do(lambda e: e.activation(P[:, i, 256 * half:256 * half + 256], ps[:, b, 0:256], ACT.Copy), t)
                    banks.give(b, v)
                    vn.append(v)
                gemm_tm(w, 8, 2048 + 256 * half, 256, by["x"], 4, post)
            vb_toks = []
            vb_sem = [sem(f"vb{l}"), 0]
            for j in range(4):
                for i in range(8):
                    r0 = 64 * (i % 2) + BAND0[j]
                    t = G.dma(lambda e, j=j, i=i, r0=r0: e.dma_start(
                        VB[32 * (i % 4):32 * (i % 4) + 32, j, i // 4, :], P[r0:r0 + 32, i // 2, :]), vb_sem, *vn)
            vb_toks = [t]
            vx = []
            for half in range(2):
                def post(i, b, t, half=half):
                    v = V.do(lambda e: e.tensor_copy(VX[:, i, 256 * half:256 * half + 256], ps[:, b, 0:256]), t)
                    banks.give(b, v)
                    vx.append(v)
                gemm_tm(w, 8, 2048 + 256 * half, 256, by["c"], 2, post)
            kk_toks, qq_toks = {"x": [], "c": []}, {"x": {}, "c": {}}
            for pair in range(2):
                def post(n, s, b, t, pair=pair):
                    t0, nt = OFF[s]
                    k = 2 * pair + n
                    a, v = split_to(ps[:, b, 0:nt], KH[:, k, t0:t0 + nt], KL[:, k, t0:t0 + nt], [t])
                    banks.give(b, a, v)
                    kk_toks[s] += [a, v]
                gemm_fm(w, 8, [1536 + 256 * pair, 1664 + 256 * pair], [by[s] for s in sets], post)
            for stage, c0 in enumerate((0, 512, 256)):
                def post(n, s, b, t, stage=stage):
                    t0, nt = OFF[s]
                    o = CV[:, n, t0:t0 + nt]
                    src = ps[:, b, 0:nt]
                    if stage == 0:
                        v = V.do(lambda e: e.tensor_copy(o, src), t)
                    elif stage == 1:
                        i, fr = tmp.take()
                        a_ = Tm[:, i, 0:nt]
                        cw = lambda k: p("conv_w_2", 6 * l + 2 * k + n)
                        v = V.do(lambda e: e.tensor_tensor(a_, o, src, ALU.mult), t, cv[n, s], fr)
                        v = V.do(lambda e: e.tensor_scalar(o, a_, cw(1), None, ALU.mult), v)
                        v = V.do(lambda e: e.scalar_tensor_tensor(o[:, 1:nt], a_[:, 0:nt - 1], cw(0), o[:, 1:nt],
                                                                  ALU.mult, ALU.add), v)
                        v = V.do(lambda e: e.scalar_tensor_tensor(o[:, 0:nt - 1], a_[:, 1:nt], cw(2),
                                                                  o[:, 0:nt - 1], ALU.mult, ALU.add), v)
                        tmp.give(i, v)
                    else:
                        v = V.do(lambda e: e.tensor_tensor(o, o, src, ALU.mult), t, cv[n, s])
                    banks.give(b, v)
                    cv[n, s] = v
                gemm_fm(w, 8, [c0, c0 + 128], fa, post)
            pv = {}
            pt_free = [None]

            def pool_post(n, s, b, t):
                t0, nt = OFF[s]
                W_ = nt + 16
                buf = [PT[:, 528 * q:528 * q + W_] for q in range(3)]
                v0 = V.do(lambda e: e.memset(buf[0], 0.0), *pt_free)
                v = V.do(lambda e: e.tensor_copy(buf[0][:, 8:8 + nt], ps[:, b, 0:nt]), t, v0)
                banks.give(b, v)

                def add(dst, src, lo, hi, a, b_, rows, *tk):
                    r = slice(*rows)
                    return V.do(lambda e: e.tensor_tensor(dst[r, lo:hi], src[r, lo - a:hi - a],
                                                          src[r, lo + b_:hi + b_], ALU.add), *tk)
                s2_ = add(buf[1], buf[0], 1, W_, 1, 0, (0, 128), v, *pt_free)
                if n == 0:
                    s4_ = add(buf[2], buf[1], 8, 8 + nt, 1, 1, (64, 128), s2_)
                    src = [(slice(0, 64), buf[1]), (slice(64, 128), buf[2])]
                    last = [s2_, s4_]
                else:
                    s4_ = add(buf[2], buf[1], 2, W_ - 1, 1, 1, (0, 128), s2_)
                    s8_ = add(buf[1], buf[2], 4, W_ - 3, 2, 2, (0, 128), s4_)
                    s16 = add(buf[2], buf[1], 8, 8 + nt, 4, 4, (64, 128), s8_)
                    src = [(slice(0, 64), buf[1]), (slice(64, 128), buf[2])]
                    last = [s8_, s16]
                o = PV[:, n, t0:t0 + nt]
                ws = []
                for r, bf in src:
                    ws.append(V.do(lambda e, r=r, bf=bf: e.scalar_tensor_tensor(
                        o[r, 8:nt - 8], bf[r, 16:nt], c2[r, C2_RW + n:C2_RW + n + 1], buf[0][r, 16:nt],
                        ALU.mult, ALU.subtract), *last, t_c2))
                    for e0, x0 in ((0, 0), (8, nt - 8)):
                        ed = c2[r, C2_EDGE + 16 * n + e0:C2_EDGE + 16 * n + e0 + 8]
                        q = V.do(lambda e, r=r, bf=bf, ed=ed, x0=x0: e.tensor_tensor(
                            o[r, x0:x0 + 8], bf[r, 8 + x0:16 + x0], ed, ALU.mult), *last, t_c2)
                        ws.append(V.do(lambda e, r=r, x0=x0: e.tensor_tensor(
                            o[r, x0:x0 + 8], o[r, x0:x0 + 8], buf[0][r, 8 + x0:16 + x0], ALU.subtract), q))
                pt_free[:] = ws

                def second():
                    b2, fr = banks.take()
                    t2 = mm(ps[:, b2, 0:nt], PW[:, n, :], o, True, True, ws, t_pw, fr, inc=True)
                    v2 = V.do(lambda e: e.tensor_scalar(o, ps[:, b2, 0:nt], p("pool_scale_2", 2 * l + n), None,
                                                        ALU.mult), t2)
                    banks.give(b2, v2)
                    pv[n, s] = v2
                later.append(second)
            gemm_fm(w, 8, [768, 896], fa, pool_post)
            held = []
            for pair in range(2):
                gemm_fm(w, 8, [1024 + 256 * pair, 1152 + 256 * pair], fa,
                        lambda n, s, b, t, pair=pair: held.append((2 * pair + n, s, b, t)))
            h_free = [PE.last()]
            for k, s, b, t in sorted(held, key=lambda x: x[0]):
                t0, nt = OFF[s]
                hi, lo, src = Hh[:, 4 + k, t0:t0 + nt], Hl[:, 4 + k, t0:t0 + nt], ps[:, b, 0:nt]
                if s == "x":
                    hi, lo = (y.rearrange("p (j r c) -> p j r c", j=4, c=16) for y in (hi, lo))
                    src = src.rearrange("p (r j c) -> p j r c", r=8, c=16)
                a = A.do(lambda e: e.activation(hi, src, ACT.Copy, scale=0.125), t, h_free)
                for j in range(4 if s == "x" else 1):
                    lo_, src_, hi_ = (y[:, j] if s == "x" else y for y in (lo, src, hi))
                    v = V.do(lambda e: e.scalar_tensor_tensor(lo_, src_, 0.125, hi_, ALU.mult, ALU.subtract), a)
                banks.give(b, a, v)
                qq_toks[s][k] = [a, v]
            mix = {s: [[] for _ in range(8)] for s in full}

            def mix_cp(s):
                t0, nt = OFF[s]
                for n in range(2):
                    a, v = split_to(CV[:, n, t0:t0 + nt], Hh[:, n, t0:t0 + nt], Hl[:, n, t0:t0 + nt],
                                    [cv[n, s], *h_free])
                    mix[s][n] = [a, v]
                    a, v = split_to(PV[:, n, t0:t0 + nt], Hh[:, 2 + n, t0:t0 + nt], Hl[:, 2 + n, t0:t0 + nt],
                                    [pv[n, s], *h_free])
                    mix[s][2 + n] = [a, v]
            tap(f"CV{l}", CV[:, :, :], [cv[n, s] for n in range(2) for s in full])
            tap(f"PV{l}", PV[:, :, :], [pv[n, s] for n in range(2) for s in full])

            pr, ptr = Ring(4), Ring(3)
            for q in range(4):
                pr.give(q, vb_toks[0])
            for q in range(3):
                ptr.give(q, *pt_free)
            PT3 = PT[:, 0:1584].rearrange("p (a b) -> p a b", a=3)
            rb_done = {}
            rb_tok = {}
            rb_sem = [[sem(f"rb{l}{i}"), 0] for i in range(4)]

            def bias_load(h):
                for r in range(8):
                    src = bass.AP(d["rpb_2"].tensor, ((l * 8 + h) * 16 + 7 - r) * 64, [[1, 16], [1, 512]])
                    t = G.dma(lambda e, r=r, src=src: e.dma_start(RB[16 * r:16 * r + 16, h % 4, :], src),
                              rb_sem[h % 4], rb_done.get(h - 4, t_mask))
                rb_tok[h] = t

            def n_scores(u, box):
                h, kind, j = u
                if kind == "x" and j == 0 and h % 2 == 0:
                    for hh in ([0, 1, 2, 3] if h == 0 else [h + 2, h + 3] if h < 6 else []):
                        bias_load(hh)
                r = slice(64 * (h % 2), 64 * (h % 2) + 64)
                b, f = banks.take()
                def scores(out, q_, k_, *toks, first=True):
                    mm(out, q_(Hh), k_(KH), first, False, f, *toks)
                    mm(out, q_(Hh), k_(KL), False, False)
                    return mm(out, q_(Hl), k_(KH), False, True, inc=True)

                if kind == "x":
                    q_ = lambda H_: H_[r, 4 + h // 2, 128 * j:128 * j + 128]
                    mm(ps[:, b, 0:256], identr[:, :], maskr[:, 256 * KIND[j]:256 * KIND[j] + 256], True, False,
                       t_ir, t_mask, f)
                    scores(ps[:, b, 0:256].rearrange("p (i c) -> p i c", c=32), q_,
                           lambda K_: K_[r, h // 2, 0:T].rearrange("p (i c) -> p i c", c=64)[
                               :, :, BAND0[j]:BAND0[j] + 32], qq_toks["x"][h // 2], kk_toks["x"], first=False)
                    t = scores(ps[:, b, 256:512], q_, lambda K_: K_[r, h // 2, T:T + TC], kk_toks["c"])
                    sl = ps[:, b, 0:256].rearrange("p (i c) -> p i c", c=32)
                    off = BAND0[j] - 16 * j
                    bi = RB[:, h % 4, :].rearrange("p (i c) -> p i c", c=64)[:, :, 32 - off:-off:-1]
                    t = V.do(lambda e: e.tensor_tensor(sl, sl, bi, ALU.add), t, rb_tok[h])
                    if j == 3:
                        rb_done[h] = t
                    n = 512
                else:
                    t = scores(ps[:, b, 0:TC], lambda H_: H_[r, 4 + h // 2, T + 128 * j:T + 128 * j + 128],
                               lambda K_: K_[r, h // 2, T:T + TC], qq_toks["c"][h // 2], kk_toks["c"])
                    n = TC
                q, fq = pr.take()
                jj, a = softmax(b, n, t, P, q, fq)
                box.update(q=q, j=jj, t=a, n=n)

            def n_scale(u, box):
                q, jj, n = box["q"], box["j"], box["n"]
                v = V.do(lambda e: e.reciprocal(sm[:, jj, 3:4], sm[:, jj, 1:2]), box["t"])
                box["t"] = V.do(lambda e: e.tensor_scalar(P[:, q, 0:n], P[:, q, 0:n], sm[:, jj, 3:4], None,
                                                          ALU.mult), v)
                small.give(jj, box["t"])

            def n_turn(u, box):
                box["m"], box["t2"] = turn(P, box["q"], box["n"], box["t"], PT3, pr, ptr, A)

            def n_out(u, box):
                h, kind, j = u
                m = box["m"]
                key, hb = (h // 2, kind, j), h % 2
                if hb == 0:
                    ot[key] = [*banks.take(), []]
                b, f, ts = ot[key]
                nk = box["n"] // 128
                for k in range(nk):
                    if kind == "x":
                        vv = VB[:, j, k, 64 * h:64 * h + 64] if k < 2 else VX[:, k - 2, 64 * h:64 * h + 64]
                    else:
                        vv = VX[:, k, 64 * h:64 * h + 64]
                    t = mm(ps[64 * hb:64 * hb + 64, b, 0:128], vv, PT3[:, m, 128 * k:128 * k + 128], k == 0,
                           k == nk - 1, box["t2"], vb_toks, vx, f, inc=k == nk - 1)
                ptr.give(m, t)
                ts.append(t)

            def n_final(u, box):
                h, kind, j = u
                if h % 2 == 0:
                    return
                b, _, ts = ot[h // 2, kind, j]
                k = 4 + h // 2
                t0 = 128 * j + OFF[kind][0]
                a, v = split_to(ps[:, b, 0:128], Hh[:, k, t0:t0 + 128], Hl[:, k, t0:t0 + 128], [*ts, *h_free])
                banks.give(b, a, v)
                mix[kind][k] += [a, v]
            ot = {}
            units = []
            for hp in range(4):
                for kind in full:
                    for j in range(4 if kind == "x" else 2):
                        units += [(2 * hp, kind, j), (2 * hp + 1, kind, j)]
            pipeline(units, [n_turn, n_scores, n_scale, n_out, n_final], [3, 0, 1, 4, 5],
                     {2 + 3 * n: [lambda s=s: mix_cp(s)] for n, s in enumerate(full)})
            residual(d["w_out_2"][l], 8, [(s, Hh, Hl, OFF[s][0], OFF[s][1], mix[s]) + ((True,) if s == "x" else ()) for s in full],
                     lambda k, s: CF[l][:, 4, k, SI[s]:SI[s] + 1], C=C,
                     next_norm=following(l, 1) if l == 0 else None)
            fence()
            s5.close()
            tap(f"X5{l}", X[:, :, :], [xt["x", k] for k in range(8)])
            if l == 0:
                tap(f"C5{l}", C[:, :, :], [xt["c", k] for k in range(8)])
            ffn(l, 1, 2, full, f"b{l}")
            tap(f"X6{l}", X[:, :, :], [xt["x", k] for k in range(8)])

        b, t = rstd_spread(rstd_sums(sums["x"], 0, T, 1024), T)
        for k in range(8):
            v = V.do(lambda e, k=k: e.scalar_tensor_tensor(X[:, k, :], X[:, k, :], p("final_g_2", k), ps[:, b, :],
                                                           ALU.mult, ALU.mult), t)
            st = S.dma(lambda e, k=k: e.dma_start(d["out"][128 * k:128 * k + 128, :], X[:, k, :]), store_sem, v)
        S.wait(st)

        if plan is not None:
            block = ctx.enter_context(nc.Block())
            block.sync(S.play)
            block.tensor(PE.play)
            block.scalar(A.play)
            block.vector(V.play)
            block.gpsimd(G.play)
    return listing


def layouts(a):
    def cols(v):
        return v.reshape(-1, 128).T

    two = lambda v: np.concatenate([v, v], 0)
    pk = {
        "norm_mix_g": cols(a["norm_mix_g"][0]), "mix_out_g": cols(a["mix_out_g"][0].reshape(-1)),
        "norm_mem_g": cols(a["norm_mem_g"][0]), "mem_kv_norm_g": cols(a["mem_kv_norm_g"][0]),
        "norm_ffn_g": cols(a["norm_ffn_g"][0]), "q_norm_g": two(a["q_norm_g"][0])[:, None],
        "k_norm_g": two(a["k_norm_g"][0].T), "cmp_b1": cols(a["cmp_b1"][0].reshape(-1)),
        "cmp_b2": two(a["cmp_b2"][0, 0])[:, None], "mem_q_norm_g": a["mem_q_norm_g"][0][:, None],
        "mem_k_norm_g": a["mem_k_norm_g"][0][:, None], "sg_b": a["sg_b"][0].T,
        "cmp_pos": a["cmp_pos"][0].reshape(2, 16, 128).transpose(2, 0, 1).reshape(128, 32),
        "norm_g_2": cols(a["norm_g_2"].reshape(-1)), "b_mod_2": cols(a["b_mod_2"].reshape(-1)),
        "conv_w_2": cols(a["conv_w_2"].reshape(-1)), "pool_scale_2": cols(a["pool_scale_2"].reshape(-1)),
        "final_g_2": cols(a["final_g_2"]),
    }
    c, c1, c2 = constants()
    w_in = a["w_in"][0]
    q = w_in[:, 1024:1536].reshape(1024, 2, 4, 64).transpose(0, 2, 1, 3).reshape(1024, 512)
    rows = np.concatenate([a["sg_ln_g"][0], a["sg_ln_b"][0], a["cmp_b2"][0, 1]])
    return {
        "x": a["x"][0].T, "mem": a["mem"][0].T, "ctx_2": a["ctx_2"][0].T,
        "par": np.concatenate([pk[n] for n, _ in PARAMS], 1), "con": c, "c1": c1, "c2": c2,
        "rows": np.broadcast_to(rows, (128, 1088)),
        "w_in": np.concatenate([w_in[:, :1024], q, w_in[:, 1536:]], 1),
        "sg_w": a["sg_w"][0].transpose(2, 0, 1), "cmp_w1": a["cmp_w1"][0],
        "cmp_w2": np.concatenate([a["cmp_w2"][0]] * 2, 2).reshape(2, 2, 128, 128).transpose(2, 0, 1, 3),
        "w_out": a["w_out"][0], "w_mq": a["w_mq"][0], "w_mkv": a["w_mkv"][0], "w_mo": a["w_mo"][0],
        "w_ff1": a["w_ff1"][0], "w_ff2": a["w_ff2"][0], "w_mod_t": a["w_mod_2"].transpose(0, 2, 1),
        "cc_rows": np.broadcast_to(np.concatenate([a["c_2"][0], a["c_ctx_2"]]), (128, 2048)),
        "ffn_w_in_2": a["ffn_w_in_2"], "ffn_w_out_2": a["ffn_w_out_2"], "w_in_2": a["w_in_2"],
        "pool_w_2": a["pool_w_2"], "w_out_2": a["w_out_2"],
        "rpb_2": np.pad(a["rpb_2"], ((0, 0), (0, 0), (0, 1), (16, 17)))[..., ::-1],
    }


def kernel(**inputs):
    import concourse.bacc as _bacc
    from concourse.bass_utils import run_bass_kernel_spmd as _run

    arrays = {k: np.ascontiguousarray(v) for k, v in layouts({k: np.asarray(v) for k, v in inputs.items()}).items()}

    nc = _bacc.Bacc("TRN2", target_bir_lowering=False, num_devices=1)
    scratch = _bacc.Bacc("TRN2", target_bir_lowering=False, num_devices=1)
    build(nc, scratch, {k: v.shape for k, v in arrays.items()})
    r = _run(nc, [{f"in_{k}": v for k, v in arrays.items()}], core_ids=[0])
    return np.ascontiguousarray(r.results[0]["out"].T).reshape(1, T, 1024)


def build(nc, scratch, shapes, taps=None, stop=None):
    d = {k: nc.dram_tensor(f"in_{k}", s, F32, kind="ExternalInput").ap() for k, s in shapes.items()}
    d["out"] = nc.dram_tensor("out", (1024, T), F32, kind="ExternalOutput").ap()
    tp = {k: nc.dram_tensor("tap_" + k, s, F32, kind="ExternalOutput").ap() for k, s in (taps or {}).items()}
    plan = program(scratch, d, None, stop, tp)
    program(nc, d, plan, stop, tp)
```

```python
from contextlib import ExitStack

import numpy as np

import concourse.bass as bass
from concourse import mybir

F32 = mybir.dt.float32
F32R = mybir.dt.float32r
ALU = mybir.AluOpType
ACT = mybir.ActivationFunctionType
AX = mybir.AxisListType

NEG = -1e30
EPS = 1e-6
T = 512
TC = 256
FF2 = 2816
RAW = 3
HL = 3
AHEAD = 2

PARAMS = [("norm_mix_g", 8), ("mix_out_g", 8), ("norm_mem_g", 8), ("mem_kv_norm_g", 8),
          ("norm_ffn_g", 8), ("q_norm_g", 1), ("k_norm_g", 3), ("cmp_b1", 4), ("cmp_b2", 1),
          ("mem_q_norm_g", 1), ("mem_k_norm_g", 1), ("sg_b", 8), ("cmp_pos", 32),
          ("norm_g_2", 48), ("b_mod_2", 144), ("conv_w_2", 12),
          ("pool_scale_2", 4), ("final_g_2", 8)]
PCOL = {}
_at = 0
for _n, _w in PARAMS:
    PCOL[_n] = _at
    _at += _w
NPAR = _at
CIDENT, CONES, CBLOCK, NCONST = 0, 128, 256, 384
C1_CAUSAL, C1_SGU, C1_CMP, NC1 = 128, 256, 384, 384 + 124
C2_EDGE, C2_RW, C2_MASK, NC2 = 0, 32, 34, 34 + 768
BAND0 = [0, 8, 24, 32]
KIND = [0, 1, 1, 2]


def constants():
    c = np.zeros((128, NCONST), np.float32)
    c[:, CIDENT:CIDENT + 128] = np.eye(128)
    c[:, CONES:CONES + 128] = 1
    c[:64, CBLOCK:CBLOCK + 64] = 1
    c[64:, CBLOCK + 64:CBLOCK + 128] = 1
    c1 = np.zeros((128, NC1), np.float32)
    q, k = np.arange(128)[:, None], np.arange(128)[None, :]
    c1[:, C1_CAUSAL:C1_CAUSAL + 128] = np.where(k <= q, 0, NEG)
    c1[:, C1_SGU:C1_SGU + 128] = q <= k
    for i in range(4):
        n = np.arange(31)[None, :]
        c1[:, C1_CMP + 31 * i:C1_CMP + 31 * i + 31] = np.where(16 * n + 31 <= q + 128 * i, 0, NEG)
    c2 = np.zeros((128, NC2), np.float32)
    for kind, j in ((0, 0), (1, 1), (2, 3)):
        col = 16 * j + np.arange(128)[:, None] % 16
        kc = BAND0[j] + np.arange(256)[None, :] % 32
        start = np.clip(col - 8, 0, 48)
        c2[:, C2_MASK + 256 * kind:C2_MASK + 256 * kind + 256] = np.where((kc >= start) & (kc < start + 16), 0, NEG)
    for tile in range(2):
        for half in range(2):
            w = (2, 4, 8, 16)[2 * tile + half]
            rows = slice(64 * half, 64 * half + 64)
            for e in range(8):
                c2[rows, C2_EDGE + 16 * tile + e] = 1 / (min(e + w - w // 2, 10 ** 6) - max(e - w // 2, 0))
                back = 8 - e
                c2[rows, C2_EDGE + 16 * tile + 8 + e] = 1 / (min(w - w // 2, back) + w // 2)
            c2[rows, C2_RW + tile] = 1 / w
    return c, c1, c2


class Recorder:

    def activation(self, *a, **k):
        return lambda e: e.activation(*a, **k)

    def tensor_tensor(self, *a, **k):
        return lambda e: e.tensor_tensor(*a, **k)

    def tensor_scalar(self, *a, **k):
        return lambda e: e.tensor_scalar(*a, **k)

    def scalar_tensor_tensor(self, *a, **k):
        return lambda e: e.scalar_tensor_tensor(*a, **k)

    def tensor_tensor_reduce(self, *a, **k):
        return lambda e: e.tensor_tensor_reduce(*a, **k)

    def tensor_reduce(self, *a, **k):
        return lambda e: e.tensor_reduce(*a, **k)

    def tensor_copy(self, *a, **k):
        return lambda e: e.tensor_copy(*a, **k)

    def reciprocal(self, *a, **k):
        return lambda e: e.reciprocal(*a, **k)

    def memset(self, *a, **k):
        return lambda e: e.memset(*a, **k)

    def bn_stats(self, *a, **k):
        return lambda e: e.bn_stats(*a, **k)

    def bn_aggr(self, *a, **k):
        return lambda e: e.bn_aggr(*a, **k)

    def matmul(self, *a, **k):
        return lambda e: e.matmul(*a, **k)

    def transpose(self, *a, **k):
        return lambda e: e.transpose(*a, **k)

    def dma_start(self, *a, **k):
        return lambda e: e.dma_start(*a, **k)


RECORD = Recorder()


class Lane:

    def __init__(self, name, sem):
        self.name, self.sem, self.n, self.ops, self.seen = name, sem, 0, [], {}

    def wait(self, *toks):
        for t in toks:
            if t is None:
                continue
            if isinstance(t, list):
                self.wait(*t)
                continue
            sem, v = t
            if self.seen.get(id(sem), 0) < v:
                self.seen[id(sem)] = v
                self.ops.append(("w", sem, v))

    def do(self, fn, *toks):
        self.wait(*toks)
        self.n += 1
        self.ops.append(("i", fn(RECORD), self.sem, 1))
        return (self.sem, self.n)

    def go(self, fn, *toks):
        self.wait(*toks)
        self.ops.append(("n", fn(RECORD)))

    def dma(self, fn, count, *toks):
        self.wait(*toks)
        count[1] += 16
        self.ops.append(("i", fn(RECORD), count[0], 16))
        return (count[0], count[1])

    def last(self):
        return (self.sem, self.n) if self.n else None

    def play(self, eng):
        for op in self.ops:
            if op[0] == "w":
                eng.wait_ge(op[1], op[2])
            elif op[0] == "i":
                op[1](eng).then_inc(op[2], op[3])
            else:
                op[1](eng)


class Banks:

    def __init__(self, n):
        self.free = [(i, []) for i in range(n)]

    def take(self):
        return self.free.pop(0)

    def give(self, i, *toks):
        self.free.append((i, list(toks)))


class Ring:

    def __init__(self, n):
        self.n, self.at, self.toks = n, 0, [[] for _ in range(n)]

    def take(self):
        i = self.at % self.n
        self.at += 1
        t, self.toks[i] = self.toks[i], None
        assert t is not None
        return i, t

    def give(self, i, *toks):
        self.toks[i] = list(toks)


class Chunk:

    def __init__(self, i, kt, cols, raw):
        self.i, self.kt, self.cols, self.raw = i, kt, cols, raw


def program(nc, d, plan):
    listing = []
    ctx = ExitStack()
    with ctx:
        def sb(name, shape, dt=F32, where=None):
            return (where or ctx).enter_context(nc.sbuf_tensor(name, shape, dt))

        def sem(name):
            return ctx.enter_context(nc.semaphore(name))

        PE, A, V, G, S = (Lane(n, sem("done_" + n)) for n in ("pe", "act", "dve", "pool", "sp"))
        LANES = [PE, A, V, G]
        raw_sem = [[sem(f"raw{i}"), 0] for i in range(RAW)]
        load_sems = [[sem(f"load{i}"), 0] for i in range(32)]
        load_at = [0]
        store_sem = [sem("store"), 0]

        ps = ctx.enter_context(nc.psum_tensor("ps", [128, 8, 512], F32))
        X = sb("X", [128, 8, T])
        Hh = sb("Hh", [128, 8, T + TC], F32R)
        Hl = sb("Hl", [128, 8, T + TC], F32R)
        rawb = sb("rawb", [128, RAW, 1024])
        hib = sb("hib", [128, HL, 1024], F32R)
        lob = sb("lob", [128, HL, 1024], F32R)
        Tm = sb("Tm", [128, 4, 512])
        ACC = sb("ACC", [128, T + TC])
        par = sb("par", [128, NPAR])
        con = sb("con", [128, NCONST])
        M = sb("M", [128, 2, 72, 2])
        M2 = sb("M2", [128, 72, 2])
        gm = sb("gm", [128, 8])
        sm = sb("sm", [128, 24, 8])
        identr = sb("identr", [128, 128], F32R)
        ident, ones, blk = con[:, 0:128], con[:, 128:256], con[:, 256:384]

        banks = Banks(8)
        tmp = Ring(4)
        small = Ring(24)
        chunks_done = {}
        hl_done = {}
        ready = {}
        later = []
        state = {"issued": 0, "used": 0}

        def load(lane, dst, src, *toks):
            s = load_sems[load_at[0]]
            load_at[0] += 1
            return lane.dma(lambda e: e.dma_start(dst, src), s, *toks)

        def p(name, i=0, n=1):
            return par[:, PCOL[name] + i:PCOL[name] + i + n]

        def issue(upto):
            while state["issued"] < min(upto, len(plan)):
                i = state["issued"]
                state["issued"] += 1
                src, kt, cols, raw = plan[i]
                r = rawb[:, i % RAW, 0:kt * cols].rearrange("p (k c) -> p k c", c=cols)
                each = cols // len(src)
                for n, piece in enumerate(src):
                    t = S.dma(lambda e, o=r[:, :, n * each:n * each + each], x=piece: e.dma_start(o, x),
                              raw_sem[i % RAW], chunks_done.get(i - RAW))
                if raw:
                    ready[i] = t
                    continue
                flat = rawb[:, i % RAW, 0:kt * cols]
                hi, lo = hib[:, i % HL, 0:kt * cols], lob[:, i % HL, 0:kt * cols]
                a = A.do(lambda e, hi=hi, flat=flat: e.activation(hi, flat, ACT.Copy), t, hl_done.get(i - HL))
                b = V.do(lambda e, hi=hi, lo=lo, flat=flat: e.tensor_tensor(lo, flat, hi, ALU.subtract),
                         a, hl_done.get(i - HL))
                ready[i] = [a, b]
                chunks_done[i] = [a, b]

        def chunk(src, kt, cols, raw=False, ahead=AHEAD):
            listing.append((src, kt, cols, raw))
            c = Chunk(state["used"], kt, cols, raw)
            state["used"] += 1
            if plan is not None:
                issue(c.i + 1 + ahead)
            c.ready = ready.get(c.i)
            if raw:
                c.w = rawb[:, c.i % RAW, 0:kt * cols].rearrange("p (k c) -> p k c", c=cols)
            else:
                c.hi = hib[:, c.i % HL, 0:kt * cols].rearrange("p (k c) -> p k c", c=cols)
                c.lo = lob[:, c.i % HL, 0:kt * cols].rearrange("p (k c) -> p k c", c=cols)
            return c

        def used(c, tok):
            hl_done[c.i] = tok
            if c.raw:
                chunks_done[c.i] = tok

        def mm(out, lhsT, rhs, start, stop, *toks, inc=False):
            f = lambda e: e.matmul(out, lhsT, rhs, start=start, stop=stop)
            if inc:
                return PE.do(f, *toks)
            PE.go(f, *toks)

        def run_later():
            todo, later[:] = later[:], []
            for f in todo:
                f()

        between = []

        def gemm(parts, outs, pick, post):
            got = [banks.take() for _ in outs]
            last_k = parts[-1][1] + parts[-1][2] - 1
            toks = [None] * len(outs)

            def products(c, k0, kt, some):
                for n, o in some:
                    b, free = got[n]
                    for kc in range(kt):
                        k = k0 + kc
                        out, lh, ll, rh, rl, wt = pick(o, c, k, kc)
                        dst = out(b)
                        mm(dst, lh, rh, k == 0, False, c.ready, free if k == 0 else None, wt)
                        mm(dst, lh, rl, False, False)
                        end = kc == kt - 1
                        t = mm(dst, ll, rh, False, k == last_k, inc=end)
                    toks[n] = t
                return t

            each = list(enumerate(outs))
            first = []
            if between:
                first = [chunk(parts[0][0], *parts[0][2:]), chunk(parts[1][0], *parts[1][2:], ahead=1)]
                late = [x for x in each if x[1][1][0] == "c"] if isinstance(outs[0], tuple) else []
                early = [x for x in each if x not in late]
                steps, between[:] = between[:], []
                done = [products(first[0], *parts[0][1:3], early)]
                steps[0]()
                done.append(products(first[1], *parts[1][1:3], early[:1]))
                steps[1]()
                done[1] = products(first[1], *parts[1][1:3], early[1:])
                for f in steps[2:]:
                    f()
                for n in range(2):
                    used(first[n], products(first[n], *parts[n][1:3], late) if late else done[n])
                run_later()
                mod_step()
                mod_step()
            for src, k0, kt, cols in parts[len(first):]:
                c = chunk(src, kt, cols)
                used(c, products(c, k0, kt, each))
                run_later()
                mod_step()
            for n, o in enumerate(outs):
                post(o, got[n][0], toks[n])

        def rows(w, k0, kt, c0, cols):
            return [w.rearrange("(k p) n -> p k n", p=128)[:, k0:k0 + kt, c0:c0 + cols]]

        def k_parts(total):
            return [(k, min(4, total - k)) for k in range(0, total, 4)]

        def gemm_fm(w, kt, cols2, acts, post):
            parts = []
            for k0, n in k_parts(kt):
                if len(cols2) == 1:
                    parts.append((rows(w, k0, n, cols2[0], 128), k0, n, 128))
                elif cols2[1] == cols2[0] + 128:
                    parts.append((rows(w, k0, n, cols2[0], 256), k0, n, 256))
                else:
                    parts.append((rows(w, k0, n, cols2[0], 128) + rows(w, k0, n, cols2[1], 128), k0, n, 256))
            outs = [(n, a) for a in acts for n in range(len(cols2))]

            def pick(o, c, k, kc):
                n, (_, hi, lo, t0, nt, tk, *by_block) = o
                if by_block and k >= 4:
                    turned = lambda x: x[:, k, t0:t0 + nt].rearrange("p (j r c) -> p r j c", j=4, c=16)
                    return (lambda b: ps[:, b, 0:nt].rearrange("p (r j c) -> p r j c", j=4, c=16),
                            c.hi[:, kc, 128 * n:128 * n + 128], c.lo[:, kc, 128 * n:128 * n + 128],
                            turned(hi), turned(lo), tk[k])
                return (lambda b: ps[:, b, 0:nt], c.hi[:, kc, 128 * n:128 * n + 128],
                        c.lo[:, kc, 128 * n:128 * n + 128], hi[:, k, t0:t0 + nt], lo[:, k, t0:t0 + nt],
                        tk[k])
            gemm(parts, outs, pick, lambda o, b, t: post(o[0], o[1][0], b, t))

        def gemm_tm(w, kt, c0, cols, act, tiles, post):
            parts = [(rows(w, k0, n, c0, cols), k0, n, cols) for k0, n in
                     (k_parts(kt) if cols > 128 else [(0, kt)])]
            _, hi, lo, t0, _, tk = act
            pass_cols = cols

            def pick(o, c, k, kc):
                a = t0 + 128 * o
                return (lambda b: ps[:, b, 0:pass_cols], hi[:, k, a:a + 128], lo[:, k, a:a + 128],
                        c.hi[:, kc, :], c.lo[:, kc, :], tk[k])
            gemm(parts, list(range(tiles)), pick, post)

        mods = []
        mod_state = {"loaded": 0, "used": 0, "slots": [], "left": 0, "last": None}
        mod_sem = [[sem(f"mod{i}"), 0] for i in range(4)]

        def mod_begin(layer):
            mod_state.update(layer=layer)
            mods.extend((n, h) for n in range(72) for h in range(2))

        def mod_open(count, slots, scb, junk):
            t = load(G, scb, d["cc_rows"])
            t = A.do(lambda e: e.activation(scb, scb, ACT.Silu), t)
            mod_state.update(slots=slots, scb=scb.rearrange("p (s h k) -> p s h k", s=2, h=2), junk=junk,
                             left=min(2 * count, len(mods)), done=[None] * 4, base=mod_state["used"],
                             loaded=mod_state["used"], silu=t, last=None)
            mod_load()

        def mod_slot(u):
            return (u - mod_state["base"]) % len(mod_state["slots"])

        def mod_load():
            while plan is not None and mod_state["loaded"] < mod_state["used"] + min(len(mod_state["slots"]), mod_state["left"]):
                u = mod_state["loaded"]
                mod_state["loaded"] += 1
                n, h = mods[u - mod_state["used"]]
                m = mod_slot(u)
                o = mod_state["slots"][m]
                x = d["w_mod_t"][mod_state["layer"]][128 * n:128 * n + 128, 512 * h:512 * h + 512]
                mod_state["tok", m] = G.dma(lambda e: e.dma_start(o, x), mod_sem[m], mod_state["done"][m])

        def mod_step():
            for _ in range(2):
                if not mod_state["left"] or plan is None:
                    return
                u, (n, h) = mod_state["used"], mods.pop(0)
                m = mod_slot(u)
                w, scb, l = mod_state["slots"][m], mod_state["scb"], mod_state["layer"]
                for q in range(2):
                    to = (M[:, l, n, q:q + 1], M2[:, n, q:q + 1])[h]
                    o = w if q else mod_state["junk"]
                    t = V.do(lambda e: e.tensor_tensor_reduce(o, w, scb[:, q, h, :], 1.0, 0.0, ALU.mult, ALU.add, to),
                             mod_state["tok", m], mod_state["silu"], mod_state["last"] if not q else None)
                    if not q:
                        mod_state["last"] = t
                mod_state["done"][m] = t
                mod_state["used"] += 1
                mod_state["left"] -= 1
                mod_load()

        def mod_close():
            while plan is not None and mod_state["left"]:
                mod_step()

        def mod_end():
            mod_close()
            if plan is None:
                mods[:] = []
            assert not mods
            l = mod_state["layer"]
            both = M[:, l, :, :]
            bias = p("b_mod_2", 72 * l, 72).unsqueeze(2).to_broadcast([128, 72, 2])
            t = V.do(lambda e: e.tensor_tensor(both, both, M2[:, :, :], ALU.add), V.last())
            return V.do(lambda e: e.tensor_tensor(both, both, bias, ALU.add), t)

        def mcol(l, i, k, s):
            return M[:, l, 8 * i + k, s:s + 1]

        def square_in(src, t0, nt, k, *toks):
            acc = ACC[:, t0:t0 + nt]
            if k == 0:
                return A.do(lambda e: e.activation(acc, src, ACT.Square), *toks)
            i, free = tmp.take()
            a = A.do(lambda e: e.activation(Tm[:, i, 0:nt], src, ACT.Square), free, *toks[:-1])
            v = V.do(lambda e: e.tensor_tensor(acc, acc, Tm[:, i, 0:nt], ALU.add), a, toks[-1])
            tmp.give(i, v)
            return v

        def rstd_sums(sum_tok, t0, nt, width):
            n = nt // 128
            b, free = banks.take()
            for i in range(n):
                t = mm(ps[:, b, i:i + 1], ACC[:, t0 + 128 * i:t0 + 128 * i + 128], ones[:, 0:1], True, True,
                       sum_tok, free, inc=i == n - 1)
            j, fr = small.take()
            a = A.do(lambda e: e.activation(sm[:, j, 0:n], ps[:, b, 0:n], ACT.Sqrt, bias=eps[:, 0:1],
                                            scale=1.0 / width), t, fr)
            v = V.do(lambda e: e.reciprocal(sm[:, j, 4:4 + n], sm[:, j, 0:n]), a)
            i, free2 = tmp.take()
            for q in range(n):
                w = V.do(lambda e, q=q: e.tensor_scalar(Tm[:, i, 128 * q:128 * q + 128], ident,
                                                       sm[:, j, 4 + q:5 + q], None, ALU.mult), v, free2)
            small.give(j, w)
            return b, i, w, a

        def rstd_spread(r, nt):
            b, i, w, a = r
            t = mm(ps[:, b, 0:nt], ones, Tm[:, i, 0:nt], True, True, w, a, inc=True)
            tmp.give(i, t)
            return b, t

        def split_to(src, hi, lo, toks, shift=None, eng=None):
            if shift is None:
                a = A.do(lambda e: e.activation(hi, src, ACT.Copy), *toks)
                v = (eng or V).do(lambda e: e.tensor_tensor(lo, src, hi, ALU.subtract), a, *toks)
            else:
                a = A.do(lambda e: e.activation(hi, src, ACT.Identity, bias=shift), *toks)
                v = V.do(lambda e: e.scalar_tensor_tensor(lo, src, shift, hi, ALU.add, ALU.subtract), a, *toks)
            return a, v

        def norm_steps(spec):
            src, nt, t0, sum_tok, gain, shift, toks = spec
            box, out, done = {}, [None] * 8, []

            def sums_():
                box["r"] = rstd_sums(sum_tok(), t0, nt, 1024)

            def spread():
                box["b"], box["t"] = rstd_spread(box["r"], nt)
                done.append(box["t"])

            def scale(k):
                b, t = box["b"], box["t"]
                i, free = tmp.take()
                v = V.do(lambda e: e.scalar_tensor_tensor(Tm[:, i, 0:nt], src[:, k, 0:nt], gain(k),
                                                          ps[:, b, 0:nt], ALU.mult, ALU.mult), t, free, toks())
                if k == 7:
                    banks.give(b, v)
                box[k] = (i, v)

            def apply(k):
                for x in {0: [0, 1], 7: []}.get(k, [k + 1]):
                    scale(x)
                i, v = box[k]
                hi, lo = Hh[:, k, t0:t0 + nt], Hl[:, k, t0:t0 + nt]
                a, w = split_to(Tm[:, i, 0:nt], hi, lo, [v, toks()], shift(k) if shift else None)
                tmp.give(i, w, a)
                out[k] = [a, w]
                if k == 7:
                    done.append([a, w])
            return [sums_, spread] + [lambda k=k: apply(k) for k in range(8)], out, done

        def norms(specs):
            got = [norm_steps(x) for x in specs]
            for fs in zip(*[g[0] for g in got]):
                for f in fs:
                    f()
            return [(g[1], g[2]) for g in got]

        def in_turn(steps, each=1):
            if not steps:
                return
            n = 1 if len(steps) > 8 else each

            def run():
                for f in steps[:n]:
                    f()
                in_turn(steps[n:], each)
            later.append(run)

        def head_norm(b, tok, width, nt, gain, out, blocked=True, *toks, halves=None):
            i, free = tmp.take()
            a = A.do(lambda e: e.activation(Tm[:, i, 0:nt], ps[:, b, 0:nt], ACT.Square), tok, free)

            def second():
                b2, fr = banks.take()
                t = mm(ps[:, b2, 0:nt], blk if blocked else ones, Tm[:, i, 0:nt], True, True, a, fr, inc=True)
                r = A.do(lambda e: e.activation(Tm[:, i, 0:nt], ps[:, b2, 0:nt], ACT.Sqrt,
                                                bias=eps[:, 0:1], scale=1.0 / width), t)
                v = V.do(lambda e: e.reciprocal(Tm[:, i, 0:nt], Tm[:, i, 0:nt]), r)
                banks.give(b2, r)
                if halves:
                    w = V.do(lambda e: e.scalar_tensor_tensor(
                        Tm[:, i, 0:nt], ps[:, b, 0:nt], gain, Tm[:, i, 0:nt], ALU.mult, ALU.mult), v)
                    banks.give(b, w)
                    w = [*split_to(Tm[:, i, 0:nt], *halves, [w, *toks])]
                    tmp.give(i, w)
                else:
                    w = V.do(lambda e: e.scalar_tensor_tensor(
                        out[0], ps[:, b, 0:nt], gain, Tm[:, i, 0:nt], ALU.mult, ALU.mult), v, *toks)
                    tmp.give(i, w)
                    banks.give(b, w)
                out[1](w)
            later.append(second)

        def query_sums(held, bank, put, block, width, out, toks):
            bs, free_s = bank
            heads = block.shape[-1]
            for k, b, t in held:
                i, free = tmp.take()
                a = A.do(lambda e: e.activation(Tm[:, i, :], ps[:, b, :], ACT.Square), t, free)
                toks += put(k, ps[:, b, :], b, a)

                def sums_(k=k, i=i, a=a):
                    for q in range(4):
                        c = heads * (4 * k + q)
                        t = mm(ps[:, bs, c:c + heads], Tm[:, i, 128 * q:128 * q + 128], block, True, True, a, free_s,
                               inc=q == 3)
                    tmp.give(i, t)
                    if k == 3:
                        n = 16 * heads
                        r = A.do(lambda e: e.activation(out, ps[:, bs, 0:n], ACT.Sqrt, bias=eps[:, 0:1],
                                                        scale=1.0 / width), t)
                        banks.give(bs, r)
                        toks.append(V.do(lambda e: e.reciprocal(out, out), r))
                later.append(sums_)

        def fence():
            ts = [l.last() for l in LANES]
            for l in (A, V, G):
                l.wait(*ts)

        def softmax(b, n, tok, P, i, free, scale=None):
            j, fr = small.take()
            v = V.do(lambda e: e.tensor_reduce(sm[:, j, 0:1], ps[:, b, 0:n], AX.X, ALU.max, negate=True),
                     tok, fr)
            bias = sm[:, j, 0:1]
            if scale is not None:
                v = V.do(lambda e: e.tensor_scalar(sm[:, j, 2:3], sm[:, j, 0:1], scale, None, ALU.mult), v)
                bias = sm[:, j, 2:3]
            a = A.do(lambda e: e.activation(P[:, i, 0:n], ps[:, b, 0:n], ACT.Exp, bias=bias,
                                            scale=1.0 if scale is None else scale,
                                            accum_out=sm[:, j, 1:2]), v, free)
            banks.give(b, a)
            return j, a

        flip = [0]

        def turn(P, i, n, tok, PT, pring, ptring, lane=None):
            b, free = banks.take()
            for k in range(n // 128):
                t = (PE.do if k == n // 128 - 1 else PE.go)(
                    lambda e, k=k: e.transpose(ps[:, b, 128 * k:128 * k + 128], P[:, i, 128 * k:128 * k + 128],
                                               ident), tok, free)
            pring.give(i, t)
            m, fr = ptring.take()
            flip[0] += 1
            lane = lane or (V, A)[flip[0] % 2]
            f = ((lambda e: e.tensor_copy(PT[:, m, 0:n], ps[:, b, 0:n])) if lane is V else
                 (lambda e: e.activation(PT[:, m, 0:n], ps[:, b, 0:n], ACT.Copy)))
            v = lane.do(f, t, fr)
            banks.give(b, v)
            return m, v

        def pipeline(units, stages, skew, extra={}):
            box = [{} for _ in units]
            for step in range(len(units) + skew[-1]):
                for s, f in enumerate(stages):
                    u = step - skew[s]
                    if 0 <= u < len(units):
                        f(units[u], box[u])
                for f in extra.get(step, []):
                    f()

        eps = sb("eps", [128, 2])
        t_con = load(A, con[:, :], d["con"])
        t_par = load(A, par[:, :], d["par"])
        x_dram = d["x"].rearrange("(k p) t -> p k t", p=128)
        t_xs = [load((A, G)[k % 2], X[:, k, :], x_dram[:, k, :]) for k in range(8)]
        t_x = t_xs
        t_eps = V.do(lambda e: e.memset(eps[:, 0:1], EPS))
        start = [t_con, t_par, t_eps]
        for l in LANES:
            l.wait(*start)
        t_ir = A.do(lambda e: e.activation(identr[:, :], ident, ACT.Copy))
        mod_begin(0)

        s2 = ctx.enter_context(ExitStack())
        U = sb("U", [128, 4, 512], where=s2)
        VV = sb("VV", [128, 4, 512], where=s2)
        s1 = ctx.enter_context(ExitStack())
        sgw = sb("sgw", [128, 8, 128], where=s1)
        KF = [sb(f"KF{n}", [128, 2, 512], F32R, where=s1) for n in range(2)]
        KC2 = sb("KC2", [128, 2, 2, 512], where=s1)
        XIN = sb("XIN", [128, 16, 2, 31], where=s1)
        RQ = sb("RQ", [128, 32], where=s1)
        HC = sb("HC", [128, 2, 2, 62], where=s1)
        KCT = sb("KCT", [128, 32], where=s1)
        KCR = sb("KCR", [128, 2, 32], F32R, where=s1)
        causalr = sb("causalr", [128, 256], F32R, where=s1)
        VC = sb("VC", [128, 2, 64], where=s1)
        VS = sb("VS", [128, 4, 128], where=s1)
        VW = sb("VW", [128, 4, 128], where=s1)
        SILU = sb("SILU", [128, 4, 512], where=s1)
        P = sb("P", [128, 4, 512], where=s1)
        PT = sb("PT", [128, 4, 512], where=s1)
        GA = sb("GA", [128, 4, 24], where=s1)
        rowp = sb("rowp", [128, 1088], where=s1)
        c1 = sb("c1", [128, NC1], where=s1)
        W2 = sb("W2", [128, 2, 2, 128], where=s1)
        ms = sb("ms", [128, 32], where=s1)
        kz = G.do(lambda e: e.memset(KCT[:, :], 0.0))

        tk = None
        for k in range(8):
            tk = square_in(X[:, k, :], 0, T, k, t_xs[k], tk)
        S.wait(t_xs[3])
        if plan is not None:
            issue(3)
        (hx, _), = norms([(X, T, 0, lambda: tk, lambda k: p("norm_mix_g", k), None, lambda: t_x)])
        mod_open(16, [P[:, q, :] for q in range(4)], SILU[:, :, :].rearrange("p a b -> p (a b)"), PT[:, 0, :])
        t_row = load(G, rowp[:, :], d["rows"])
        t_c1 = load(G, c1[:, :], d["c1"])
        t_sgw = load(G, sgw[:, :, :], d["sg_w"])
        t_w2 = load(G, W2[:, :, :, :], d["cmp_w2"])
        ax = ("x", Hh, Hl, 0, T, hx)
        w_in = d["w_in"]

        u_tok, v_tok = [], []

        def uv_product(dst, c0, box):
            for half in range(2):
                def post(i, b, t, dst=dst, half=half, box=box):
                    a = A.do(lambda e: e.activation(dst[:, i, 256 * half:256 * half + 256], ps[:, b, 0:256],
                                                    ACT.Gelu_apprx_tanh), t)
                    banks.give(b, a)
                    box.append(a)
                gemm_tm(w_in, 8, c0 + 256 * half, 256, ax, 4, post)

        uv_product(VV, 512, v_tok)

        t_cr = A.do(lambda e: e.activation(causalr[:, :], c1[:, 0:256], ACT.Copy), t_c1)

        sgm = V.do(lambda e: e.tensor_tensor(sgw[:, :, :], sgw[:, :, :],
                                             c1[:, C1_SGU:C1_SGU + 128].unsqueeze(1).to_broadcast([128, 8, 128]),
                                             ALU.mult), t_sgw, t_c1)
        lane_toks = []
        for i in range(4):
            row = VV[:, i, :]
            j, fr = small.take()
            j2, fr2 = small.take()
            v = V.do(lambda e, j=j, row=row: e.bn_stats(sm[:, j, 0:6], row), v_tok, fr)
            v = V.do(lambda e, j=j, j2=j2: e.bn_aggr(sm[:, j2, 0:2], sm[:, j, 0:6]), v, fr2)
            a = A.do(lambda e, j2=j2: e.activation(sm[:, j2, 2:3], sm[:, j2, 1:2], ACT.Sqrt, bias=eps[:, 0:1],
                                                   scale=1.0), v)
            v = V.do(lambda e, j2=j2: e.reciprocal(sm[:, j2, 3:4], sm[:, j2, 2:3]), a)
            v = V.do(lambda e, j2=j2, row=row: e.tensor_scalar(row, row, sm[:, j2, 0:1], sm[:, j2, 3:4],
                                                               ALU.subtract, ALU.mult), v)
            small.give(j, v)
            small.give(j2, v)
            g = G.do(lambda e, row=row: e.tensor_tensor(row, row, rowp[:, 0:512], ALU.mult), v, t_row)
            g = G.do(lambda e, row=row: e.tensor_tensor(row, row, rowp[:, 512:1024], ALU.add), g)
            lane_toks.append(g)

        c_toks = [[], []]

        def post(n, s, b, t):
            last = []
            for h in range(2):
                src = ps[64 * h:64 * h + 64, b, :]
                a = A.do(lambda e, h=h, src=src: e.activation(KC2[0:64, n, h, :], src, ACT.Copy), t)
                v = V.do(lambda e, h=h, src=src: e.tensor_copy(KC2[64:128, n, h, 0:511], src[:, 1:512]), t, a)
                last += [a, v]
            banks.give(b, *last)
            c_toks[n] += last
        gemm_fm(w_in, 8, [1536, 1664], [ax], post)

        uv_product(U, 0, u_tok)
        a_toks = []
        for g in range(8):
            b, free = banks.take()
            t = mm(ps[:, b, 0:256].rearrange("p (c x) -> p c x", x=64), sgw[:, g, :], VV[:, :, 64 * g:64 * g + 64],
                   True, True, sgm, lane_toks, free, inc=True)
            uu = U[:, :, 64 * g:64 * g + 64]
            v = V.do(lambda e, b=b, g=g, uu=uu: e.scalar_tensor_tensor(
                uu, ps[:, b, 0:256].rearrange("p (c x) -> p c x", x=64), p("sg_b", g), uu, ALU.add, ALU.mult),
                t, u_tok)
            banks.give(b, v)
            a_toks.append(v)

        comp_state = {}
        kct, vct = [], []

        def blocks(n):
            XIN_free = comp_state.get("xin")
            x_t = []
            for h in range(2):
                for part in range(2):
                    s2 = KC2[:, n, h, 16 * part:16 * part + 496].rearrange("p (m j e) -> p j m e", m=31, e=2)[:, :, :, 0]
                    po = p("cmp_pos", 16 * n + 8 * part, 8).unsqueeze(2).to_broadcast([128, 8, 31])
                    v = V.do(lambda e, s2=s2, po=po, h=h, part=part: e.tensor_tensor(
                        XIN[:, 8 * part:8 * part + 8, h, :], s2, po, ALU.add), c_toks[n],
                        XIN_free)
                    x_t.append(v)
            comp_state["x"] = x_t

        def compress(n):
            x_t = comp_state["x"]
            b0, f0 = banks.take()
            b1, f1 = banks.take()
            w1 = d["cmp_w1"][n].rearrange("(j p) n -> p j n", p=128)
            for q in range(4):
                c = chunk([w1[:, 4 * q:4 * q + 4, :]], 4, 256, raw=True)
                for half, b, f in ((0, b0, f0), (1, b1, f1)):
                    for jj in range(4):
                        j = 4 * q + jj
                        t = mm(ps[:, b, 0:62], c.w[:, jj, 128 * half:128 * half + 128],
                               XIN[:, j, :, :].rearrange("p h m -> p (h m)"), j == 0, j == 15,
                               c.ready, x_t, f, inc=jj == 3)
                    if half == 0:
                        t0_ = t
                used(c, t)
                run_later()
            comp_state["xin"] = [t0_, t]
            hh = []
            for half, b, tt in ((0, b0, t0_), (1, b1, t)):
                a = A.do(lambda e, half=half, b=b, n=n: e.activation(
                    HC[:, n, half, :], ps[:, b, 0:62], ACT.Gelu_apprx_tanh, bias=p("cmp_b1", 2 * n + half),
                    scale=1.0), tt)
                banks.give(b, a)
                hh.append(a)
            if n == 0:
                b, f = banks.take()
                for half in range(2):
                    t = mm(ps[:, b, 0:62], W2[:, 0, half, :], HC[:, 0, half, :], half == 0, half == 1, hh, t_w2,
                           f, inc=half == 1)
                j, fr = tmp.take()
                kc = Tm[:, j, 0:62]
                sq = Tm[:, j, 64:126]
                a = A.do(lambda e: e.activation(kc, ps[:, b, 0:62], ACT.Identity, bias=p("cmp_b2")), t, fr)
                a2 = A.do(lambda e: e.activation(sq, kc, ACT.Square), a)
                banks.give(b, a)
                b, f = banks.take()
                t = mm(ps[:, b, 0:62], blk, sq, True, True, a2, f, inc=True)
                a = A.do(lambda e: e.activation(Tm[:, j, 128:190], ps[:, b, 0:62], ACT.Sqrt, bias=eps[:, 0:1],
                                                scale=1.0 / 64), t)
                v = V.do(lambda e: e.reciprocal(Tm[:, j, 192:254], Tm[:, j, 128:190]), a)
                banks.give(b, a)
                for h in range(2):
                    r = slice(64 * h, 64 * h + 64)
                    kct.append(V.do(lambda e, r=r, h=h: e.scalar_tensor_tensor(
                        KCT[r, 0:31], Tm[r, j, 31 * h:31 * h + 31], p("k_norm_g", 0)[r],
                        Tm[r, j, 192 + 31 * h:192 + 31 * h + 31], ALU.mult, ALU.mult), v, kz))
                tmp.give(j, *kct)
                kct[:] = split_to(KCT[:, :], KCR[:, 0, :], KCR[:, 1, :], list(kct))
            else:
                for h in range(2):
                    b, f = banks.take()
                    for half in range(2):
                        t = mm(ps[0:31, b, 0:64], HC[:, 1, half, 31 * h:31 * h + 31], W2[:, 1, half, 0:64],
                               half == 0, half == 1, hh, t_w2, f, inc=half == 1)
                    v = V.do(lambda e, b=b, h=h: e.tensor_tensor(VC[0:31, h, :], ps[0:31, b, 0:64],
                                                                 rowp[0:31, 1024:1088], ALU.add), t)
                    banks.give(b, v)
                    vct.append(v)
        blocks(0)
        compress(0)
        q_toks, k_toks = [], {}

        kv_v = []
        for n, (vdst, gi) in enumerate(((VS, 1), (VW, 2))):
            c0 = 1792 + 256 * n
            got = [banks.take() for _ in range(5)]
            for k0, kt in k_parts(8):
                c = chunk(rows(w_in, k0, kt, c0, 256), kt, 256)
                for kc in range(kt):
                    k = k0 + kc
                    b, free = got[4]
                    mm(ps[:, b, :], c.hi[:, kc, 0:128], Hh[:, k, 0:T], k == 0, False, c.ready, free, hx[k])
                    mm(ps[:, b, :], c.hi[:, kc, 0:128], Hl[:, k, 0:T], False, False)
                    t = mm(ps[:, b, :], c.lo[:, kc, 0:128], Hh[:, k, 0:T], False, k == 7, inc=True)
                kt_tok = t
                vts = []
                for i in range(4):
                    b, free = got[i]
                    for kc in range(kt):
                        k = k0 + kc
                        h_, l_ = Hh[:, k, 128 * i:128 * i + 128], Hl[:, k, 128 * i:128 * i + 128]
                        mm(ps[:, b, 0:128], h_, c.hi[:, kc, 128:256], k == 0, False, free)
                        mm(ps[:, b, 0:128], h_, c.lo[:, kc, 128:256], False, False)
                        t = mm(ps[:, b, 0:128], l_, c.hi[:, kc, 128:256], False, k == 7, inc=True)
                    vts.append(t)
                used(c, t)
                run_later()
                mod_step()
            for i in range(4):
                b = got[i][0]
                v = V.do(lambda e, b=b, i=i, vdst=vdst: e.tensor_copy(vdst[:, i, :], ps[:, b, 0:128]), vts[i])
                banks.give(b, v)
                kv_v.append(v)
            head_norm(got[4][0], kt_tok, 64, T, p("k_norm_g", gi),
                      (None, lambda w, n=n: k_toks.update({n: w})), True, halves=(KF[n][:, 0, :], KF[n][:, 1, :]))

        g_toks = []

        def post(i, b, t):
            a = A.do(lambda e: e.activation(GA[:, i, :], ps[:, b, 0:24], ACT.Sigmoid), t)
            banks.give(b, a)
            g_toks.append(a)
        gemm_tm(w_in, 8, 2304, 24, ax, 4, post)
        gq = V.do(lambda e: e.tensor_scalar(gm[:, 0:1], p("q_norm_g"), 0.125, None, ALU.mult))
        blocks(1)
        held = []
        for pair in range(2):
            gemm_fm(w_in, 8, [1024 + 256 * pair, 1152 + 256 * pair], [ax],
                    lambda n, s, b, t, pair=pair: held.append((2 * pair + n, b, t)))
        h_free = [PE.last()]

        def put(k, src, b, t):
            hi, lo = Hh[:, 4 + k, 0:T], Hl[:, 4 + k, 0:T]
            a = A.do(lambda e: e.activation(hi, src, ACT.Copy, scale=gm[:, 0:1]), t, gq, h_free)
            v = V.do(lambda e: e.scalar_tensor_tensor(lo, src, gm[:, 0:1], hi, ALU.mult, ALU.subtract), a)
            banks.give(b, v)
            return [a, v]
        query_sums(held, banks.take(), put, blk[:, 0:128:64], 64, RQ[:, :], q_toks)
        compress(1)
        run_later()

        for i in range(4):
            q, free = tmp.take()
            a = A.do(lambda e: e.activation(Tm[:, q, :], U[:, i, :], ACT.Square, accum_out=ms[:, i:i + 1]),
                     free, a_toks)
            tmp.give(q, a)
        a = A.do(lambda e: e.activation(ms[:, 4:8], ms[:, 0:4], ACT.Sqrt, bias=eps[:, 0:1], scale=1.0 / 512), a)
        t_ms = V.do(lambda e: e.reciprocal(ms[:, 8:12], ms[:, 4:8]), a)

        def to_mixed(src, i, k0, gcol):
            q, free = tmp.take()
            v = V.do(lambda e: e.tensor_scalar(Tm[:, q, :], src[:, i, :], ms[:, 8 + i:9 + i], None, ALU.mult), t_ms, free)
            b, fr = banks.take()
            for k in range(4):
                t = (PE.do if k == 3 else PE.go)(
                    lambda e, k=k: e.transpose(ps[:, b, 128 * k:128 * k + 128], Tm[:, q, 128 * k:128 * k + 128],
                                               ident), v, fr)
            out = []
            for k in range(4):
                hi = Hh[:, k0 + k, 128 * i:128 * i + 128]
                pk = ps[:, b, 128 * k:128 * k + 128]
                a = A.do(lambda e, hi=hi, pk=pk, k=k: e.activation(hi, pk, ACT.Copy, scale=gcol(k)), t,
                         h_free)
            for k in range(4):
                hi = Hh[:, k0 + k, 128 * i:128 * i + 128]
                lo = Hl[:, k0 + k, 128 * i:128 * i + 128]
                pk = ps[:, b, 128 * k:128 * k + 128]
                v = V.do(lambda e, hi=hi, lo=lo, pk=pk, k=k: e.scalar_tensor_tensor(
                    lo, pk, gcol(k), hi, ALU.mult, ALU.subtract), a)
                out += [a, v]
            tmp.give(q, t)
            banks.give(b, *out)
            return out

        mix = [[] for _ in range(8)]

        def mix_tile(src, i, k0):
            o = to_mixed(src, i, k0, lambda k: p("mix_out_g", k0 + k))
            for k in range(4):
                mix[k0 + k] += o
        mod_close()

        pr, ptr = Ring(4), Ring(4)
        for q in range(4):
            pr.give(q, V.last())
            ptr.give(q, V.last())

        def gate(i, h, br):
            return GA[:, i, 3 * h + br:3 * h + br + 1]

        def c_scores(i, box):
            b, f = banks.take()
            t = None
            for h in range(8):
                r = slice(64 * (h // 4), 64 * (h // 4) + 64)
                qh, ql = (H_[r, 4 + h % 4, 128 * i:128 * i + 128] for H_ in (Hh, Hl))
                to = ps[:, b, 32 * h:32 * h + 32]
                mm(to, qh, KCR[r, 0, :], True, False, q_toks, kct, f, t)
                mm(to, qh, KCR[r, 1, :], False, False)
                t = mm(to, ql, KCR[r, 0, :], False, True, inc=h in (3, 7))
            s3 = ps[:, b, 0:256].rearrange("p (h n) -> p h n", n=32)[:, :, 0:31]
            rq = RQ[:, :].rearrange("p (k q s) -> p s k q", k=4, q=4)[:, :, :, i].unsqueeze(3).to_broadcast([128, 2, 4, 31])
            s4 = ps[:, b, 0:256].rearrange("p (s k n) -> p s k n", s=2, k=4)[:, :, :, 0:31]
            for half in range(2):
                t = V.do(lambda e: e.tensor_tensor(s4[:, half], s4[:, half], rq[:, half], ALU.mult), t, q_toks)
            mk = c1[:, C1_CMP + 31 * i:C1_CMP + 31 * i + 31].unsqueeze(1).to_broadcast([128, 8, 31])
            v = V.do(lambda e: e.tensor_tensor(s3, s3, mk, ALU.add), t)
            j, fr = small.take()
            j2, fr2 = small.take()
            v = V.do(lambda e: e.tensor_reduce(sm[:, j, :], s3, AX.X, ALU.max), v, fr)
            v = V.do(lambda e: e.tensor_scalar(sm[:, j, :], sm[:, j, :], -1e29, None, ALU.max), v)
            q, fq = pr.take()
            P3 = P[:, q, 0:256].rearrange("p (h n) -> p h n", n=32)
            vz = V.do(lambda e: e.memset(P[:, q, 0:256], 0.0), fq)
            v = V.do(lambda e: e.tensor_tensor(P3[:, :, 0:31], s3, sm[:, j, :].unsqueeze(2).to_broadcast([128, 8, 31]),
                                               ALU.subtract), v, vz)
            banks.give(b, v)
            a = A.do(lambda e: e.activation(P3[:, :, 0:31], P3[:, :, 0:31], ACT.Exp), v)
            v = V.do(lambda e: e.tensor_reduce(sm[:, j2, :], P3[:, :, 0:31], AX.X, ALU.add), a, fr2)
            v = V.do(lambda e: e.tensor_scalar(sm[:, j2, :], sm[:, j2, :], 1e-6, None, ALU.max), v)
            v = V.do(lambda e: e.reciprocal(sm[:, j, :], sm[:, j2, :]), v)
            g8 = GA[:, i, :].rearrange("p (h b) -> p h b", b=3)[:, :, 0]
            v = V.do(lambda e: e.tensor_tensor(sm[:, j2, :], sm[:, j, :], g8, ALU.mult), v, g_toks)
            small.give(j, v)
            v = V.do(lambda e: e.tensor_tensor(P3[:, :, 0:31], P3[:, :, 0:31],
                                               sm[:, j2, :].unsqueeze(2).to_broadcast([128, 8, 31]), ALU.mult), v)
            small.give(j2, v)
            box.update(q=q, t=v)

        def c_turn(i, box):
            q = box["q"]
            b, f = banks.take()
            b2, f2 = banks.take()
            for h in range(8):
                t = (PE.do if h == 7 else PE.go)(
                    lambda e, h=h: e.transpose(ps[0:32, (b, b2)[h // 4], 128 * (h % 4):128 * (h % 4) + 128],
                                               P[:, q, 32 * h:32 * h + 32], ident), box["t"], f, f2)
            pr.give(q, t)
            m, fm_ = ptr.take()
            m2, fm2 = ptr.take()
            v = V.do(lambda e: e.tensor_copy(PT[0:32, m, :], ps[0:32, b, :]), t, fm_)
            a = A.do(lambda e: e.activation(PT[0:32, m2, :], ps[0:32, b2, :], ACT.Copy), t, fm2)
            banks.give(b, v)
            banks.give(b2, a)
            box.update(m=(m, m2), t2=[v, a])

        gathered = {}

        def part(i, h):
            return ps[64 * (h % 2):64 * (h % 2) + 64, gathered[i][0], 128 * (h // 2):128 * (h // 2) + 128]

        def c_out(i, box):
            gathered[i] = [*banks.take(), None]
            for half in range(2):
                mm(ps[64 * half:64 * half + 64, gathered[i][0], :], c1[:, 0:64], rowp[:, 0:512], True, False,
                   t_c1, t_row, gathered[i][1])
            for h in range(8):
                t = mm(part(i, h), VC[0:31, h // 4, :], PT[0:31, box["m"][h // 4], 128 * (h % 4):128 * (h % 4) + 128],
                       False, False, box["t2"], vct, inc=h == 7)
            ptr.give(box["m"][0], t)
            ptr.give(box["m"][1], t)

        def f_scores(u, box):
            i, h, br = u
            n = 128 * (i + 1)
            r = slice(64 * (h // 4), 64 * (h // 4) + 64)
            qh, ql = (H_[r, 4 + h % 4, 128 * i:128 * i + 128] for H_ in (Hh, Hl))
            kk, wide = KF[br - 1], max(n, 256)
            b, f = banks.take()
            mm(ps[:, b, 0:wide], qh, kk[r, 0, 0:wide], True, False, q_toks, k_toks[br - 1], f)
            mm(ps[:, b, 0:wide], qh, kk[r, 1, 0:wide], False, False)
            mm(ps[:, b, 0:wide], ql, kk[r, 0, 0:wide], False, False)
            m = min(n, 256)
            t = mm(ps[:, b, n - m:n], identr[:, :], causalr[:, 256 - m:256], False, True, t_cr, t_ir, inc=True)
            q, fq = pr.take()
            c = 2 * (4 * (h % 4) + i) + h // 4
            j, a = softmax(b, n, t, P, q, fq, scale=RQ[:, c:c + 1])
            box.update(q=q, j=j, t=a)

        def f_scale(u, box):
            i, h, br = u
            q, j, n = box["q"], box["j"], 128 * (i + 1)
            v = V.do(lambda e: e.reciprocal(sm[:, j, 3:4], sm[:, j, 1:2]), box["t"])
            box["t"] = V.do(lambda e: e.tensor_scalar(P[:, q, 0:n], P[:, q, 0:n], sm[:, j, 3:4], gate(i, h, br),
                                                      ALU.mult, ALU.mult), v, g_toks)
            small.give(j, box["t"])

        def f_turn(u, box):
            box["m"], box["t2"] = turn(P, box["q"], 128 * (u[0] + 1), box["t"], PT, pr, ptr, A)

        def f_out(u, box):
            i, h, br = u
            vv = (VS, VW)[br - 1]
            m = box["m"]
            for k in range(i + 1):
                t = mm(part(i, h), vv[:, k, 64 * (h // 4):64 * (h // 4) + 64], PT[:, m, 128 * k:128 * k + 128],
                       False, h >= 6 and br == 2 and k == i, box["t2"], kv_v, inc=k == i)
            ptr.give(m, t)
            gathered[i][2] = t

        def mix_squares(i):
            b, _, t = gathered[i]
            q, free = tmp.take()
            a = A.do(lambda e: e.activation(Tm[:, q, :], ps[:, b, :], ACT.Square), t, free)
            gathered[i] += [q, a]

        def mix_attention(i):
            b, _, _, q, a = gathered[i]
            b2, f = banks.take()
            for k in range(4):
                t = mm(ps[:, b2, 0:128], ones, Tm[:, q, 128 * k:128 * k + 128], k == 0, k == 3, a, f, inc=k == 3)
            q2, free = tmp.take()
            r = A.do(lambda e: e.activation(Tm[:, q2, 0:128], ps[:, b2, 0:128], ACT.Sqrt, bias=eps[:, 0:1],
                                            scale=1.0 / 512), t, free)
            banks.give(b2, r)
            v = V.do(lambda e: e.reciprocal(Tm[:, q2, 0:128], Tm[:, q2, 0:128]), r)
            three = lambda x: x.rearrange("p (k t) -> p k t", k=4)
            v = V.do(lambda e: e.tensor_tensor(three(Tm[:, q, :]), three(ps[:, b, :]),
                                               Tm[:, q2, 0:128].unsqueeze(1).to_broadcast([128, 4, 128]), ALU.mult), v)
            tmp.give(q2, v)
            banks.give(b, v)
            last = []
            for k in range(4):
                hi, lo = (H_[:, 4 + k, 128 * i:128 * i + 128] for H_ in (Hh, Hl))
                x, g = Tm[:, q, 128 * k:128 * k + 128], p("mix_out_g", 4 + k)
                a = A.do(lambda e: e.activation(hi, x, ACT.Copy, scale=g), v)
                w = V.do(lambda e: e.scalar_tensor_tensor(lo, x, g, hi, ALU.mult, ALU.subtract), a)
                mix[4 + k] += [a, w]
                last += [a, w]
            tmp.give(q, *last)

        MT = U[:, :, :].rearrange("p a (b t) -> p (a b) t", b=2)
        MK = VV[:, 0:2, :].rearrange("p a (b t) -> p (a b) t", b=2)
        MV = VV[:, 2:4, :]
        mk_toks, mv_toks = [], []
        w_mkv = d["w_mkv"]
        mem = {}

        def mem_load():
            mem["t"] = load(G, MT, d["mem"].rearrange("(k p) t -> p k t", p=128), mix[0], mix[3])
            tk = None
            for k in range(8):
                tk = square_in(MT[:, k, :], T, TC, k, mem["t"], tk)
            mem["sum"] = tk

        def mem_norm():
            (hm, _), = norms([(MT, TC, T, lambda: mem["sum"], lambda k: p("mem_kv_norm_g", k), None, lambda: mem["t"])])
            mem["act"] = ("c", Hh, Hl, T, TC, hm)

        def mem_k(pair):
            def post(n, s, b, t):
                head_norm(b, t, 128, TC, p("mem_k_norm_g"), (MK[:, 2 * pair + n, :], mk_toks.append),
                          False, a_toks)
            gemm_fm(w_mkv, 8, [256 * pair, 256 * pair + 128], [mem["act"]], post)

        def mem_v(half):
            def post(i, b, t):
                v = V.do(lambda e: e.tensor_copy(MV[:, i, 256 * half:256 * half + 256], ps[:, b, 0:256]), t)
                banks.give(b, v)
                mv_toks.append(v)
            gemm_tm(w_mkv, 8, 512 + 256 * half, 256, mem["act"], 2, post)

        extra = {}
        for n in range(4):
            extra.setdefault(1 + 2 * n, []).append(lambda n=n: mix_tile(U, n, 0))
            if n < 3:
                extra.setdefault(17 * n + 21, []).append(lambda n=n: mix_squares(n))
                extra.setdefault(17 * n + 22, []).append(lambda n=n: mix_attention(n))
        extra.setdefault(9, []).append(mem_load)
        extra.setdefault(14, []).append(mem_norm)
        for n in range(2):
            extra.setdefault(24 + 8 * n, []).append(lambda n=n: mem_k(n))
            extra.setdefault(40 + 8 * n, []).append(lambda n=n: mem_v(n))
        units = []
        for i in range(4):
            units += [(i, None, 0)] + [(i, h, br) for h in range(8) for br in (1, 2)]
        stages = [lambda u, box, c=c, f=f: c(u[0], box) if u[2] == 0 else f(u, box)
                  for c, f in ((c_turn, f_turn), (c_scores, f_scores), (lambda i, box: None, f_scale),
                               (c_out, f_out))]
        pipeline(units, stages, [3, 0, 1, 4], extra)
        run_later()
        mix_squares(3)
        mix_attention(3)

        xt = {("x", k): t_xs[k] for k in range(8)}
        sums = {}

        def residual(w, kt, acts, coef, C=None, final=True, next_norm=None):
            def post(n, s, b, t, n0=None):
                k = n0 + n
                dst, nt, t0 = (X, T, 0) if s == "x" else (C, TC, T)
                o = dst[:, k, :]
                cf = coef(k, s)
                if cf is None:
                    v = V.do(lambda e: e.tensor_tensor(o, ps[:, b, 0:nt], o, ALU.add), t, xt[s, k])
                else:
                    v = V.do(lambda e: e.scalar_tensor_tensor(o, ps[:, b, 0:nt], cf, o, ALU.mult, ALU.add),
                             t, xt[s, k])
                xt[s, k] = v
                banks.give(b, v)
                if final:
                    sums[s] = square_in(o, t0, nt, k, v, sums.get((s, "free"), []) if k == 0 else sums[s])
            for some in [[a] for a in acts] if next_norm else [acts]:
                for pair in range(4):
                    if final and pair == 3:
                        A.do(lambda e: e.activation(eps[:, 1:2], eps[:, 0:1], ACT.Sqrt))
                    gemm_fm(w, kt, [256 * pair, 256 * pair + 128], some,
                            lambda n, s, b, t, pair=pair: post(n, s, b, t, 2 * pair))
                if next_norm and some[0][0] == "x":
                    steps, toks, done = norm_steps(next_norm)
                    in_turn(steps)
                    pending["x"] = (toks, done)
            if next_norm:
                while later:
                    run_later()

        am = ("x", Hh, Hl, 0, T, mix)
        residual(d["w_out"], 8, [am], lambda k, s: None)
        fence()
        s1.close()

        RM = sb("RM", [128, 16], where=s2)
        MQ = sb("MQ", [128, 4, T], where=s2)
        P = sb("P2", [128, 4, 512], where=s2)
        PT = sb("PT2", [128, 16, 256], where=s2)
        mq_toks = []
        (h1, h1done), = norms([(X, T, 0, lambda: sums["x"], lambda k: p("norm_mem_g", k), None, lambda: [])])
        sums["x", "free"] = h1done
        ax = ("x", Hh, Hl, 0, T, h1)
        held = []
        for pair in range(2):
            gemm_fm(d["w_mq"], 8, [256 * pair, 256 * pair + 128], [ax],
                    lambda n, s, b, t, pair=pair: held.append((2 * pair + n, b, t)))
        gmem = V.do(lambda e: e.tensor_scalar(gm[:, 1:2], p("mem_q_norm_g"), 128.0 ** -0.5, None, ALU.mult))

        def put(k, src, b, t):
            v = V.do(lambda e: e.tensor_scalar(MQ[:, k, :], src, gm[:, 1:2], None, ALU.mult), t, gmem)
            banks.give(b, v)
            return [v]
        query_sums(held, banks.take(), put, ones[:, 0:1], 128, RM[:, :], mq_toks)
        run_later()
        h_free = [PE.last()]
        pr = Ring(4)
        ptoks = {}

        def m_scores(u, box):
            h, i = u
            b, f = banks.take()
            t = mm(ps[:, b, 0:TC], MQ[:, h, 128 * i:128 * i + 128], MK[:, h, :], True, True, mq_toks, mk_toks,
                   f, inc=True)
            q, fq = pr.take()
            j, a = softmax(b, TC, t, P, q, fq, scale=RM[:, 4 * h + i:4 * h + i + 1])
            box.update(q=q, t=a, j=j)

        def m_scale(u, box):
            q, j = box["q"], box["j"]
            v = V.do(lambda e: e.reciprocal(sm[:, j, 3:4], sm[:, j, 1:2]), box["t"])
            v = V.do(lambda e: e.tensor_scalar(P[:, q, 0:TC], P[:, q, 0:TC], sm[:, j, 3:4], None, ALU.mult), v)
            small.give(j, v)
            box["t"] = v

        def m_turn(u, box):
            h, i = u
            b, f = banks.take()
            for k in range(2):
                t = (PE.do if k == 1 else PE.go)(
                    lambda e, k=k: e.transpose(ps[:, b, 128 * k:128 * k + 128],
                                               P[:, box["q"], 128 * k:128 * k + 128], ident), box["t"], f)
            pr.give(box["q"], t)
            dst = PT[:, 4 * h:4 * h + 4, :].rearrange("p a b -> p (a b)").rearrange("p (k t) -> p k t", k=2)[
                :, :, 128 * i:128 * i + 128]
            src = ps[:, b, 0:256].rearrange("p (k t) -> p k t", k=2)
            v = A.do(lambda e: e.activation(dst, src, ACT.Copy), t)
            banks.give(b, v)
            ptoks.setdefault(h, []).append(v)

        ho = [[] for _ in range(4)]

        def m_out(u, box):
            h, i = u
            if i != 3:
                return
            b, f = banks.take()
            pt = PT[:, 4 * h:4 * h + 4, :].rearrange("p a b -> p (a b)").rearrange("p (k t) -> p k t", k=2)
            for k in range(2):
                t = mm(ps[:, b, :], MV[:, k, 128 * h:128 * h + 128], pt[:, k, :], k == 0, k == 1, ptoks[h],
                       mv_toks, f, inc=k == 1)
            a, v = split_to(ps[:, b, :], Hh[:, h, 0:T], Hl[:, h, 0:T], [t, *h_free])
            banks.give(b, a, v)
            ho[h] = [a, v]
        pipeline([(h, i) for h in range(4) for i in range(4)], [m_turn, m_scores, m_scale, m_out],
                 [3, 0, 1, 4])
        residual(d["w_mo"], 4, [("x", Hh, Hl, 0, T, ho)], lambda k, s: None)
        fence()
        s2.close()

        s3 = ctx.enter_context(ExitStack())
        C = None
        Gh = sb("Gh", [128, 11, T + TC], F32R, where=s3)
        Gl = sb("Gl", [128, 11, T + TC], F32R, where=s3)
        MR = sb("MR", [128, 9, 512], where=s3)
        (h1, h1done), = norms([(X, T, 0, lambda: sums["x"], lambda k: p("norm_ffn_g", k), None, lambda: [])])
        mod_open(72, [MR[:, q, :] for q in range(4)], MR[:, 4:8, :].rearrange("p a b -> p (a b)"), MR[:, 8, :])
        sums["x", "free"] = h1done
        ax = ("x", Hh, Hl, 0, T, h1)
        g_free = [None]
        for part in range(4):
            gt = [[] for _ in range(8)]
            for pair in range(4):
                def post(n, s, b, t, pair=pair):
                    k = 2 * pair + n
                    i, fr = tmp.take()
                    a = A.do(lambda e: e.activation(Tm[:, i, :], ps[:, b, :], ACT.Relu), t, fr)
                    banks.give(b, a)
                    v = V.do(lambda e: e.tensor_tensor(Tm[:, i, :], Tm[:, i, :], Tm[:, i, :], ALU.mult), a)
                    a, v = split_to(Tm[:, i, :], Gh[:, k, 0:T], Gl[:, k, 0:T], [v, *g_free])
                    tmp.give(i, a, v)
                    gt[k] = [a, v]
                gemm_fm(d["w_ff1"], 8, [1024 * part + 256 * pair, 1024 * part + 256 * pair + 128], [ax], post)
            residual(d["w_ff2"][1024 * part:1024 * part + 1024, :], 8, [("x", Gh, Gl, 0, T, gt)],
                     lambda k, s: None, final=part == 3)
            g_free = [PE.last()]
        mod_tok = mod_end()
        fence()
        s3.close()

        sC = ctx.enter_context(ExitStack())
        C = sb("C", [128, 8, TC], where=sC)
        t_c = load(G, C[:, :, :], d["ctx_2"].rearrange("(k p) t -> p k t", p=128))
        for k in range(8):
            xt["c", k] = t_c

        CF = [sb(f"CF{l}", [128, 6, 8, 2]) for l in range(2)]

        def mod_norm_cols(l, i):
            out = []
            for s in range(2):
                g = p("norm_g_2", 24 * l + 8 * i, 8)
                mm_ = M[:, l, 8 * (3 * i + 1):8 * (3 * i + 2), s]
                mg = M[:, l, 8 * (3 * i + 2):8 * (3 * i + 3), s]
                half = 1.0 if i == 1 else 0.5
                out.append(V.do(lambda e, s=s, g=g, mm_=mm_: e.scalar_tensor_tensor(
                    CF[l][:, i, :, s], mm_, 1.0, g, ALU.add, ALU.mult), mod_tok))
                out.append(V.do(lambda e, s=s, mg=mg: e.tensor_scalar(CF[l][:, 3 + i, :, s], mg, half, None, ALU.mult),
                                mod_tok))
            return out

        SI = {"x": 0, "c": 1}

        pending = {}

        def norm2_spec(l, i, s):
            src, nt, t0 = (X, T, 0) if s == "x" else (C, TC, T)
            return (src, nt, t0, lambda: sums[s], lambda k: CF[l][:, i, k, SI[s]:SI[s] + 1],
                    lambda k: mcol(l, 3 * i, k, SI[s]), lambda: [cf_tok[l], [xt[s, k] for k in range(8)]])

        def norm2(l, i, sets):
            got = dict(pending)
            pending.clear()
            if "x" not in got:
                got["x"], = norms([norm2_spec(l, i, "x")])
            if "c" in sets:
                steps, toks, done = norm_steps(norm2_spec(l, i, "c"))
                got["c"] = (toks, done)
                between.extend(steps)
            acts = []
            for s in sets:
                toks, done = got[s]
                sums[s, "free"] = done
                nt, t0 = (T, 0) if s == "x" else (TC, T)
                acts.append((s, Hh, Hl, t0, nt, toks))
            return acts

        def following(l, i):
            return norm2_spec(*((l, i + 1) if i < 2 else (l + 1, 0)), "x")

        def ffn(l, j, i, sets, tokname):
            s4 = ctx.enter_context(ExitStack())
            Gh = sb(f"Gh{tokname}", [128, 11, T + TC], F32R, where=s4)
            Gl = sb(f"Gl{tokname}", [128, 11, T + TC], F32R, where=s4)
            if mods:
                MR = sb(f"MR{tokname}", [128, 8, 512], where=s4)
            acts = norm2(l, i, sets)
            if mods:
                mod_open(72, [MR[:, q, :] for q in range(3)], MR[:, 3:7, :].rearrange("p a b -> p (a b)"),
                         MR[:, 7, :])
            g_free = [None]
            w1, w2 = d["ffn_w_in_2"][l, j], d["ffn_w_out_2"][l, j]
            for part in range(2):
                gt = {s: [None] * 11 for s in sets}
                for f in range(11):
                    fc = 11 * part + f
                    box = {}

                    def post(n, s, b, t, f=f, box=box, gt=gt):
                        if n == 0:
                            box[s] = (b, t)
                            return
                        ba, ta = box[s]
                        nt, t0 = (T, 0) if s == "x" else (TC, T)
                        q, fr = tmp.take()
                        a = A.do(lambda e: e.activation(Tm[:, q, 0:nt], ps[:, ba, 0:nt], ACT.Silu), ta, fr)
                        banks.give(ba, a)
                        v = V.do(lambda e: e.tensor_tensor(Tm[:, q, 0:nt], Tm[:, q, 0:nt], ps[:, b, 0:nt], ALU.mult),
                                 a, t)
                        banks.give(b, v)
                        a, v = split_to(Tm[:, q, 0:nt], Gh[:, f, t0:t0 + nt], Gl[:, f, t0:t0 + nt], [v, *g_free])
                        tmp.give(q, a, v)
                        gt[s][f] = [a, v]
                    gemm_fm(w1, 8, [128 * fc, FF2 + 128 * fc], acts, post)
                    if fc % 3 == 2:
                        mod_step()
                residual(w2[1408 * part:1408 * part + 1408, :], 11,
                         [(s, Gh, Gl, 0 if s == "x" else T, T if s == "x" else TC, gt[s]) for s in sets],
                         lambda k, s: CF[l][:, 3 + i, k, SI[s]:SI[s] + 1], C=C, final=part == 1,
                         next_norm=following(l, i) if part == 1 and len(sets) == 2 else None)
                g_free = [PE.last()]
            mod_close()
            fence()
            s4.close()

        cf_tok = {}
        for i in range(3):
            cf_tok.setdefault(0, []).extend(mod_norm_cols(0, i))
        pending["x"], = norms([norm2_spec(0, 0, "x")])
        tk = t_c
        for k in range(8):
            tk = square_in(C[:, k, :], T, TC, k, t_c, tk)
        sums["c"] = tk
        mod_begin(1)
        for l in range(2):
            ffn(l, 0, 0, ["x", "c"], f"a{l}")
            if l == 0:
                mod_tok = mod_end()
                for i in range(3):
                    cf_tok.setdefault(1, []).extend(mod_norm_cols(1, i))

            s5 = ctx.enter_context(ExitStack())
            CV = sb(f"CV{l}", [128, 2, T + TC], where=s5)
            PV = sb(f"PV{l}", [128, 2, T + TC], where=s5)
            KH = sb(f"KH{l}", [128, 4, T + TC], F32R, where=s5)
            KL = sb(f"KL{l}", [128, 4, T + TC], F32R, where=s5)
            VB = sb(f"VB{l}", [128, 4, 2, 512], where=s5)
            VX = sb(f"VX{l}", [128, 2, 512], where=s5)
            P = sb(f"P{l}", [128, 4, 512], where=s5)
            PT = sb(f"PTt{l}", [128, 1584], where=s5)
            RB = sb(f"RB{l}", [128, 4, 512], where=s5)
            c2 = sb(f"c2{l}", [128, C2_MASK], where=s5)
            maskr = sb(f"maskr{l}", [128, 768], F32R, where=s5)
            PW = sb(f"PW{l}", [128, 2, 128], where=s5)
            t_c2 = load(A, c2[:, :], d["c2"][:, 0:C2_MASK])
            raw_mask = RB[:, 0:2, :].rearrange("p a b -> p (a b)")[:, 0:768]
            t_mask = load(A, raw_mask, d["c2"][:, C2_MASK:NC2])
            t_mask = A.do(lambda e: e.activation(maskr[:, :], raw_mask, ACT.Copy), t_mask)
            z = G.do(lambda e: e.memset(PW[:, :, :], 0.0))
            t_pw = []
            for g in range(4):
                r = slice(64 * (g % 2), 64 * (g % 2) + 64)
                t_pw.append(load(G, PW[r, g // 2, 64 * (g % 2):64 * (g % 2) + 64], d["pool_w_2"][l, g], z))
            sets = ["x", "c"]
            full = sets if l == 0 else ["x"]
            acts = norm2(l, 1, sets)
            by = {a[0]: a for a in acts}
            fa = [by[s] for s in full]
            w = d["w_in_2"][l]
            OFF = {"x": (0, T), "c": (T, TC)}
            cv = {}
            vn = []
            for half in range(2):
                def post(i, b, t, half=half):
                    v = A.do(lambda e: e.activation(P[:, i, 256 * half:256 * half + 256], ps[:, b, 0:256], ACT.Copy), t)
                    banks.give(b, v)
                    vn.append(v)
                gemm_tm(w, 8, 2048 + 256 * half, 256, by["x"], 4, post)
            vb_toks = []
            vb_sem = [sem(f"vb{l}"), 0]
            for j in range(4):
                for i in range(8):
                    r0 = 64 * (i % 2) + BAND0[j]
                    t = G.dma(lambda e, j=j, i=i, r0=r0: e.dma_start(
                        VB[32 * (i % 4):32 * (i % 4) + 32, j, i // 4, :], P[r0:r0 + 32, i // 2, :]), vb_sem, *vn)
            vb_toks = [t]
            vx = []
            for half in range(2):
                def post(i, b, t, half=half):
                    v = V.do(lambda e: e.tensor_copy(VX[:, i, 256 * half:256 * half + 256], ps[:, b, 0:256]), t)
                    banks.give(b, v)
                    vx.append(v)
                gemm_tm(w, 8, 2048 + 256 * half, 256, by["c"], 2, post)
            kk_toks, qq_toks = {"x": [], "c": []}, {"x": {}, "c": {}}
            for pair in range(2):
                def post(n, s, b, t, pair=pair):
                    t0, nt = OFF[s]
                    k = 2 * pair + n
                    a, v = split_to(ps[:, b, 0:nt], KH[:, k, t0:t0 + nt], KL[:, k, t0:t0 + nt], [t])
                    banks.give(b, a, v)
                    kk_toks[s] += [a, v]
                gemm_fm(w, 8, [1536 + 256 * pair, 1664 + 256 * pair], [by[s] for s in sets], post)
            for stage, c0 in enumerate((0, 512, 256)):
                def post(n, s, b, t, stage=stage):
                    t0, nt = OFF[s]
                    o = CV[:, n, t0:t0 + nt]
                    src = ps[:, b, 0:nt]
                    if stage == 0:
                        v = V.do(lambda e: e.tensor_copy(o, src), t)
                    elif stage == 1:
                        i, fr = tmp.take()
                        a_ = Tm[:, i, 0:nt]
                        cw = lambda k: p("conv_w_2", 6 * l + 2 * k + n)
                        v = V.do(lambda e: e.tensor_tensor(a_, o, src, ALU.mult), t, cv[n, s], fr)
                        v = V.do(lambda e: e.tensor_scalar(o, a_, cw(1), None, ALU.mult), v)
                        v = V.do(lambda e: e.scalar_tensor_tensor(o[:, 1:nt], a_[:, 0:nt - 1], cw(0), o[:, 1:nt],
                                                                  ALU.mult, ALU.add), v)
                        v = V.do(lambda e: e.scalar_tensor_tensor(o[:, 0:nt - 1], a_[:, 1:nt], cw(2),
                                                                  o[:, 0:nt - 1], ALU.mult, ALU.add), v)
                        tmp.give(i, v)
                    else:
                        v = V.do(lambda e: e.tensor_tensor(o, o, src, ALU.mult), t, cv[n, s])
                    banks.give(b, v)
                    cv[n, s] = v
                gemm_fm(w, 8, [c0, c0 + 128], fa, post)
            pv = {}
            pt_free = [None]

            def pool_post(n, s, b, t):
                t0, nt = OFF[s]
                W_ = nt + 16
                buf = [PT[:, 528 * q:528 * q + W_] for q in range(3)]
                v0 = V.do(lambda e: e.memset(buf[0], 0.0), *pt_free)
                v = V.do(lambda e: e.tensor_copy(buf[0][:, 8:8 + nt], ps[:, b, 0:nt]), t, v0)
                banks.give(b, v)

                def add(dst, src, lo, hi, a, b_, rows, *tk):
                    r = slice(*rows)
                    return V.do(lambda e: e.tensor_tensor(dst[r, lo:hi], src[r, lo - a:hi - a],
                                                          src[r, lo + b_:hi + b_], ALU.add), *tk)
                s2_ = add(buf[1], buf[0], 1, W_, 1, 0, (0, 128), v, *pt_free)
                if n == 0:
                    s4_ = add(buf[2], buf[1], 8, 8 + nt, 1, 1, (64, 128), s2_)
                    src = [(slice(0, 64), buf[1]), (slice(64, 128), buf[2])]
                    last = [s2_, s4_]
                else:
                    s4_ = add(buf[2], buf[1], 2, W_ - 1, 1, 1, (0, 128), s2_)
                    s8_ = add(buf[1], buf[2], 4, W_ - 3, 2, 2, (0, 128), s4_)
                    s16 = add(buf[2], buf[1], 8, 8 + nt, 4, 4, (64, 128), s8_)
                    src = [(slice(0, 64), buf[1]), (slice(64, 128), buf[2])]
                    last = [s8_, s16]
                o = PV[:, n, t0:t0 + nt]
                ws = []
                for r, bf in src:
                    ws.append(V.do(lambda e, r=r, bf=bf: e.scalar_tensor_tensor(
                        o[r, 8:nt - 8], bf[r, 16:nt], c2[r, C2_RW + n:C2_RW + n + 1], buf[0][r, 16:nt],
                        ALU.mult, ALU.subtract), *last, t_c2))
                    for e0, x0 in ((0, 0), (8, nt - 8)):
                        ed = c2[r, C2_EDGE + 16 * n + e0:C2_EDGE + 16 * n + e0 + 8]
                        q = V.do(lambda e, r=r, bf=bf, ed=ed, x0=x0: e.tensor_tensor(
                            o[r, x0:x0 + 8], bf[r, 8 + x0:16 + x0], ed, ALU.mult), *last, t_c2)
                        ws.append(V.do(lambda e, r=r, x0=x0: e.tensor_tensor(
                            o[r, x0:x0 + 8], o[r, x0:x0 + 8], buf[0][r, 8 + x0:16 + x0], ALU.subtract), q))
                pt_free[:] = ws

                def second():
                    b2, fr = banks.take()
                    t2 = mm(ps[:, b2, 0:nt], PW[:, n, :], o, True, True, ws, t_pw, fr, inc=True)
                    v2 = V.do(lambda e: e.tensor_scalar(o, ps[:, b2, 0:nt], p("pool_scale_2", 2 * l + n), None,
                                                        ALU.mult), t2)
                    banks.give(b2, v2)
                    pv[n, s] = v2
                later.append(second)
            gemm_fm(w, 8, [768, 896], fa, pool_post)
            held = []
            for pair in range(2):
                gemm_fm(w, 8, [1024 + 256 * pair, 1152 + 256 * pair], fa,
                        lambda n, s, b, t, pair=pair: held.append((2 * pair + n, s, b, t)))
            h_free = [PE.last()]
            for k, s, b, t in sorted(held, key=lambda x: x[0]):
                t0, nt = OFF[s]
                hi, lo, src = Hh[:, 4 + k, t0:t0 + nt], Hl[:, 4 + k, t0:t0 + nt], ps[:, b, 0:nt]
                if s == "x":
                    hi, lo = (y.rearrange("p (j r c) -> p j r c", j=4, c=16) for y in (hi, lo))
                    src = src.rearrange("p (r j c) -> p j r c", r=8, c=16)
                a = A.do(lambda e: e.activation(hi, src, ACT.Copy, scale=0.125), t, h_free)
                for j in range(4 if s == "x" else 1):
                    lo_, src_, hi_ = (y[:, j] if s == "x" else y for y in (lo, src, hi))
                    v = V.do(lambda e: e.scalar_tensor_tensor(lo_, src_, 0.125, hi_, ALU.mult, ALU.subtract), a)
                banks.give(b, a, v)
                qq_toks[s][k] = [a, v]
            mix = {s: [[] for _ in range(8)] for s in full}

            def mix_cp(s):
                t0, nt = OFF[s]
                for n in range(2):
                    a, v = split_to(CV[:, n, t0:t0 + nt], Hh[:, n, t0:t0 + nt], Hl[:, n, t0:t0 + nt],
                                    [cv[n, s], *h_free])
                    mix[s][n] = [a, v]
                    a, v = split_to(PV[:, n, t0:t0 + nt], Hh[:, 2 + n, t0:t0 + nt], Hl[:, 2 + n, t0:t0 + nt],
                                    [pv[n, s], *h_free])
                    mix[s][2 + n] = [a, v]

            pr, ptr = Ring(4), Ring(3)
            for q in range(4):
                pr.give(q, vb_toks[0])
            for q in range(3):
                ptr.give(q, *pt_free)
            PT3 = PT[:, 0:1584].rearrange("p (a b) -> p a b", a=3)
            rb_done = {}
            rb_tok = {}
            rb_sem = [[sem(f"rb{l}{i}"), 0] for i in range(4)]

            def bias_load(h):
                for r in range(8):
                    src = bass.AP(d["rpb_2"].tensor, ((l * 8 + h) * 16 + 7 - r) * 64, [[1, 16], [1, 512]])
                    t = G.dma(lambda e, r=r, src=src: e.dma_start(RB[16 * r:16 * r + 16, h % 4, :], src),
                              rb_sem[h % 4], rb_done.get(h - 4, t_mask))
                rb_tok[h] = t

            def n_scores(u, box):
                h, kind, j = u
                if kind == "x" and j == 0 and h % 2 == 0:
                    for hh in ([0, 1, 2, 3] if h == 0 else [h + 2, h + 3] if h < 6 else []):
                        bias_load(hh)
                r = slice(64 * (h % 2), 64 * (h % 2) + 64)
                b, f = banks.take()
                def scores(out, q_, k_, *toks, first=True):
                    mm(out, q_(Hh), k_(KH), first, False, f, *toks)
                    mm(out, q_(Hh), k_(KL), False, False)
                    return mm(out, q_(Hl), k_(KH), False, True, inc=True)

                if kind == "x":
                    q_ = lambda H_: H_[r, 4 + h // 2, 128 * j:128 * j + 128]
                    mm(ps[:, b, 0:256], identr[:, :], maskr[:, 256 * KIND[j]:256 * KIND[j] + 256], True, False,
                       t_ir, t_mask, f)
                    scores(ps[:, b, 0:256].rearrange("p (i c) -> p i c", c=32), q_,
                           lambda K_: K_[r, h // 2, 0:T].rearrange("p (i c) -> p i c", c=64)[
                               :, :, BAND0[j]:BAND0[j] + 32], qq_toks["x"][h // 2], kk_toks["x"], first=False)
                    t = scores(ps[:, b, 256:512], q_, lambda K_: K_[r, h // 2, T:T + TC], kk_toks["c"])
                    sl = ps[:, b, 0:256].rearrange("p (i c) -> p i c", c=32)
                    off = BAND0[j] - 16 * j
                    bi = RB[:, h % 4, :].rearrange("p (i c) -> p i c", c=64)[:, :, 32 - off:-off:-1]
                    t = V.do(lambda e: e.tensor_tensor(sl, sl, bi, ALU.add), t, rb_tok[h])
                    if j == 3:
                        rb_done[h] = t
                    n = 512
                else:
                    t = scores(ps[:, b, 0:TC], lambda H_: H_[r, 4 + h // 2, T + 128 * j:T + 128 * j + 128],
                               lambda K_: K_[r, h // 2, T:T + TC], qq_toks["c"][h // 2], kk_toks["c"])
                    n = TC
                q, fq = pr.take()
                jj, a = softmax(b, n, t, P, q, fq)
                box.update(q=q, j=jj, t=a, n=n)

            def n_scale(u, box):
                q, jj, n = box["q"], box["j"], box["n"]
                v = V.do(lambda e: e.reciprocal(sm[:, jj, 3:4], sm[:, jj, 1:2]), box["t"])
                box["t"] = V.do(lambda e: e.tensor_scalar(P[:, q, 0:n], P[:, q, 0:n], sm[:, jj, 3:4], None,
                                                          ALU.mult), v)
                small.give(jj, box["t"])

            def n_turn(u, box):
                box["m"], box["t2"] = turn(P, box["q"], box["n"], box["t"], PT3, pr, ptr, A)

            def n_out(u, box):
                h, kind, j = u
                m = box["m"]
                key, hb = (h // 2, kind, j), h % 2
                if hb == 0:
                    ot[key] = [*banks.take(), []]
                b, f, ts = ot[key]
                nk = box["n"] // 128
                for k in range(nk):
                    if kind == "x":
                        vv = VB[:, j, k, 64 * h:64 * h + 64] if k < 2 else VX[:, k - 2, 64 * h:64 * h + 64]
                    else:
                        vv = VX[:, k, 64 * h:64 * h + 64]
                    t = mm(ps[64 * hb:64 * hb + 64, b, 0:128], vv, PT3[:, m, 128 * k:128 * k + 128], k == 0,
                           k == nk - 1, box["t2"], vb_toks, vx, f, inc=k == nk - 1)
                ptr.give(m, t)
                ts.append(t)

            def n_final(u, box):
                h, kind, j = u
                if h % 2 == 0:
                    return
                b, _, ts = ot[h // 2, kind, j]
                k = 4 + h // 2
                t0 = 128 * j + OFF[kind][0]
                a, v = split_to(ps[:, b, 0:128], Hh[:, k, t0:t0 + 128], Hl[:, k, t0:t0 + 128], [*ts, *h_free])
                banks.give(b, a, v)
                mix[kind][k] += [a, v]
            ot = {}
            units = []
            for hp in range(4):
                for kind in full:
                    for j in range(4 if kind == "x" else 2):
                        units += [(2 * hp, kind, j), (2 * hp + 1, kind, j)]
            pipeline(units, [n_turn, n_scores, n_scale, n_out, n_final], [3, 0, 1, 4, 5],
                     {2 + 3 * n: [lambda s=s: mix_cp(s)] for n, s in enumerate(full)})
            residual(d["w_out_2"][l], 8, [(s, Hh, Hl, OFF[s][0], OFF[s][1], mix[s]) + ((True,) if s == "x" else ()) for s in full],
                     lambda k, s: CF[l][:, 4, k, SI[s]:SI[s] + 1], C=C,
                     next_norm=following(l, 1) if l == 0 else None)
            fence()
            s5.close()
            ffn(l, 1, 2, full, f"b{l}")

        b, t = rstd_spread(rstd_sums(sums["x"], 0, T, 1024), T)
        for k in range(8):
            v = V.do(lambda e, k=k: e.scalar_tensor_tensor(X[:, k, :], X[:, k, :], p("final_g_2", k), ps[:, b, :],
                                                           ALU.mult, ALU.mult), t)
            st = S.dma(lambda e, k=k: e.dma_start(d["out"][128 * k:128 * k + 128, :], X[:, k, :]), store_sem, v)
        S.wait(st)

        if plan is not None:
            block = ctx.enter_context(nc.Block())
            block.sync(S.play)
            block.tensor(PE.play)
            block.scalar(A.play)
            block.vector(V.play)
            block.gpsimd(G.play)
    return listing


def layouts(a):
    def cols(v):
        return v.reshape(-1, 128).T

    two = lambda v: np.concatenate([v, v], 0)
    pk = {
        "norm_mix_g": cols(a["norm_mix_g"][0]), "mix_out_g": cols(a["mix_out_g"][0].reshape(-1)),
        "norm_mem_g": cols(a["norm_mem_g"][0]), "mem_kv_norm_g": cols(a["mem_kv_norm_g"][0]),
        "norm_ffn_g": cols(a["norm_ffn_g"][0]), "q_norm_g": two(a["q_norm_g"][0])[:, None],
        "k_norm_g": two(a["k_norm_g"][0].T), "cmp_b1": cols(a["cmp_b1"][0].reshape(-1)),
        "cmp_b2": two(a["cmp_b2"][0, 0])[:, None], "mem_q_norm_g": a["mem_q_norm_g"][0][:, None],
        "mem_k_norm_g": a["mem_k_norm_g"][0][:, None], "sg_b": a["sg_b"][0].T,
        "cmp_pos": a["cmp_pos"][0].reshape(2, 16, 128).transpose(2, 0, 1).reshape(128, 32),
        "norm_g_2": cols(a["norm_g_2"].reshape(-1)), "b_mod_2": cols(a["b_mod_2"].reshape(-1)),
        "conv_w_2": cols(a["conv_w_2"].reshape(-1)), "pool_scale_2": cols(a["pool_scale_2"].reshape(-1)),
        "final_g_2": cols(a["final_g_2"]),
    }
    c, c1, c2 = constants()
    w_in = a["w_in"][0]
    q = w_in[:, 1024:1536].reshape(1024, 2, 4, 64).transpose(0, 2, 1, 3).reshape(1024, 512)
    rows = np.concatenate([a["sg_ln_g"][0], a["sg_ln_b"][0], a["cmp_b2"][0, 1]])
    return {
        "x": a["x"][0].T, "mem": a["mem"][0].T, "ctx_2": a["ctx_2"][0].T,
        "par": np.concatenate([pk[n] for n, _ in PARAMS], 1), "con": c, "c1": c1, "c2": c2,
        "rows": np.broadcast_to(rows, (128, 1088)),
        "w_in": np.concatenate([w_in[:, :1024], q, w_in[:, 1536:]], 1),
        "sg_w": a["sg_w"][0].transpose(2, 0, 1), "cmp_w1": a["cmp_w1"][0],
        "cmp_w2": np.concatenate([a["cmp_w2"][0]] * 2, 2).reshape(2, 2, 128, 128).transpose(2, 0, 1, 3),
        "w_out": a["w_out"][0], "w_mq": a["w_mq"][0], "w_mkv": a["w_mkv"][0], "w_mo": a["w_mo"][0],
        "w_ff1": a["w_ff1"][0], "w_ff2": a["w_ff2"][0], "w_mod_t": a["w_mod_2"].transpose(0, 2, 1),
        "cc_rows": np.broadcast_to(np.concatenate([a["c_2"][0], a["c_ctx_2"]]), (128, 2048)),
        "ffn_w_in_2": a["ffn_w_in_2"], "ffn_w_out_2": a["ffn_w_out_2"], "w_in_2": a["w_in_2"],
        "pool_w_2": a["pool_w_2"], "w_out_2": a["w_out_2"],
        "rpb_2": np.pad(a["rpb_2"], ((0, 0), (0, 0), (0, 1), (16, 17)))[..., ::-1],
    }


def kernel(**inputs):
    import concourse.bacc as _bacc
    from concourse.bass_utils import run_bass_kernel_spmd as _run

    arrays = {k: np.ascontiguousarray(v) for k, v in layouts({k: np.asarray(v) for k, v in inputs.items()}).items()}

    nc = _bacc.Bacc("TRN2", target_bir_lowering=False, num_devices=1)
    scratch = _bacc.Bacc("TRN2", target_bir_lowering=False, num_devices=1)
    build(nc, scratch, {k: v.shape for k, v in arrays.items()})
    r = _run(nc, [{f"in_{k}": v for k, v in arrays.items()}], core_ids=[0])
    return np.ascontiguousarray(r.results[0]["out"].T).reshape(1, T, 1024)


def build(nc, scratch, shapes):
    d = {k: nc.dram_tensor(f"in_{k}", s, F32, kind="ExternalInput").ap() for k, s in shapes.items()}
    d["out"] = nc.dram_tensor("out", (1024, T), F32, kind="ExternalOutput").ap()
    plan = program(scratch, d, None)
    program(nc, d, plan)
```
